# Optimizing a Trainium2 kernel written in Bass

```python
import math
import jax, jax.numpy as jnp
from jax import lax
import numpy as np

D_MODEL = 1024
BATCH = 1
SEQ = 256
DEPTH = 2

CONV_CH = D_MODEL // 2
CONV_WIDTH = 31
SB_HEADS = 8
SB_HEAD_DIM = 64
SB_WIDTH = SB_HEADS * SB_HEAD_DIM
Q_BLOCK = 128
EV_IN = 2 * CONV_CH + 3 * SB_WIDTH
EV_OUT_IN = CONV_CH + SB_WIDTH
LRU_WIDTH = D_MODEL
LRU_BLOCKS = 8
LRU_BLOCK_SIZE = LRU_WIDTH // LRU_BLOCKS
LRU_CONV_WIDTH = 4
LRU_C = 8.0
N_GROUPS = 4
EXPERTS_PER_GROUP = 4
N_EXPERTS = N_GROUPS * EXPERTS_PER_GROUP
TOP_K = 2
GROUP_SCORE_K = 2
D_FF_EXPERT = 512
MOE_BLOCK = 128

N_EVEN = (DEPTH + 1) // 2
N_ODD = DEPTH // 2
EPS = 1e-6


def rms_norm(x, g):
    xf = x.astype(jnp.float32)
    y = xf * lax.rsqrt(jnp.mean(xf * xf, axis=-1, keepdims=True) + EPS)
    return (y * g.astype(jnp.float32)).astype(x.dtype)

def layer_norm(x, g, b):
    xf = x.astype(jnp.float32)
    mu = jnp.mean(xf, axis=-1, keepdims=True)
    xc = xf - mu
    var = jnp.mean(xc * xc, axis=-1, keepdims=True)
    y = xc * lax.rsqrt(var + EPS) * g.astype(jnp.float32) + b.astype(jnp.float32)
    return y.astype(x.dtype)

def causal_dwconv(x, w, b):
    width = w.shape[0]
    y = lax.conv_general_dilated(
        x, w[:, None, :].astype(x.dtype), window_strides=(1,),
        padding=[(width - 1, 0)], dimension_numbers=('NWC', 'WIO', 'NWC'),
        feature_group_count=x.shape[-1])
    return y + b.astype(x.dtype)

def stick_breaking_attention(q, k, v):
    seq = q.shape[2]
    scale = 1.0 / math.sqrt(q.shape[-1])
    outs = []
    for blk in range(seq // Q_BLOCK):
        q0 = blk * Q_BLOCK
        end = q0 + Q_BLOCK
        qb = q[:, :, q0:end]
        kb = k[:, :, :end]
        vb = v[:, :, :end]
        z = jnp.einsum('bhqd,bhkd->bhqk', qb, kb).astype(jnp.float32) * scale
        qpos = q0 + jnp.arange(Q_BLOCK)[:, None]
        kpos = jnp.arange(end)[None, :]
        causal = kpos < qpos
        log_1m = jnp.where(causal, jax.nn.log_sigmoid(-z), 0.0)
        between = lax.cumsum(log_1m, axis=3, reverse=True) - log_1m
        wts = jnp.where(causal, jnp.exp(jax.nn.log_sigmoid(z) + between), 0.0)
        outs.append(jnp.einsum('bhqk,bhkd->bhqd', wts.astype(v.dtype), vb))
    return jnp.concatenate(outs, axis=2)

def even_mixer(h, in_w, dw_w, dw_b, ln_g, ln_b, q_g, k_g, out_w):
    bsz, seq, _ = h.shape
    proj = h @ in_w
    a_val, a_gate, q, k, v = jnp.split(
        proj, [CONV_CH, 2 * CONV_CH, 2 * CONV_CH + SB_WIDTH, 2 * CONV_CH + 2 * SB_WIDTH], axis=-1)
    u = a_val * jax.nn.sigmoid(a_gate)
    u = causal_dwconv(u, dw_w, dw_b)
    u = jax.nn.silu(layer_norm(u, ln_g, ln_b))
    def heads(t):
        return t.reshape(bsz, seq, SB_HEADS, SB_HEAD_DIM)
    qh = rms_norm(heads(q), q_g).transpose(0, 2, 1, 3)
    kh = rms_norm(heads(k), k_g).transpose(0, 2, 1, 3)
    vh = heads(v).transpose(0, 2, 1, 3)
    o = stick_breaking_attention(qh, kh, vh).transpose(0, 2, 1, 3).reshape(bsz, seq, SB_WIDTH)
    return jnp.concatenate([u, o], axis=-1) @ out_w

def block_diag_linear(x, w, b):
    nb, bs, _ = w.shape
    xb = x.reshape(x.shape[:-1] + (nb, bs))
    return jnp.einsum('bsnk,nkj->bsnj', xb, w).reshape(x.shape) + b

def lru_combine(earlier, later):
    a1, b1 = earlier
    a2, b2 = later
    return a1 * a2, a2 * b1 + b2

def odd_mixer(h, in_w, conv_w, conv_b, rg_w, rg_b, ig_w, ig_b, lam, out_w):
    proj = h @ in_w
    y_branch, x_branch = jnp.split(proj, 2, axis=-1)
    xc = causal_dwconv(x_branch, conv_w, conv_b)
    r = jax.nn.sigmoid(block_diag_linear(xc, rg_w, rg_b))
    i = jax.nn.sigmoid(block_diag_linear(xc, ig_w, ig_b))
    log_a = LRU_C * r.astype(jnp.float32) * jax.nn.log_sigmoid(lam.astype(jnp.float32))
    a = jnp.exp(log_a)
    mult = jnp.sqrt(-jnp.expm1(2.0 * log_a))
    b_in = mult * (i * xc).astype(jnp.float32)
    _, hseq = lax.associative_scan(lru_combine, (a, b_in), axis=1)
    return (jax.nn.gelu(y_branch) * hseq.astype(h.dtype)) @ out_w

def moe(h2, router_w, router_b, w1, w3, w2):
    n_tok, d = h2.shape
    logits = h2.astype(jnp.float32) @ router_w.astype(jnp.float32)
    scores = jax.nn.sigmoid(logits)
    biased = (scores + router_b.astype(jnp.float32)).reshape(n_tok, N_GROUPS, EXPERTS_PER_GROUP)
    group_score = jnp.sum(lax.top_k(biased, GROUP_SCORE_K)[0], axis=-1)
    gidx = jnp.argmax(group_score, axis=-1)
    in_group = jnp.take_along_axis(biased, gidx[:, None, None], axis=1)[:, 0]
    _, loc = lax.top_k(in_group, TOP_K)
    eid = gidx[:, None] * EXPERTS_PER_GROUP + loc
    sel = jnp.take_along_axis(scores, eid, axis=1)
    gates = (sel / jnp.sum(sel, axis=-1, keepdims=True)).astype(h2.dtype)
    n_asg = n_tok * TOP_K
    flat_e = eid.reshape(n_asg)
    flat_tok = jnp.repeat(jnp.arange(n_tok, dtype=jnp.int32), TOP_K)
    flat_g = gates.reshape(n_asg)
    order = jnp.argsort(flat_e)
    se = flat_e[order]
    stok = flat_tok[order]
    sg = flat_g[order]
    counts = jnp.bincount(flat_e, length=N_EXPERTS)
    starts = jnp.cumsum(counts) - counts
    padded = (counts + MOE_BLOCK - 1) // MOE_BLOCK * MOE_BLOCK
    pad_end = jnp.cumsum(padded)
    pad_start = pad_end - padded
    dest = pad_start[se] + (jnp.arange(n_asg) - starts[se])
    n_blocks = -(-n_asg // MOE_BLOCK) + N_EXPERTS
    buf_len = n_blocks * MOE_BLOCK
    buf_tok = jnp.zeros((buf_len,), jnp.int32).at[dest].set(stok)
    buf_g = jnp.zeros((buf_len,), h2.dtype).at[dest].set(sg)
    blk_e = jnp.minimum(
        jnp.searchsorted(pad_end, jnp.arange(n_blocks) * MOE_BLOCK, side='right'), N_EXPERTS - 1)

    def run_block(args):
        tok, g, e = args
        xb = h2[tok]
        y = (jax.nn.silu(xb @ w1[e]) * (xb @ w3[e])) @ w2[e]
        return y * g[:, None]

    ys = lax.map(run_block, (buf_tok.reshape(n_blocks, MOE_BLOCK),
                             buf_g.reshape(n_blocks, MOE_BLOCK), blk_e))
    return jnp.zeros_like(h2).at[buf_tok].add(ys.reshape(buf_len, d))

def first_inputs(seed: int = 0) -> dict:
    key = jax.random.key(seed)
    ks = jax.random.split(key, 28)
    f32 = jnp.float32

    def nrm(k, shape, scale):
        return jax.random.normal(k, shape, f32) * scale

    def gain(k, shape):
        return 1.0 + 0.05 * jax.random.normal(k, shape, f32)

    u = jax.random.uniform(ks[24], (N_ODD, LRU_WIDTH), f32, 0.9, 0.999)
    s = u ** (1.0 / LRU_C)
    lam = jnp.log(s) - jnp.log1p(-s)
    return {
        'x': nrm(ks[0], (BATCH, SEQ, D_MODEL), 1.0),
        'c': nrm(ks[1], (BATCH, D_MODEL), 1.0),
        'mod_w': nrm(ks[2], (DEPTH, D_MODEL, 6 * D_MODEL), 0.5 * D_MODEL ** -0.5),
        'mod_b': nrm(ks[3], (DEPTH, 6 * D_MODEL), 0.02),
        'mix_norm_g': gain(ks[4], (DEPTH, D_MODEL)),
        'ffn_norm_g': gain(ks[5], (DEPTH, D_MODEL)),
        'ev_in_w': nrm(ks[6], (N_EVEN, D_MODEL, EV_IN), D_MODEL ** -0.5),
        'ev_dw_w': nrm(ks[7], (N_EVEN, CONV_WIDTH, CONV_CH), CONV_WIDTH ** -0.5),
        'ev_dw_b': nrm(ks[8], (N_EVEN, CONV_CH), 0.02),
        'ev_ln_g': gain(ks[9], (N_EVEN, CONV_CH)),
        'ev_ln_b': nrm(ks[10], (N_EVEN, CONV_CH), 0.02),
        'ev_q_g': gain(ks[11], (N_EVEN, SB_HEAD_DIM)),
        'ev_k_g': gain(ks[12], (N_EVEN, SB_HEAD_DIM)),
        'ev_out_w': nrm(ks[13], (N_EVEN, EV_OUT_IN, D_MODEL), EV_OUT_IN ** -0.5),
        'od_in_w': nrm(ks[14], (N_ODD, D_MODEL, 2 * LRU_WIDTH), D_MODEL ** -0.5),
        'od_conv_w': nrm(ks[15], (N_ODD, LRU_CONV_WIDTH, LRU_WIDTH), LRU_CONV_WIDTH ** -0.5),
        'od_conv_b': nrm(ks[16], (N_ODD, LRU_WIDTH), 0.02),
        'od_rg_w': nrm(ks[17], (N_ODD, LRU_BLOCKS, LRU_BLOCK_SIZE, LRU_BLOCK_SIZE), LRU_BLOCK_SIZE ** -0.5),
        'od_rg_b': nrm(ks[18], (N_ODD, LRU_WIDTH), 0.02),
        'od_ig_w': nrm(ks[19], (N_ODD, LRU_BLOCKS, LRU_BLOCK_SIZE, LRU_BLOCK_SIZE), LRU_BLOCK_SIZE ** -0.5),
        'od_ig_b': nrm(ks[20], (N_ODD, LRU_WIDTH), 0.02),
        'od_lam': lam,
        'od_out_w': nrm(ks[21], (N_ODD, LRU_WIDTH, D_MODEL), LRU_WIDTH ** -0.5),
        'router_w': nrm(ks[22], (D_MODEL, N_EXPERTS), D_MODEL ** -0.5),
        'router_b': nrm(ks[23], (N_EXPERTS,), 0.01),
        'ex_w1': nrm(ks[25], (DEPTH, N_EXPERTS, D_MODEL, D_FF_EXPERT), D_MODEL ** -0.5),
        'ex_w3': nrm(ks[26], (DEPTH, N_EXPERTS, D_MODEL, D_FF_EXPERT), D_MODEL ** -0.5),
        'ex_w2': nrm(ks[27], (DEPTH, N_EXPERTS, D_FF_EXPERT, D_MODEL), D_FF_EXPERT ** -0.5),
    }

def first_block(x, c, mod_w, mod_b, mix_norm_g, ffn_norm_g, ev_in_w, ev_dw_w, ev_dw_b,
              ev_ln_g, ev_ln_b, ev_q_g, ev_k_g, ev_out_w, od_in_w, od_conv_w, od_conv_b,
              od_rg_w, od_rg_b, od_ig_w, od_ig_b, od_lam, od_out_w, router_w, router_b,
              ex_w1, ex_w3, ex_w2):
    bsz, seq, d = x.shape
    cond = jax.nn.silu(c)
    for layer in range(DEPTH):
        mod = cond @ mod_w[layer] + mod_b[layer]
        sh1, sc1, g1, sh2, sc2, g2 = [m[:, None, :] for m in jnp.split(mod, 6, axis=-1)]
        h = rms_norm(x, mix_norm_g[layer]) * (1 + sc1) + sh1
        if layer % 2 == 0:
            e = layer // 2
            mix = even_mixer(h, ev_in_w[e], ev_dw_w[e], ev_dw_b[e], ev_ln_g[e], ev_ln_b[e],
                             ev_q_g[e], ev_k_g[e], ev_out_w[e])
        else:
            o = layer // 2
            mix = odd_mixer(h, od_in_w[o], od_conv_w[o], od_conv_b[o], od_rg_w[o], od_rg_b[o],
                            od_ig_w[o], od_ig_b[o], od_lam[o], od_out_w[o])
        x = x + g1 * mix
        h = rms_norm(x, ffn_norm_g[layer]) * (1 + sc2) + sh2
        ffn = moe(h.reshape(bsz * seq, d), router_w, router_b,
                  ex_w1[layer], ex_w3[layer], ex_w2[layer]).reshape(bsz, seq, d)
        x = x + g2 * ffn
    return x


HEAD_DIM = 64
D_ATTN = 512
N_ATTN_HEADS = D_ATTN // HEAD_DIM
D_SGU = 512
N_SGU_GROUPS = 4
SGU_GROUP_DIM = D_SGU // N_SGU_GROUPS
CHUNK = 128
D_MIX = D_ATTN + D_SGU
D_IN = 3 * D_ATTN + 2 * D_SGU
D_FF = 2816
DILATED_PATTERNS = ((128, 1), (512, 4), (2048, 16))
ROPE_THETA = 500000.0
ROPE_DIM = HEAD_DIM // 4
NEG_INF = -1e30


def rms_norm_2(x, g):
    xf = x.astype(jnp.float32)
    y = xf * lax.rsqrt(jnp.mean(xf * xf, axis=-1, keepdims=True) + EPS)
    return (y * g.astype(jnp.float32)).astype(x.dtype)

def layer_norm_2(x, g, b):
    xf = x.astype(jnp.float32)
    mu = jnp.mean(xf, axis=-1, keepdims=True)
    xc = xf - mu
    y = xc * lax.rsqrt(jnp.mean(xc * xc, axis=-1, keepdims=True) + EPS)
    return (y * g.astype(jnp.float32) + b.astype(jnp.float32)).astype(x.dtype)

def swiglu(h, w_gate, w_up, w_down):
    return (jax.nn.silu(h @ w_gate) * (h @ w_up)) @ w_down

def partial_rotary(x, positions):
    half = ROPE_DIM // 2
    inv_freq = ROPE_THETA ** (-jnp.arange(0, ROPE_DIM, 2, dtype=jnp.float32) / ROPE_DIM)
    ang = positions.astype(jnp.float32)[:, None] * inv_freq[None, :]
    cos, sin = jnp.cos(ang), jnp.sin(ang)
    xr = x[..., :ROPE_DIM].astype(jnp.float32)
    x1, x2 = xr[..., :half], xr[..., half:]
    rot = jnp.concatenate([x1 * cos - x2 * sin, x1 * sin + x2 * cos], axis=-1)
    return jnp.concatenate([rot.astype(x.dtype), x[..., ROPE_DIM:]], axis=-1)

def banded_attention(q, k, v, half):
    *lead, L, Dh = q.shape
    blk = half
    nb = -(-L // blk)
    pad = nb * blk - L
    lead_pad = [(0, 0)] * len(lead)

    def blocks(t):
        t = jnp.pad(t, lead_pad + [(0, pad), (0, 0)])
        return t.reshape(*lead, nb, blk, Dh)

    def windows(t):
        tp = jnp.pad(t, lead_pad + [(1, 1), (0, 0), (0, 0)])
        return jnp.concatenate([tp[..., :-2, :, :], tp[..., 1:-1, :, :], tp[..., 2:, :, :]], axis=-2)

    qb = blocks(q)
    kw = windows(blocks(k))
    vw = windows(blocks(v))
    s = jnp.einsum("...nqd,...nkd->...nqk", qb, kw).astype(jnp.float32) * (1.0 / math.sqrt(Dh))
    n = jnp.arange(nb)[:, None, None]
    qi = n * blk + jnp.arange(blk)[None, :, None]
    ki = (n - 1) * blk + jnp.arange(3 * blk)[None, None, :]
    mask = (jnp.abs(ki - qi) <= half) & (ki >= 0) & (ki < L)
    s = jnp.where(mask, s, NEG_INF)
    lse = jax.nn.logsumexp(s, axis=-1)
    p = jnp.exp(s - lse[..., None])
    o = jnp.einsum("...nqk,...nkd->...nqd", p.astype(v.dtype), vw)
    o = o.reshape(*lead, nb * blk, Dh)[..., :L, :]
    lse = lse.reshape(*lead, nb * blk)[..., :L]
    return o, lse

def dilated_attention(q, k, v):
    B, H, S, Dh = q.shape
    outs, lses = [], []
    for window, dil in DILATED_PATTERNS:
        half = window // 2 // dil

        def to_strided(t):
            return t.reshape(B, H, S // dil, dil, Dh).swapaxes(2, 3)

        o, l = banded_attention(to_strided(q), to_strided(k), to_strided(v), half)
        outs.append(o.swapaxes(2, 3).reshape(B, H, S, Dh))
        lses.append(l.swapaxes(2, 3).reshape(B, H, S))
    w = jax.nn.softmax(jnp.stack(lses, axis=0), axis=0)
    out = jnp.einsum("pbhs,pbhsd->bhsd", w, jnp.stack(outs, axis=0).astype(jnp.float32))
    return out.astype(q.dtype)

def spatial_gating(u, v, ln_g, ln_b, w_s, b_s):
    B, S, _ = v.shape
    u = jax.nn.gelu(u, approximate=False)
    v = layer_norm_2(jax.nn.gelu(v, approximate=False), ln_g, ln_b)
    vc = v.reshape(B, S // CHUNK, CHUNK, N_SGU_GROUPS, SGU_GROUP_DIM)
    mixed = jnp.einsum("gts,bcsge->bctge", w_s, vc) + b_s.T[None, None, :, :, None]
    return u * mixed.reshape(B, S, D_SGU)

def second_inputs(seed: int = 0) -> dict:
    key = jax.random.key(seed)
    ks = jax.random.split(key, 20)
    f32 = jnp.float32

    def nrm(k, shape, scale):
        return jax.random.normal(k, shape, f32) * scale

    def gain(k, shape):
        return 1.0 + 0.02 * jax.random.normal(k, shape, f32)

    L = DEPTH
    return {
        "x": jax.random.normal(ks[0], (BATCH, SEQ, D_MODEL), f32),
        "norm_ffn1": gain(ks[1], (L, D_MODEL)),
        "ffn1_w_gate": nrm(ks[2], (L, D_MODEL, D_FF), D_MODEL ** -0.5),
        "ffn1_w_up": nrm(ks[3], (L, D_MODEL, D_FF), D_MODEL ** -0.5),
        "ffn1_w_down": nrm(ks[4], (L, D_FF, D_MODEL), D_FF ** -0.5),
        "norm_mix": gain(ks[5], (L, D_MODEL)),
        "w_in": nrm(ks[6], (L, D_MODEL, D_IN), D_MODEL ** -0.5),
        "sgu_ln_g": gain(ks[7], (L, D_SGU)),
        "sgu_ln_b": nrm(ks[8], (L, D_SGU), 0.02),
        "sgu_w": nrm(ks[9], (L, N_SGU_GROUPS, CHUNK, CHUNK), 0.5 * CHUNK ** -0.5),
        "sgu_b": gain(ks[10], (L, N_SGU_GROUPS, CHUNK)),
        "out_norm_attn": gain(ks[11], (L, D_ATTN)),
        "out_norm_sgu": gain(ks[12], (L, D_SGU)),
        "w_out": nrm(ks[13], (L, D_MIX, D_MODEL), D_MIX ** -0.5),
        "norm_ffn2": gain(ks[14], (L, D_MODEL)),
        "ffn2_w_gate": nrm(ks[15], (L, D_MODEL, D_FF), D_MODEL ** -0.5),
        "ffn2_w_up": nrm(ks[16], (L, D_MODEL, D_FF), D_MODEL ** -0.5),
        "ffn2_w_down": nrm(ks[17], (L, D_FF, D_MODEL), D_FF ** -0.5),
        "final_norm": gain(ks[18], (D_MODEL,)),
    }

def second_block(x, norm_ffn1, ffn1_w_gate, ffn1_w_up, ffn1_w_down, norm_mix, w_in,
              sgu_ln_g, sgu_ln_b, sgu_w, sgu_b, out_norm_attn, out_norm_sgu, w_out,
              norm_ffn2, ffn2_w_gate, ffn2_w_up, ffn2_w_down, final_norm):
    B, S, _ = x.shape
    positions = jnp.arange(S, dtype=jnp.int32)
    splits = [D_ATTN, 2 * D_ATTN, 3 * D_ATTN, 3 * D_ATTN + D_SGU]

    def heads(t):
        return t.reshape(B, S, N_ATTN_HEADS, HEAD_DIM).transpose(0, 2, 1, 3)

    for l in range(DEPTH):
        x = x + 0.5 * swiglu(rms_norm_2(x, norm_ffn1[l]), ffn1_w_gate[l], ffn1_w_up[l], ffn1_w_down[l])

        h = rms_norm_2(x, norm_mix[l])
        proj = h @ w_in[l]
        q, k, v, u, g = jnp.split(proj, splits, axis=-1)
        q = partial_rotary(heads(q), positions)
        k = partial_rotary(heads(k), positions)
        a = dilated_attention(q, k, heads(v))
        a = a.transpose(0, 2, 1, 3).reshape(B, S, D_ATTN)
        sg = spatial_gating(u, g, sgu_ln_g[l], sgu_ln_b[l], sgu_w[l], sgu_b[l])
        mixed = jnp.concatenate([rms_norm_2(a, out_norm_attn[l]), rms_norm_2(sg, out_norm_sgu[l])], axis=-1)
        x = x + mixed @ w_out[l]

        x = x + 0.5 * swiglu(rms_norm_2(x, norm_ffn2[l]), ffn2_w_gate[l], ffn2_w_up[l], ffn2_w_down[l])

    return rms_norm_2(x, final_norm)


_first_inputs = second_inputs


def second_inputs(seed=0):
    import zlib

    import numpy as np

    out = dict(_first_inputs(seed))
    spreads = {}
    factors = {'norm_ffn1': 4.481,
     'sgu_ln_g': 60.013,
     'sgu_ln_b': 64.0,
     'sgu_b': 32.711,
     'out_norm_attn': 18.215,
     'out_norm_sgu': 18.308,
     'norm_ffn2': 7.366,
     'final_norm': 8.476}
    for name, (base, spread) in spreads.items():
        noise = np.random.default_rng([zlib.crc32(name.encode()), seed]).standard_normal(out[name].shape)
        drawn = base * np.exp(spread * noise) if base else spread * noise
        out[name] = __import__('jax').numpy.asarray(drawn.astype(out[name].dtype))
    for name, factor in factors.items():
        out[name] = (out[name] * factor).astype(out[name].dtype)
    return out


_narrow_inputs = second_inputs


def second_inputs(seed=0):
    out = dict(_narrow_inputs(seed))
    wider = {'sgu_ln_g': 4.55, 'sgu_ln_b': 4.75, 'sgu_b': 4.5, 'out_norm_sgu': 3.04, 'final_norm': 3.25}
    for name, times in wider.items():
        mean = out[name].mean()
        out[name] = (mean + times * (out[name] - mean)).astype(out[name].dtype)
    return out


def setup_inputs(seed=0):
    out = dict(first_inputs(seed))
    for name, value in second_inputs(seed + 1).items():
        if name != "x":
            out[name + "_2"] = value
    return out


def reference(
    x, c, mod_w, mod_b, mix_norm_g, ffn_norm_g, ev_in_w, ev_dw_w, ev_dw_b, ev_ln_g, ev_ln_b,
    ev_q_g, ev_k_g, ev_out_w, od_in_w, od_conv_w, od_conv_b, od_rg_w, od_rg_b, od_ig_w, od_ig_b,
    od_lam, od_out_w, router_w, router_b, ex_w1, ex_w3, ex_w2, norm_ffn1_2, ffn1_w_gate_2,
    ffn1_w_up_2, ffn1_w_down_2, norm_mix_2, w_in_2, sgu_ln_g_2, sgu_ln_b_2, sgu_w_2, sgu_b_2,
    out_norm_attn_2, out_norm_sgu_2, w_out_2, norm_ffn2_2, ffn2_w_gate_2, ffn2_w_up_2,
    ffn2_w_down_2, final_norm_2,
):
    x = first_block(
        x, c, mod_w, mod_b, mix_norm_g, ffn_norm_g, ev_in_w, ev_dw_w, ev_dw_b, ev_ln_g, ev_ln_b,
        ev_q_g, ev_k_g, ev_out_w, od_in_w, od_conv_w, od_conv_b, od_rg_w, od_rg_b, od_ig_w,
        od_ig_b, od_lam, od_out_w, router_w, router_b, ex_w1, ex_w3, ex_w2,
    )
    return second_block(
        x, norm_ffn1_2, ffn1_w_gate_2, ffn1_w_up_2, ffn1_w_down_2, norm_mix_2, w_in_2,
        sgu_ln_g_2, sgu_ln_b_2, sgu_w_2, sgu_b_2, out_norm_attn_2, out_norm_sgu_2, w_out_2,
        norm_ffn2_2, ffn2_w_gate_2, ffn2_w_up_2, ffn2_w_down_2, final_norm_2,
    )


_drawn_inputs = setup_inputs


def setup_inputs(seed=0):
    import zlib

    import numpy as np

    out = dict(_drawn_inputs(seed))
    spreads = {}
    factors = {'od_rg_b': 8.0, 'od_ig_b': 3.741}
    for name, (base, spread) in spreads.items():
        noise = np.random.default_rng([zlib.crc32(name.encode()), seed]).standard_normal(out[name].shape)
        drawn = base * np.exp(spread * noise) if base else spread * noise
        out[name] = __import__('jax').numpy.asarray(drawn.astype(out[name].dtype))
    for name, factor in factors.items():
        out[name] = (out[name] * factor).astype(out[name].dtype)
    return out
```

```python
from contextlib import ExitStack

import numpy as np

import concourse.bass as bass
from concourse import mybir

F32 = mybir.dt.float32
ALU = mybir.AluOpType
ACT = mybir.ActivationFunctionType
X = mybir.AxisListType.X

T = 256
D = 1024
KC = D // 128
NE = 16
DFF = 2816
EPS = 1e-6
NSLOT = 5
NEG = -1e30

SHAPES = {
    "x": (1, T, D), "c": (1, D), "mod_w": (2, D, 6 * D), "mod_b": (2, 6 * D),
    "mix_norm_g": (2, D), "ffn_norm_g": (2, D), "ev_in_w": (1, D, 2560), "ev_dw_w": (1, 31, 512),
    "ev_dw_b": (1, 512), "ev_ln_g": (1, 512), "ev_ln_b": (1, 512), "ev_q_g": (1, 64), "ev_k_g": (1, 64),
    "ev_out_w": (1, D, D), "od_in_w": (1, D, 2 * D), "od_conv_w": (1, 4, D), "od_conv_b": (1, D),
    "od_rg_w": (1, 8, 128, 128), "od_rg_b": (1, D), "od_ig_w": (1, 8, 128, 128), "od_ig_b": (1, D),
    "od_lam": (1, D), "od_out_w": (1, D, D), "router_w": (D, NE), "router_b": (NE,),
    "ex_w1": (2, NE, D, 512), "ex_w3": (2, NE, D, 512), "ex_w2": (2, NE, 512, D),
    "norm_ffn1_2": (2, D), "ffn1_w_gate_2": (2, D, DFF), "ffn1_w_up_2": (2, D, DFF),
    "ffn1_w_down_2": (2, DFF, D), "norm_mix_2": (2, D), "w_in_2": (2, D, 2560),
    "sgu_ln_g_2": (2, 512), "sgu_ln_b_2": (2, 512), "sgu_w_2": (2, 4, 128, 128), "sgu_b_2": (2, 4, 128),
    "out_norm_attn_2": (2, 512), "out_norm_sgu_2": (2, 512), "w_out_2": (2, D, D),
    "norm_ffn2_2": (2, D), "ffn2_w_gate_2": (2, D, DFF), "ffn2_w_up_2": (2, D, DFF),
    "ffn2_w_down_2": (2, DFF, D), "final_norm_2": (D,),
}


def constants():
    p = np.arange(128)[:, None]
    f = np.arange(128)[None, :]
    out = {
        "ident": p == f,
        "ones": np.ones((128, 128)),
        "ntri": -(p >= f).astype(np.float32),
        "nones": -np.ones((128, 128)),
        "below": p < f,
        "negdiag": np.where(p < f, 0.0, NEG),
    }
    cnt, neg = [], []
    for th in range(2):
        q = th * 128 + p
        k = np.arange(T)[None, :]
        n = (np.abs(q - k) <= 64).astype(np.float32) + ((q - k) % 4 == 0) + ((q - k) % 16 == 0)
        cnt.append(n)
        neg.append(np.where(n > 0, 0.0, NEG))
    out["cnt"] = np.concatenate(cnt, 1)
    out["neg"] = np.concatenate(neg, 1)
    inv = np.float32(500000.0) ** (-np.arange(0, 16, 2, dtype=np.float32) / np.float32(16))
    ang = np.concatenate([(th * 128 + p).astype(np.float32) * inv[None, :] for th in range(2)], 1)
    out["cos"] = np.cos(ang.astype(np.float32))
    out["sin"] = np.sin(ang.astype(np.float32))
    i = np.arange(4)[:, None]
    j = np.arange(4)[None, :]
    out["first"] = np.broadcast_to((j < i).astype(np.float32).reshape(1, 16), (128, 16))
    out["eps"] = np.full((128, 1), EPS)
    return {n: np.ascontiguousarray(a, dtype=np.float32) for n, a in out.items()}


class Queue:

    def __init__(self, name, chained):
        self.name, self.chained = name, chained
        self.items, self.sem, self.n, self.last = [], None, 0, None

    def stage(self, sem):
        self.sem, self.n = sem, 0

    def add(self, fn, waits, signal=True, chain=None):
        waits = list(waits)
        if (self.chained if chain is None else chain) and self.last is not None:
            waits.append(self.last)
        tok = None
        if signal:
            self.n += 1
            tok = (self.sem, self.n)
            self.last = tok
        self.items.append((fn, waits, self.sem if signal else None, 1))
        return tok

    def add_dma(self, fn, waits, sem, value):
        self.items.append((fn, list(waits), sem, 16))
        return (sem, value)

    def emit(self, eng):
        seen = {}
        for fn, waits, sem, inc in self.items:
            for w in waits:
                if w is None:
                    continue
                s, v = w
                if seen.get(id(s), 0) < v:
                    eng.wait_ge(s, v)
                    seen[id(s)] = v
            if fn is None:
                continue
            ins = fn(eng)
            if sem is not None:
                ins.then_inc(sem, inc)


class Bank:

    def __init__(self, t):
        self.t, self.free = t, []


class Slot:
    def __init__(self, t, sem):
        self.t, self.sem, self.n, self.free = t, sem, 0, []


def program(nc, A, out, stop=None):
    ctx = ExitStack()
    with ctx:
        def sb(name, *shape):
            return ctx.enter_context(nc.sbuf_tensor(name, [128, *shape], F32))

        def sem(name):
            return ctx.enter_context(nc.semaphore(name))

        PE, AC, VE, PO, SP = Queue("pe", False), Queue("act", True), Queue("dve", True), Queue("pool", True), Queue("sp", False)

        def stage(name):
            for q in (PE, AC, VE, PO):
                q.stage(sem(f"s_{q.name}_{name}"))

        def pe(fn, *w, sig=False):
            return PE.add(fn, w, signal=sig)

        def ac(fn, *w):
            return AC.add(fn, w)

        def ve(fn, *w, chain=None):
            return VE.add(fn, w, chain=chain)

        def po(fn, *w):
            return PO.add(fn, w)

        def mm(o, lhsT, rhs, start, stop, *w, sig=False):
            return pe(lambda e: e.matmul(o, lhsT, rhs, start=start, stop=stop, skip_group_check=True), *w, sig=sig)

        def tr(o, i, *w, sig=False):
            return pe(lambda e: e.transpose(o, i, ident), *w, sig=sig)

        def act(o, i, func, *w, **kw):
            return ac(lambda e: e.activation(o, i, func, **kw), *w)

        def tt(o, a, b, op, *w, chain=None):
            return ve(lambda e: e.tensor_tensor(o, a, b, op), *w, chain=chain)

        def ts(o, a, s1, s2, op0, op1, *w, chain=None):
            if s2 is None:
                return ve(lambda e: e.tensor_scalar(o, a, s1, None, op0), *w, chain=chain)
            return ve(lambda e: e.tensor_scalar(o, a, s1, s2, op0, op1), *w, chain=chain)

        def stt(o, a, s, b, op0, op1, *w, chain=None):
            return ve(lambda e: e.scalar_tensor_tensor(out=o, in0=a, scalar=s, in1=b, op0=op0, op1=op1), *w, chain=chain)

        def red(o, i, op, *w):
            return ve(lambda e: e.tensor_reduce(o, i, X, op), *w)

        def recip(o, i, *w):
            return ve(lambda e: e.reciprocal(o, i), *w)

        def vcopy(o, i, *w):
            return ve(lambda e: e.tensor_copy(o, i), *w)

        def bc(ap, n, axis=1):
            a = ap.unsqueeze(axis)
            shape = list(a.shape)
            shape[axis] = n
            return a.to_broadcast(shape)

        consts = {n: a.shape[1] for n, a in constants().items()}
        cst = sb("cst", sum(consts.values()))
        C, at = {}, 0
        for n, w in consts.items():
            C[n] = cst[:, at:at + w]
            at += w
        ident, ones = C["ident"], C["ones"]
        eps = C["eps"]
        xres = sb("xres", 2, D)
        hT = sb("hT", KC, T)
        catT = sb("catT", KC, T)
        uT = sb("uT", 2, 4, T)
        acc = sb("acc", 2, D)
        gbc = sb("gbc", 2, D)
        cbc = sb("cbc", KC, 128)
        rows = sb("rows", 4, 128)
        cols = sb("cols", 4, 128)
        crow = sb("crow", 128)
        condT = sb("condT", KC)
        modc = sb("modc", 2, 4, KC)
        rw = sb("rw", KC, NE)
        rb = sb("rb", NE)
        qkg = sb("qkg", 2, 64)
        small = sb("small", 512)
        lnc = sb("lnc", 8 * 6)
        arena = sb("arena", 14336)
        slots = [Slot(sb(f"slot{i}", 4096), sem(f"s_slot{i}")) for i in range(NSLOT)]
        banks = [Bank(ctx.enter_context(nc.psum_tensor(f"bank{i}", [128, 512], F32))) for i in range(8)]

        def region(at, *shape):
            n = int(np.prod(shape))
            a = arena[:, at:at + n]
            if len(shape) == 1:
                return a
            names = "abcd"[:len(shape)]
            return a.rearrange(f"p ({' '.join(names)}) -> p {' '.join(names)}", **dict(zip(names, shape)))

        s_cst, s_x, s_rows, s_bc = sem("s_cst"), sem("s_x"), sem("s_rows"), sem("s_bc")
        s_g = [sem("s_g0"), sem("s_g1")]
        t_cst = AC.add_dma(lambda e: e.dma_start(cst[:, :], A["constants"]), [], s_cst, 16)

        def row_tile(k, parts):
            at = 0
            for src in parts:
                n = src.shape[0]
                AC.add_dma(lambda e, at=at, n=n, src=src: e.dma_start(rows[at:at + n, k, :], src), [], s_rows, 0)
                row_tile.n += 16
                at += n
            return at
        row_tile.n = 0

        def flat(name):
            a = A[name]
            k = len(a.shape)
            if k == 1:
                return a.rearrange("(k p) -> k p", p=128)
            if k == 2:
                return a.rearrange("a (k p) -> (a k) p", p=128)
            return a.rearrange("a b (k p) -> (a b k) p", p=128)

        crow8 = crow[0:8, :]
        AC.add_dma(lambda e: e.dma_start(crow8, flat("c")), [], s_rows, 0)
        row_tile.n += 16
        row_tile(0, [flat(n) for n in ("mix_norm_g", "ffn_norm_g", "mod_b")])
        row_tile(1, [flat(n) for n in ("ev_dw_w", "ev_dw_b")])
        row_tile(2, [flat(n) for n in ("ev_ln_g", "ev_ln_b", "od_conv_w", "od_conv_b", "od_rg_b", "od_ig_b", "od_lam",
                                       "norm_ffn1_2", "norm_mix_2", "sgu_b_2", "out_norm_attn_2")])
        n3 = row_tile(3, [flat(n) for n in ("out_norm_sgu_2", "norm_ffn2_2")])
        t_rows = (s_rows, row_tile.n)
        t_x = AC.add_dma(lambda e: e.dma_start(xres[:, :, :], A["x"].rearrange("a (t p) d -> p (a t) d", p=128)),
                         [], s_x, 16)
        nbc = 0
        for dst, src in ((qkg[:, 0, :], A["ev_q_g"][0, :]), (qkg[:, 1, :], A["ev_k_g"][0, :]),
                         (rb[:, :], A["router_b"])):
            AC.add_dma(lambda e, dst=dst, src=src: e.dma_start(dst, src.partition_broadcast(128)), [], s_bc, 0)
            nbc += 16
        AC.add_dma(lambda e: e.dma_start(rw[:, :, :], A["router_w"].rearrange("(k p) n -> p k n", p=128)),
                   [], s_bc, 0)
        t_bc = (s_bc, nbc + 16)

        turn = [0]

        def load(*parts):
            s = slots[turn[0] % NSLOT]
            turn[0] += 1
            at, views = 0, []
            for k, n, src in parts:
                v = s.t[:, at:at + k * n].rearrange("p (k n) -> p k n", k=k)
                SP.add_dma(lambda e, v=v, src=src: e.dma_start(v, src), s.free, s.sem, 0)
                s.n += 16
                at += k * n
                views.append(v)
            s.tok, s.views, s.free = (s.sem, s.n), views, []
            return s

        def w_cols(w, c0, n):
            return (w.shape[0] // 128, n, w.rearrange("(k p) n -> p k n", p=128)[:, :, c0:c0 + n])

        def w_rows(w, r0, k):
            return (k, w.shape[1], w[r0:r0 + 128 * k, :].rearrange("(k p) n -> p k n", p=128))

        turns = {}

        def bank(*among):
            key = among
            i = turns.get(key, 0)
            turns[key] = i + 1
            return banks[among[i % len(among)]]

        def take(b):
            w, b.free = b.free, []
            return w

        def free(b, *toks):
            b.free = b.free + [t for t in toks if t is not None]

        def tok_major(src, w, b, *waits, n=512):
            k = w.shape[1]
            for c in range(k):
                t = mm(b.t[:, 0:n], src(c), w[:, c, :], c == 0, c == k - 1, *(waits if c == 0 else ()), sig=c == k - 1)
            return t

        def chan_major(src, w, f, o, *waits, sig=True):
            k = w.shape[1]
            for c in range(k):
                t = mm(o, w[:, c, f * 128:(f + 1) * 128], src[:, c, :], c == 0, c == k - 1,
                       *(waits if c == 0 else ()), sig=sig and c == k - 1)
            return t

        state = {"x": [t_x, t_x], "hT": None, "cat": []}

        def rstd(at, n, of, *w):
            a = act(small[:, at:at + n], small[:, at:at + n], ACT.Sqrt, *w, scale=1.0 / of, bias=eps)
            return recip(small[:, at + n:at + 2 * n], small[:, at:at + n], a)

        def norm_T(scale, shift, *waits):
            xn = region(12288, 2, D)
            tl = []
            for th in range(2):
                tl.append(act(xn[:, th, :], xres[:, th, :], ACT.Square, *state["x"], state["arena"],
                              accum_out=small[:, th:th + 1]))
            r = rstd(0, 2, D, tl[-1])
            ts_ = [ts(xn[:, 0, :], xres[:, 0, :], small[:, 2:3], None, ALU.mult, None, r),
                   act(xn[:, 1, :], xres[:, 1, :], ACT.Copy, r, scale=small[:, 3:4])]
            last = []
            for c in range(KC):
                b = bank(0, 1, 2, 3)
                w = take(b)
                for th in range(2):
                    t = tr(b.t[:, th * 128:(th + 1) * 128], xn[:, th, c * 128:(c + 1) * 128], *w, ts_[th],
                           *state.get("hT_free", []), sig=th == 1)
                o = hT[:, c, :]
                if c % 2:
                    if shift is None:
                        e = act(o, b.t[:, 0:T], ACT.Copy, t, *waits, scale=scale[:, c:c + 1])
                    else:
                        e = act(o, b.t[:, 0:T], ACT.Identity, t, *waits, scale=scale[:, c:c + 1], bias=shift[:, c:c + 1])
                else:
                    if shift is None:
                        e = ts(o, b.t[:, 0:T], scale[:, c:c + 1], None, ALU.mult, None, t, *waits)
                    else:
                        e = ts(o, b.t[:, 0:T], scale[:, c:c + 1], shift[:, c:c + 1], ALU.mult, ALU.add, t, *waits)
                free(b, e)
                last.append(e)
            state["arena"] = t
            state["hT"] = last[-2:]
            return last[-2:]

        stage("pre")
        state["arena"] = None
        t_cols = []
        for k in range(4):
            n = (128, 128, 120, n3)[k]
            b = bank(0, 1, 2, 3)
            t = pe(lambda e, b=b, k=k, n=n: e.transpose(b.t[:, 0:n], rows[0:n, k, :], ident[0:n, 0:n]),
                   t_rows, t_cst, *take(b), sig=True)
            t_cols = vcopy(cols[:, k, 0:n], b.t[:, 0:n], t)
            free(b, t_cols)
        c_mix = cols[:, 0, 0:16].rearrange("p (l k) -> p l k", l=2)
        c_ffn = cols[:, 0, 16:32].rearrange("p (l k) -> p l k", l=2)
        c_modb = cols[:, 0, 32:128].rearrange("p (l v k) -> p l v k", l=2, v=6)
        c_dw = cols[:, 1, 0:124].rearrange("p (t k) -> p t k", k=4)
        c_dwb = cols[:, 1, 124:128]
        c2, at2 = {}, 0
        for n, w in (("ln_g", 4), ("ln_b", 4), ("cw", 32), ("cb", 8), ("rgb", 8), ("igb", 8), ("lam", 8),
                     ("ffn1", 16), ("mix", 16), ("sgub", 8), ("attn", 8)):
            c2[n] = cols[:, 2, at2:at2 + w]
            at2 += w
        c2["sgu"], c2["ffn2"] = cols[:, 3, 0:8], cols[:, 3, 8:24]

        t = act(crow8, crow8, ACT.Silu, t_rows)
        b = bank(0, 1, 2, 3)
        t = pe(lambda e, b=b: e.transpose(b.t[:, 0:8], crow8, ident[0:8, 0:8]), t, *take(b), sig=True)
        t_cond = vcopy(condT[:, :], b.t[:, 0:8], t)
        free(b, t_cond)
        t_cbc = vcopy(cbc[:, :, :], bc(condT[:, :], 128, 2), t_cond)

        def mod_cols(l, vs, b):
            w = take(b)
            for v in vs:
                slot_of = {0: 0, 1: 1, 3: 2, 4: 3}[v]
                for half in range(2):
                    s = load(w_cols(A["mod_w"][l], v * D + half * 512, 512))
                    for f in range(4):
                        j = half * 4 + f
                        for c in range(KC):
                            t = mm(b.t[:, j:j + 1], s.views[0][:, c, f * 128:(f + 1) * 128], condT[:, c:c + 1],
                                   c == 0, c == KC - 1, s.tok, t_cond, *w, sig=(c == KC - 1))
                    s.free = [t]
                o = modc[:, l, slot_of, :]
                t = tt(o, b.t[:, 0:8], c_modb[:, l, v, :], ALU.add, t, t_cols)
                w = [t]
                if v in (1, 4):
                    g = (c_mix if v == 1 else c_ffn)[:, l, :]
                    t = stt(o, o, 1.0, g, ALU.add, ALU.mult)
            free(b, t)
            return t

        def mod_row(l, v, k, b0, b1):
            w = state.get(("gbc", k), [])
            gn[k] += 16
            td = AC.add_dma(lambda e: e.dma_start(gbc[:, k, :], A["mod_b"][l, v * D:(v + 1) * D].partition_broadcast(128)),
                            w, s_g[k], gn[k])
            for half, b in enumerate((b0, b1)):
                s = load(w_cols(A["mod_w"][l], v * D + half * 512, 512))
                t = tok_major(lambda c: cbc[:, c, :], s.views[0], b, s.tok, t_cbc, *take(b))
                s.free = [t]
                o = gbc[:, k, half * 512:(half + 1) * 512]
                t = tt(o, b.t[:, :], o, ALU.add, t, td)
                free(b, t)
            return t

        gn = [0, 0]

        def residual(views, gate, *waits):
            done = []
            for nh, s in enumerate(views):
                for th in range(2):
                    b = bank(4, 5, 6, 7)
                    t = tok_major(lambda c: catT[:, c, th * 128:(th + 1) * 128], s.views[0], b, s.tok, *waits, *take(b))
                    o = xres[:, th, nh * 512:(nh + 1) * 512]
                    if gate is None:
                        t2 = tt(o, b.t[:, :], o, ALU.add, t)
                        free(b, t2)
                    else:
                        tmp = acc[:, th, nh * 512:(nh + 1) * 512]
                        t2 = tt(tmp, b.t[:, :], gate[:, nh * 512:(nh + 1) * 512], ALU.mult, t)
                        free(b, t2)
                        t2 = tt(o, o, tmp, ALU.add)
                    done.append(t2)
                s.free = [t]
            state["x"] = [done[-1]]
            state["cat_free"] = [t]
            return done[-1]

        class Feed:
            def __init__(self):
                self.pending, self.n, self.last_u = None, 0, {}

            def hidden(self, s1, s3, f, buf, waits):
                b = bank(0, 1, 2, 3)
                w = take(b)
                chan_major(hT, s1.views[0], f, b.t[:, 0:T], s1.tok, *waits, *w, *state["hT"], sig=False)
                t = chan_major(hT, s3.views[0], f, b.t[:, T:2 * T], s3.tok, sig=True)
                o = uT[:, buf, f, :]
                a = act(o, b.t[:, 0:T], ACT.Silu, t, *self.last_u.get(buf, []))
                v = tt(o, o, b.t[:, T:2 * T], ALU.mult, a)
                free(b, v)
                return t, v

            def down(self):
                s2, us, buf, nf, first, last, evac = self.pending
                self.pending = None
                for th in range(2):
                    for nh in range(2):
                        b = banks[4 + th * 2 + nh]
                        w = take(b) if first else []
                        for f in range(nf):
                            t = mm(b.t[:, :], uT[:, buf, f, th * 128:(th + 1) * 128],
                                   s2.views[0][:, f, nh * 512:(nh + 1) * 512], first and f == 0, last and f == nf - 1,
                                   s2.tok, us[f], *w, sig=f == nf - 1)
                        if evac is not None:
                            free(b, evac(th, nh, b, t))
                s2.free = [t]
                self.last_u[buf] = [t]

            def group(self, p1, p3, p2, nf, first, last, evac, waits=()):
                s1, s3 = load(p1), load(p3)
                buf = self.n % 2
                self.n += 1
                us = []
                for f in range(nf):
                    t, v = self.hidden(s1, s3, f, buf, waits)
                    us.append(v)
                    if f == 0 and self.pending is not None:
                        self.down()
                s1.free, s3.free = [t], [t]
                state["hT_free"] = [t]
                self.pending = (load(p2), us, buf, nf, first, last, evac)

            def finish(self):
                self.down()

        feed = Feed()

        def moe(l, k):
            gate_row = gbc[:, k, :]
            b = bank(0, 1, 2, 3)
            w = take(b)
            for th in range(2):
                for c in range(KC):
                    t = mm(b.t[:, th * NE:(th + 1) * NE], hT[:, c, th * 128:(th + 1) * 128], rw[:, c, :],
                           c == 0, c == KC - 1, *w, *state["hT"], t_bc, sig=c == KC - 1)
            S = lambda at, n: small[:, 64 + at:64 + at + n]
            score, biased = S(0, 32), S(32, 32)
            t = act(score, b.t[:, 0:32], ACT.Sigmoid, t, state.get("gates"))
            free(b, t)
            v2 = lambda a, n: a.rearrange("p (t n) -> p t n", t=2)
            v8 = lambda a: a.rearrange("p (g n) -> p g n", g=8)
            t = tt(v2(biased, 16), v2(score, 16), bc(rb[:, :], 2), ALU.add, t, t_bc)
            b8 = v8(biased)
            ps = v8(S(64, 48))
            tt(ps[:, :, 0:3], b8[:, :, 0:3], b8[:, :, 1:4], ALU.add)
            tt(ps[:, :, 3:5], b8[:, :, 0:2], b8[:, :, 2:4], ALU.add)
            tt(ps[:, :, 5:6], b8[:, :, 0:1], b8[:, :, 3:4], ALU.add)
            gs = S(112, 8)
            red(gs, ps, ALU.max)

            def below(o, vals, g, limit):
                v = vals.rearrange("p (g n) -> p g n", g=g)
                vi, vj = bc(v, 4, 3), bc(v, 4, 2)
                gt = S(128, 16 * g)
                ge = S(256, 16 * g)
                g4 = lambda a: a.rearrange("p (g i j) -> p g i j", i=4, j=4)
                g16 = lambda a: a.rearrange("p (g i) -> p g i", i=16)
                tt(g4(gt), vj, vi, ALU.is_gt)
                tt(g4(ge), vj, vi, ALU.is_ge)
                tt(ge, ge, gt, ALU.subtract)
                tt(g16(ge), g16(ge), bc(C["first"], g), ALU.mult)
                tt(gt, ge, gt, ALU.add)
                red(o, gt.rearrange("p (gi j) -> p gi j", j=4), ALU.add)
                return ts(o, o, float(limit), None, ALU.is_lt, None)

            gm, em = S(120, 8), S(384, 32)
            below(gm, gs, 2, 1)
            below(em, biased, 8, 2)
            tt(v8(em), v8(em), bc(gm, 4, 2), ALU.mult)
            tt(em, em, score, ALU.mult)
            den = S(416, 2)
            red(den, v2(em, 16), ALU.add)
            recip(den, den)
            t_gate = tt(v2(em, 16), v2(em, 16), bc(den, 16, 2), ALU.mult)

            for e in range(NE):
                def evac(th, nh, b, t, e=e):
                    o = acc[:, th, nh * 512:(nh + 1) * 512]
                    g = em[:, th * NE + e:th * NE + e + 1]
                    if e == 0:
                        return ts(o, b.t[:, :], g, None, ALU.mult, None, t, t_gate)
                    return stt(o, b.t[:, :], g, o, ALU.mult, ALU.add, t)
                feed.group(w_cols(A["ex_w1"][l, e], 0, 512), w_cols(A["ex_w3"][l, e], 0, 512),
                           w_rows(A["ex_w2"][l, e], 0, 4), 4, True, True, evac)
            feed.finish()
            for th in range(2):
                tt(acc[:, th, :], acc[:, th, :], gate_row, ALU.mult)
                t = tt(xres[:, th, :], xres[:, th, :], acc[:, th, :], ALU.add)
            state["x"] = [t]
            state["gates"] = t
            state[("gbc", k)] = [t]

        def ffn(l, pre):
            wg, wu, wd = A[pre + "_w_gate_2"][l], A[pre + "_w_up_2"][l], A[pre + "_w_down_2"][l]

            def evac(th, nh, b, t):
                o = xres[:, th, nh * 512:(nh + 1) * 512]
                t = stt(o, b.t[:, :], 0.5, o, ALU.mult, ALU.add, t)
                state["x"] = [t]
                return t
            for g in range(6):
                nf = 4 if g < 5 else 2
                feed.group(w_cols(wg, g * 512, nf * 128), w_cols(wu, g * 512, nf * 128), w_rows(wd, g * 512, nf),
                           nf, g == 0, g == 5, evac if g == 5 else None)
            feed.finish()

        t = mod_cols(0, (0, 1), banks[0])
        norm_T(modc[:, 0, 1, :], modc[:, 0, 0, :], t)

        stage("even")
        upad = region(0, 4, 286)
        u = region(1152, 4, T)
        qs = region(2176, 2, 512)
        ks = region(3200, 2, 512)
        vs = region(4224, 2, 512)
        qT = region(5248, 4, T)
        kT = region(6272, 4, T)
        L = region(7296, 6, 512)
        sq = region(10368, 1024)
        W = region(2176, 2, 512)

        t_pad = po(lambda e: e.memset(upad[:, :, 0:30], 0.0), state["arena"])
        s = load(w_cols(A["ev_in_w"][0], 0, 512))
        ab = [banks[4], banks[5]]
        ta = []
        for f in range(4):
            b = ab[f // 2]
            w = take(b) if f % 2 == 0 else []
            ta.append(chan_major(hT, s.views[0], f, b.t[:, (f % 2) * T:(f % 2 + 1) * T], s.tok, *w, *state["hT"]))
        s.free = [ta[-1]]
        s = load(w_cols(A["ev_in_w"][0], 512, 512))
        for f in range(4):
            if f % 2 == 0:
                b = banks[6 + f // 2]
                w = take(b)
            t = chan_major(hT, s.views[0], f, b.t[:, (f % 2) * T:(f % 2 + 1) * T], s.tok, *w)
            if f % 2:
                a = act(u[:, f - 1:f + 1, :], b.t[:, :].rearrange("p (a n) -> p a n", a=2), ACT.Sigmoid, t, state["arena"])
                free(b, a)
                va = tt(upad[:, f - 1:f + 1, 30:286], u[:, f - 1:f + 1, :],
                        ab[f // 2].t[:, :].rearrange("p (a n) -> p a n", a=2), ALU.mult, a, ta[f])
                free(ab[f // 2], va)
        s.free = [t]
        t_u = va
        tq = {}
        for n, (name, dst) in enumerate((("q", qs), ("k", ks), ("v", vs))):
            s = load(w_cols(A["ev_in_w"][0], 1024 + n * 512, 512))
            for th in range(2):
                b = bank(0, 1, 2, 3)
                t = tok_major(lambda c: hT[:, c, th * 128:(th + 1) * 128], s.views[0], b, s.tok, *take(b))
                tq[name, th] = act(dst[:, th, :], b.t[:, :], ACT.Copy, t)
                free(b, tq[name, th])
            s.free = [t]
        state["hT_free"] = [t]
        ts(qkg[:, 0, :], qkg[:, 0, :], 0.125, None, ALU.mult, None, t_bc)
        for name, dst, g in (("q", qs, 0), ("k", ks, 1)):
            hv = dst[:, :, :].rearrange("p t (h d) -> p (t h) d", d=64)
            sv = sq.rearrange("p (h d) -> p h d", d=64)
            tt(sv, hv, hv, ALU.mult, tq[name, 1])
            t = red(small[:, 32:48], sv, ALU.add)
            t = act(small[:, 32:48], small[:, 32:48], ACT.Sqrt, t, scale=1.0 / 64, bias=eps)
            recip(small[:, 48:64], small[:, 32:48], t)
            tt(hv, hv, bc(small[:, 48:64], 64, 2), ALU.mult)
            t = tt(hv, hv, bc(qkg[:, g, :], 16), ALU.mult)
            dT = (qT, kT)[g]
            for pr in range(2):
                b = banks[4 + 2 * g + pr]
                w = take(b)
                for a2 in range(2):
                    for th in range(2):
                        c = pr * 2 + a2
                        tp = tr(b.t[:, a2 * T + th * 128:a2 * T + (th + 1) * 128], dst[:, th, c * 128:(c + 1) * 128],
                                t, *w, sig=True)
                tp = act(dT[:, pr * 2:pr * 2 + 2, :], b.t[:, :].rearrange("p (a n) -> p a n", a=2), ACT.Copy, tp)
                free(b, tp)
        t_qk = tp
        tz = {}
        for par in range(2):
            r = slice(64 * par, 64 * par + 64)
            for j in range(2):
                b = banks[3 * par + j]
                w = take(b)
                for m in range(2):
                    tz[par, j] = mm(b.t[:, m * T:(m + 1) * T], kT[r, 2 * j + m, 0:128], qT[r, 2 * j + m, :],
                                    m == 0, m == 1, t_qk, *w, sig=m == 1)
            b = banks[3 * par + 2]
            w = take(b)
            for m in range(4):
                tz[par, 2] = mm(b.t[:, m * 128:(m + 1) * 128], kT[r, m, 128:256], qT[r, m, 128:256],
                                m == 0, m == 3, t_qk, *w, sig=m == 3)
        def diag(ap, j):
            if j == 2:
                return ap.rearrange("p (m q) -> p m q", q=128)
            return ap.rearrange("p (m n q) -> p m n q", m=2, q=128)[:, :, 0, :]
        def off(ap):
            return ap.rearrange("p (m n q) -> p m n q", m=2, q=128)[:, :, 1, :]
        tl = {}
        ta6 = {}
        for i in range(6):
            par, j = i // 3, i % 3
            t = act(L[:, i, :], banks[i].t[:, :], ACT.Abs, tz[par, j])
            t = act(L[:, i, :], L[:, i, :], ACT.Exp, scale=-1.0)
            ta6[i] = act(L[:, i, :], L[:, i, :], ACT.Ln, bias=1.0)
        for i in range(6):
            par, j = i // 3, i % 3
            t = stt(L[:, i, :], banks[i].t[:, :], 0.0, L[:, i, :], ALU.max, ALU.add, ta6[i])
            d = diag(L[:, i, :], j)
            tl[i] = tt(d, d, bc(C["below"], d.shape[1]), ALU.mult)
        tR = {}
        for par in range(2):
            for j in (2, 0, 1):
                i = 3 * par + j
                tR[i] = mm(banks[i].t[:, :], C["ntri"], L[:, i, :], False, True, tl[i], tl[3 * par + 2], sig=True)
                if j < 2:
                    tR[i] = mm(off(banks[i].t[:, :]), C["nones"],
                               L[:, 3 * par + 2, j * 256:(j + 1) * 256].rearrange("p (m q) -> p m q", q=128),
                               False, True, tl[3 * par + 2], sig=True)
        tw = {}
        t_tri = tR[4] if tR[4][1] > tR[5][1] else tR[5]
        for i in (2, 0, 1, 5, 3, 4):
            j = i % 3
            d = diag(L[:, i, :], j)
            t = tt(d, diag(banks[i].t[:, :], j), bc(C["negdiag"], d.shape[1]), ALU.add, t_tri)
            if j < 2:
                act(off(L[:, i, :]), off(banks[i].t[:, :]), ACT.Exp, t)
            tw[i] = act(d, d, ACT.Exp, t)
            free(banks[i], tw[i])
        for ch in range(4):
            if ch % 2 == 0:
                b = banks[6 + ch // 2]
                w = take(b)
            c0 = (ch % 2) * T
            for par in range(2):
                h = 2 * ch + par
                r = slice(64 * par, 64 * par + 64)
                i0, i2 = 3 * par + ch // 2, 3 * par + 2
                mm(b.t[r, c0:c0 + T], vs[:, 0, h * 64:(h + 1) * 64], L[:, i0, (ch % 2) * T:(ch % 2 + 1) * T],
                   ch % 2 == 0, False, tw[i0], tq["v", 1], *w)
                t = mm(b.t[r, c0 + 128:c0 + T], vs[:, 1, h * 64:(h + 1) * 64], L[:, i2, ch * 128:(ch + 1) * 128],
                       False, True, tw[i2], sig=par == 1)
            if ch % 2:
                t_o = act(catT[:, 3 + ch:5 + ch, :], b.t[:, :].rearrange("p (a n) -> p a n", a=2), ACT.Copy, t)
                free(b, t_o)

        cur = {}
        for k in range(31):
            for c in range(4):
                if k == 0:
                    cur[c] = ts(u[:, c, :], upad[:, c, 0:T], c_dw[:, 0, c:c + 1], c_dwb[:, c:c + 1], ALU.mult, ALU.add,
                                t_u, t_pad, t_cols, chain=False)
                else:
                    cur[c] = stt(u[:, c, :], upad[:, c, k:k + T], c_dw[:, k, c:c + 1], u[:, c, :], ALU.mult, ALU.add,
                                 cur[c], chain=False)
        t_g0 = mod_row(0, 2, 0, banks[0], banks[1])
        t_m0 = mod_cols(0, (3, 4), banks[2])
        t_m1 = mod_cols(1, (0, 1, 3, 4), banks[3])
        b = banks[4]
        w = take(b)
        for c in range(4):
            t = mm(b.t[:, 0:T], ones, u[:, c, :], c == 0, c == 3, cur[3], *w, sig=c == 3)
        t = stt(u, bc(b.t[:, 0:T], 4), -1.0 / 512, u, ALU.mult, ALU.add, t)
        free(b, t)
        t = act(region(2176, 4, T), u, ACT.Square, t)
        b = banks[5]
        w = take(b)
        for c in range(4):
            t = mm(b.t[:, 0:T], ones, region(2176, 4, T)[:, c, :], c == 0, c == 3, t, *w, sig=c == 3)
        t = act(sq[:, 0:T], b.t[:, 0:T], ACT.Sqrt, t, scale=1.0 / 512, bias=eps)
        free(b, t)
        recip(sq[:, 0:T], sq[:, 0:T], t)
        t = tt(u, u, bc(sq[:, 0:T], 4), ALU.mult)
        for c in range(4):
            t_c = act(catT[:, c, :], u[:, c, :], ACT.Silu, t, scale=c2["ln_g"][:, c:c + 1], bias=c2["ln_b"][:, c:c + 1])
        state["arena"] = t_c
        w2 = [load(w_cols(A["ev_out_w"][0], n * 512, 512)) for n in range(2)]
        t = residual(w2, gbc[:, 0, :], t_c, t_o, t_g0)
        state["gbc", 0] = [t]
        t_g1 = mod_row(0, 5, 1, banks[0], banks[1])
        norm_T(modc[:, 0, 3, :], modc[:, 0, 2, :], t_m0)
        stage("moe0")
        if stop != "even":
            moe(0, 1)

            t_g0 = mod_row(1, 2, 0, banks[0], banks[1])
            t_g1 = mod_row(1, 5, 1, banks[2], banks[3])
            norm_T(modc[:, 1, 1, :], modc[:, 1, 0, :], t_m1)
            stage("odd")
        if stop not in ("even", "moe0"):
            xb = region(0, 8, 259)
            xc = region(2080, 8, T)
            rr = region(4128, 8, T)
            ii = region(6176, 8, T)
            tn = region(8224, 8, T)
            gy = region(10272, 8, T)
            N8 = lambda i: lnc[:, 8 * i:8 * i + 8]
            lam = c2["lam"]
            t = act(N8(0), lam, ACT.Abs, t_cols)
            t = act(N8(0), N8(0), ACT.Exp, scale=-1.0)
            ts(N8(1), N8(0), 2.0, None, ALU.add, None, t)
            recip(N8(1), N8(1))
            tt(N8(1), N8(1), N8(0), ALU.mult)
            tt(N8(2), N8(1), N8(1), ALU.mult)
            ts(N8(3), N8(2), 1.0 / 19, None, ALU.mult, None)
            for k in range(17, 1, -2):
                stt(N8(3), N8(3), 1.0 / k, N8(2), ALU.add, ALU.mult)
            ts(N8(3), N8(3), 1.0, -16.0, ALU.add, ALU.mult)
            tt(N8(3), N8(3), N8(1), ALU.mult)
            ts(N8(4), lam, 0.0, 8.0, ALU.min, ALU.mult)
            t_c8 = tt(N8(3), N8(3), N8(4), ALU.add)
            c8 = N8(3)
            t_pad = po(lambda e: e.memset(xb[:, :, 0:3], 0.0), state["arena"])
            tx = []
            for half in range(2):
                s = load(w_cols(A["od_in_w"][0], D + half * 512, 512))
                for f in range(4):
                    if f % 2 == 0:
                        b = bank(4, 5, 6, 7)
                        w = take(b)
                    t = chan_major(hT, s.views[0], f, b.t[:, (f % 2) * T:(f % 2 + 1) * T], s.tok, *w, *state["hT"])
                    if f % 2:
                        ch = half * 4 + f - 1
                        a = act(xb[:, ch:ch + 2, 3:259], b.t[:, :].rearrange("p (a n) -> p a n", a=2), ACT.Copy, t,
                                state["arena"])
                        free(b, a)
                        tx += [a, a]
                s.free = [t]
            cur = {}
            for half in range(2):
                for k in range(4):
                    for ch in range(half * 4, half * 4 + 4):
                        sc = c2["cw"][:, k * 8 + ch:k * 8 + ch + 1]
                        if k == 0:
                            cur[ch] = ts(xc[:, ch, :], xb[:, ch, 0:T], sc, c2["cb"][:, ch:ch + 1], ALU.mult, ALU.add,
                                         tx[ch], t_pad, chain=False)
                        else:
                            cur[ch] = stt(xc[:, ch, :], xb[:, ch, k:k + T], sc, xc[:, ch, :], ALU.mult, ALU.add,
                                          cur[ch], chain=False)
            sy = [load(w_cols(A["od_in_w"][0], half * 512, 512)) for half in range(2)]
            for half in range(2):
                s = sy[half]
                for f in range(4):
                    if f % 2 == 0:
                        b = bank(4, 5, 6, 7)
                        w = take(b)
                    t = chan_major(hT, s.views[0], f, b.t[:, (f % 2) * T:(f % 2 + 1) * T], s.tok, *w)
                    if f % 2:
                        ch = half * 4 + f - 1
                        a = act(gy[:, ch:ch + 2, :], b.t[:, :].rearrange("p (a n) -> p a n", a=2),
                                ACT.Gelu_apprx_tanh, t)
                        free(b, a)
                s.free = [t]
            state["hT_free"] = [t]
            sg = load((8, 128, A["od_rg_w"][0].rearrange("b k j -> k b j")), (8, 128, A["od_ig_w"][0].rearrange("b k j -> k b j")))
            for ch in range(8):
                for n, (dst, bias) in enumerate(((rr, "rgb"), (ii, "igb"))):
                    b = bank(0, 1, 2, 3)
                    t = mm(b.t[:, 0:T], sg.views[n][:, ch, :], xc[:, ch, :], True, True, sg.tok, cur[ch], *take(b), sig=True)
                    a = act(dst[:, ch, :], b.t[:, 0:T], ACT.Sigmoid, t, bias=c2[bias][:, ch:ch + 1])
                    free(b, a)
            sg.free = [t]
            for half in range(2):
                h4 = slice(half * 4, half * 4 + 4)
                t = tt(rr[:, h4, :], rr[:, h4, :], bc(c8[:, h4], T, 2), ALU.mult, a, t_c8)
                act(tn[:, h4, :], rr[:, h4, :], ACT.Tanh, t, scale=-1.0)
                t_a = act(rr[:, h4, :], rr[:, h4, :], ACT.Exp)
                xb8 = xb[:, :, 0:T]
                ts(xb8[:, h4, :], tn[:, h4, :], 1.0, None, ALU.add, None, t_a)
                recip(xb8[:, h4, :], xb8[:, h4, :])
                t = tt(tn[:, h4, :], tn[:, h4, :], xb8[:, h4, :], ALU.mult)
                t_s = act(tn[:, h4, :], tn[:, h4, :], ACT.Sqrt, t, scale=2.0)
                tt(ii[:, h4, :], ii[:, h4, :], xc[:, h4, :], ALU.mult)
                tt(ii[:, h4, :], ii[:, h4, :], tn[:, h4, :], ALU.mult, t_s)
                for ch in range(half * 4, half * 4 + 4):
                    ve(lambda e, ch=ch: e.tensor_tensor_scan(tn[:, ch, :], rr[:, ch, :], ii[:, ch, :], 0.0, ALU.mult, ALU.add))
                t = tt(catT[:, h4, :], gy[:, h4, :], tn[:, h4, :], ALU.mult, *state["cat_free"])
            state["arena"] = t
            w2 = [load(w_cols(A["od_out_w"][0], n * 512, 512)) for n in range(2)]
            residual(w2, gbc[:, 0, :], t, t_g0)
            norm_T(modc[:, 1, 3, :], modc[:, 1, 2, :])
            stage("moe1")
        if stop not in ("even", "moe0", "odd"):
            moe(1, 1)

        def mixer2(l):
            u_ = region(0, 2, 512)
            g_ = region(1024, 2, 512)
            q = region(2048, 2, 512)
            k = region(3072, 2, 512)
            v = region(4096, 2, 512)
            qT = region(5120, 4, T)
            kT = region(6144, 4, T)
            Px = region(7168, 4, 512)
            PT = region(9216, 4, 512)
            o_ = region(11264, 2, 512)
            lng, lnb = acc[:, 0, 0:512], acc[:, 0, 512:1024]
            wsT = acc[:, 1, 0:512].rearrange("p (g t) -> p g t", g=4)
            wsr = acc[:, 1, 512:1024].rearrange("p (g t) -> p g t", g=4)
            s_l = sem(f"s_sgu{l}")
            wx = [*state["x"], state["arena"]]
            AC.add_dma(lambda e: e.dma_start(lng, A["sgu_ln_g_2"][l, :].partition_broadcast(128)), wx, s_l, 0)
            AC.add_dma(lambda e: e.dma_start(lnb, A["sgu_ln_b_2"][l, :].partition_broadcast(128)), wx, s_l, 0)
            AC.add_dma(lambda e: e.dma_start(wsr, A["sgu_w_2"][l].rearrange("g t s -> t g s")), wx, s_l, 0)
            t_l = (s_l, 48)
            tq = {}
            small_at = 64

            def proj(n, dst, func):
                s = load(w_cols(A["w_in_2"][l], n * 512, 512))
                for th in range(2):
                    b = bank(4, 5, 6, 7)
                    t = tok_major(lambda c: hT[:, c, th * 128:(th + 1) * 128], s.views[0], b, s.tok, *state["hT"], *take(b))
                    tq[n, th] = act(dst[:, th, :], b.t[:, :], func, t, state["arena"])
                    free(b, tq[n, th])
                s.free = [t]
                state["hT_free"] = [t]

            proj(0, q, ACT.Copy)
            proj(1, k, ACT.Copy)
            proj(2, v, ACT.Copy)
            b = bank(4, 5, 6, 7)
            w = take(b)
            for g in range(4):
                t = tr(b.t[:, g * 128:(g + 1) * 128], wsr[:, g, :], t_l, *w, sig=True)
            t_ws = act(wsT, b.t[:, :].rearrange("p (g t) -> p g t", g=4), ACT.Copy, t)
            free(b, t_ws)
            cs = [bc(C[n].rearrange("p (t f) -> p t f", t=2), 8, 2) for n in ("cos", "sin")]
            tT = {}
            for n, dst, dT in ((0, q, qT), (1, k, kT)):
                hv = dst.rearrange("p t (h d) -> p t h d", d=64)
                x1, x2 = hv[:, :, :, 0:8], hv[:, :, :, 8:16]
                R = [region(7168 + i * 128, 2, 8, 8) for i in range(4)]
                tt(R[0], x1, cs[0], ALU.mult, tq[n, 1])
                tt(R[1], x2, cs[1], ALU.mult)
                tt(R[2], x1, cs[1], ALU.mult)
                tt(R[3], x2, cs[0], ALU.mult)
                tt(x1, R[0], R[1], ALU.subtract)
                t = tt(x2, R[2], R[3], ALU.add)
                for pr in range(2):
                    b = bank(0, 1, 2, 3)
                    w = take(b)
                    for a2 in range(2):
                        for th in range(2):
                            c = pr * 2 + a2
                            tp = tr(b.t[:, a2 * T + th * 128:a2 * T + (th + 1) * 128],
                                    dst[:, th, c * 128:(c + 1) * 128], t, *w, sig=True)
                    tp = act(dT[:, pr * 2:pr * 2 + 2, :], b.t[:, :].rearrange("p (a n) -> p a n", a=2), ACT.Copy, tp)
                    free(b, tp)
            t_qk = tp
            nm, den = small[:, 64:80], small[:, 80:96]
            jobs = [(th, par, j) for th in range(2) for par in range(2) for j in range(2)]
            tz = {}

            def scores(n):
                th, par, j = jobs[n]
                r = slice(64 * par, 64 * par + 64)
                b = bank(0, 1, 2, 3)
                w = take(b)
                for m in range(2):
                    t = mm(b.t[:, m * T:(m + 1) * T], qT[r, 2 * j + m, th * 128:(th + 1) * 128], kT[r, 2 * j + m, :],
                           m == 0, m == 1, t_qk, *w, sig=m == 1)
                tz[n] = (b, t)

            tp_ = {}

            def soft(n):
                th, par, j = jobs[n]
                b, t = tz[n]
                P = Px[:, n % 4, :].rearrange("p (m k) -> p m k", m=2)
                neg = bc(C["neg"][:, th * T:(th + 1) * T], 2)
                cnt = bc(C["cnt"][:, th * T:(th + 1) * T], 2)
                t = stt(P, b.t[:, :].rearrange("p (m k) -> p m k", m=2), 0.125, neg, ALU.mult, ALU.add, t, tt4.get(n % 4))
                free(b, t)
                nn = nm[:, 2 * n:2 * n + 2]
                t = ve(lambda e: e.tensor_reduce(nn, P, X, ALU.max, negate=True))
                for m in range(2):
                    t = act(P[:, m, :], P[:, m, :], ACT.Exp, t, bias=nn[:, m:m + 1])
                tp_[n] = (t, P, cnt)

            def weigh(n):
                t, P, cnt = tp_[n]
                t = tt(P, P, cnt, ALU.mult, t)
                red(den[:, 2 * n:2 * n + 2], P, ALU.add)
                tp_[n] = t

            tt4 = {}
            tpt = {}
            ob = [banks[4], banks[5]]

            def turnP(n):
                b = bank(6, 7)
                w = take(b)
                P = Px[:, n % 4, :]
                for i in range(4):
                    t = tr(b.t[:, i * 128:(i + 1) * 128], P[:, i * 128:(i + 1) * 128], tp_[n], *w, sig=True)
                tt4[n % 4] = t
                t = act(PT[:, n % 4, :], b.t[:, :], ACT.Copy, t, tpv.get(n % 4))
                free(b, t)
                tpt[n] = t

            tpv = {}
            firsts = [True, True]

            def pv(n):
                th, par, j = jobs[n]
                b = ob[th]
                w = take(b) if firsts[th] else []
                for m in range(2):
                    h = 2 * (2 * j + m) + par
                    for kb in range(2):
                        i = m * 2 + kb
                        t = mm(b.t[:, h * 64:(h + 1) * 64], PT[:, n % 4, i * 128:(i + 1) * 128], v[:, kb, h * 64:(h + 1) * 64],
                               firsts[th], kb == 1, tpt[n], tq[2, 1], *w, sig=i == 3)
                        firsts[th] = False
                tpv[n % 4] = t
                tpv[th, "all"] = t

            for n in range(4):
                scores(n)
            for n in range(8):
                soft(n)
                if n >= 1:
                    weigh(n - 1)
                    turnP(n - 1)
                    if n - 1 + 4 < 8:
                        scores(n - 1 + 4)
                if n >= 2:
                    pv(n - 2)
            weigh(7)
            turnP(7)
            pv(6)
            pv(7)
            t_den = recip(den, den)
            for th in range(2):
                for par in range(2):
                    o4 = o_[:, th, :].rearrange("p (c two d) -> p c two d", two=2, d=64)[:, :, par, :]
                    b4 = ob[th].t[:, :].rearrange("p (c two d) -> p c two d", two=2, d=64)[:, :, par, :]
                    dd = den[:, 8 * th + 4 * par:8 * th + 4 * par + 4]
                    t = tt(o4, b4, bc(dd, 64, 2), ALU.mult, t_den, tpv[th, "all"])
                free(ob[th], t)
            t_o = t

            proj(3, u_, ACT.Gelu)
            proj(4, g_, ACT.Gelu)
            red(small[:, 96:98], g_, ALU.add, tq[4, 1])
            ts(small[:, 96:98], small[:, 96:98], -1.0 / 512, None, ALU.mult, None)
            for th in range(2):
                t = ts(g_[:, th, :], g_[:, th, :], small[:, 96 + th:97 + th], None, ALU.add, None)
            for th in range(2):
                t = act(Px[:, th, :], g_[:, th, :], ACT.Square, t, tt4[3], tt4[2], tt4[1], tt4[0],
                        accum_out=small[:, 100 + th:101 + th])
            t = rstd(100, 2, 512, t)
            for th in range(2):
                ts(g_[:, th, :], g_[:, th, :], small[:, 102 + th:103 + th], None, ALU.mult, None)
            tt(g_, g_, bc(lng, 2), ALU.mult, t_l)
            t_g = tt(g_, g_, bc(lnb, 2), ALU.add)
            for th in range(2):
                b = bank(4, 5, 6, 7)
                w = take(b)
                for g in range(4):
                    t = mm(b.t[:, g * 128:(g + 1) * 128], wsT[:, g, :], g_[:, th, g * 128:(g + 1) * 128], g == 0, g == 3,
                           t_g, t_ws, *w, sig=g == 3)
                for g in range(4):
                    s_ = slice(g * 128, (g + 1) * 128)
                    t2 = stt(u_[:, th, s_], b.t[:, s_], c2["sgub"][:, l * 4 + g:l * 4 + g + 1], u_[:, th, s_],
                             ALU.add, ALU.mult, t)
                free(b, t2)
            for th in range(2):
                act(Px[:, th, :], o_[:, th, :], ACT.Square, t_o, accum_out=small[:, 104 + th:105 + th])
                t = act(Px[:, 2 + th, :], u_[:, th, :], ACT.Square, t2, accum_out=small[:, 106 + th:107 + th])
            t = rstd(104, 4, 512, t)
            for th in range(2):
                ts(o_[:, th, :], o_[:, th, :], small[:, 108 + th:109 + th], None, ALU.mult, None)
                t = ts(u_[:, th, :], u_[:, th, :], small[:, 110 + th:111 + th], None, ALU.mult, None)
            for c in range(8):
                src, col = (o_, c2["attn"]) if c < 4 else (u_, c2["sgu"])
                b = bank(0, 1, 2, 3)
                w = take(b)
                cc = c % 4
                for th in range(2):
                    tp = tr(b.t[:, th * 128:(th + 1) * 128], src[:, th, cc * 128:(cc + 1) * 128], t, *w,
                            sig=th == 1)
                g = col[:, l * 4 + cc:l * 4 + cc + 1]
                if c % 2:
                    e1 = act(catT[:, c, :], b.t[:, 0:T], ACT.Copy, tp, *state["cat_free"], scale=g)
                    free(b, e1)
                else:
                    e2 = ts(catT[:, c, :], b.t[:, 0:T], g, None, ALU.mult, None, tp, *state["cat_free"])
                    free(b, e2)
            state["arena"] = tp
            w2 = [load(w_cols(A["w_out_2"][l], n * 512, 512)) for n in range(2)]
            residual(w2, None, e1, e2)

        order = ["even", "moe0", "odd", "moe1"]
        if stop is None or stop not in order:
            c_f1 = c2["ffn1"].rearrange("p (l k) -> p l k", l=2)
            c_f2 = c2["ffn2"].rearrange("p (l k) -> p l k", l=2)
            c_mx = c2["mix"].rearrange("p (l k) -> p l k", l=2)
            for l in range(2):
                stage(f"ffa{l}")
                norm_T(c_f1[:, l, :], None)
                ffn(l, "ffn1")
                if stop == f"ffa{l}":
                    break
                stage(f"mix{l}")
                norm_T(c_mx[:, l, :], None)
                mixer2(l)
                if stop == f"mix{l}":
                    break
                stage(f"ffb{l}")
                norm_T(c_f2[:, l, :], None)
                ffn(l, "ffn2")
                if stop == f"ffb{l}":
                    break
        stage("end")
        s_out, s_fin = sem("s_out"), sem("s_fin")
        dst = out.rearrange("a (t p) d -> p (a t) d", p=128)
        if stop is not None:
            SP.add_dma(lambda e: e.dma_start(dst, xres[:, :, :]), state["x"], s_out, 16)
            SP.items.append((None, [(s_out, 16)], None, 0))
        else:
            fin = region(0, D)
            td = AC.add_dma(lambda e: e.dma_start(fin, A["final_norm_2"].partition_broadcast(128)),
                            [state["arena"]], s_fin, 16)
            xn = region(12288, 2, D)
            for th in range(2):
                t = act(xn[:, th, :], xres[:, th, :], ACT.Square, *state["x"], state["arena"],
                        accum_out=small[:, th:th + 1])
            t = rstd(0, 2, D, t)
            for th in range(2):
                t = stt(xn[:, th, :], xres[:, th, :], small[:, 2 + th:3 + th], fin, ALU.mult, ALU.mult, td)
                SP.add_dma(lambda e, th=th: e.dma_start(dst[:, th, :], xn[:, th, :]), [t], s_out, 16)
            SP.items.append((None, [(s_out, 32)], None, 0))

        block = ctx.enter_context(nc.Block())

        @block.sync
        def _(eng):
            SP.emit(eng)

        @block.gpsimd
        def _(eng):
            PO.emit(eng)

        @block.scalar
        def _(eng):
            AC.emit(eng)

        @block.vector
        def _(eng):
            VE.emit(eng)

        @block.tensor
        def _(eng):
            PE.emit(eng)


def build(nc, stop=None):
    A = {}
    for n, shape in SHAPES.items():
        A[n] = nc.dram_tensor(f"in_{n}", shape, F32, kind="ExternalInput").ap()
    k = constants()
    width = sum(a.shape[1] for a in k.values())
    A["constants"] = nc.dram_tensor("in_constants", (128, width), F32, kind="ExternalInput").ap()
    out = nc.dram_tensor("out_0", (1, T, D), F32, kind="ExternalOutput").ap()
    program(nc, A, out, stop)


def kernel(**inputs):
    import concourse.bacc as bacc
    from concourse.bass_utils import run_bass_kernel_spmd

    nc = bacc.Bacc("TRN2", target_bir_lowering=False, num_devices=1)
    build(nc)
    arrays = {f"in_{n}": np.ascontiguousarray(inputs[n]) for n in SHAPES}
    arrays["in_constants"] = np.concatenate(list(constants().values()), axis=1)
    r = run_bass_kernel_spmd(nc, [arrays], core_ids=[0])
    return r.results[0]["out_0"]
```

```python
from contextlib import ExitStack

import numpy as np

import concourse.bass as bass
from concourse import mybir

F32 = mybir.dt.float32
F32R = mybir.dt.float32r
ALU = mybir.AluOpType
ACT = mybir.ActivationFunctionType
X = mybir.AxisListType.X

T = 256
D = 1024
KC = D // 128
NE = 16
DFF = 2816
EPS = 1e-6
NRAW = 3
NPAIR = 3
GRAN = 2048
NEG = -1e30

SHAPES = {
    "x": (1, T, D), "c": (1, D), "mod_w": (2, D, 6 * D), "mod_b": (2, 6 * D),
    "mix_norm_g": (2, D), "ffn_norm_g": (2, D), "ev_in_w": (1, D, 2560), "ev_dw_w": (1, 31, 512),
    "ev_dw_b": (1, 512), "ev_ln_g": (1, 512), "ev_ln_b": (1, 512), "ev_q_g": (1, 64), "ev_k_g": (1, 64),
    "ev_out_w": (1, D, D), "od_in_w": (1, D, 2 * D), "od_conv_w": (1, 4, D), "od_conv_b": (1, D),
    "od_rg_w": (1, 8, 128, 128), "od_rg_b": (1, D), "od_ig_w": (1, 8, 128, 128), "od_ig_b": (1, D),
    "od_lam": (1, D), "od_out_w": (1, D, D), "router_w": (D, NE), "router_b": (NE,),
    "ex_w1": (2, NE, D, 512), "ex_w3": (2, NE, D, 512), "ex_w2": (2, NE, 512, D),
    "norm_ffn1_2": (2, D), "ffn1_w_gate_2": (2, D, DFF), "ffn1_w_up_2": (2, D, DFF),
    "ffn1_w_down_2": (2, DFF, D), "norm_mix_2": (2, D), "w_in_2": (2, D, 2560),
    "sgu_ln_g_2": (2, 512), "sgu_ln_b_2": (2, 512), "sgu_w_2": (2, 4, 128, 128), "sgu_b_2": (2, 4, 128),
    "out_norm_attn_2": (2, 512), "out_norm_sgu_2": (2, 512), "w_out_2": (2, D, D),
    "norm_ffn2_2": (2, D), "ffn2_w_gate_2": (2, D, DFF), "ffn2_w_up_2": (2, D, DFF),
    "ffn2_w_down_2": (2, DFF, D), "final_norm_2": (D,),
}


def constants():
    p = np.arange(128)[:, None]
    f = np.arange(128)[None, :]
    out = {
        "ident": p == f,
        "ones": np.ones((128, 128)),
        "ntri": -(p >= f).astype(np.float32),
        "nones": -np.ones((128, 128)),
        "below": p < f,
        "negdiag": np.where(p < f, 0.0, NEG),
    }
    cnt, neg = [], []
    for th in range(2):
        q = th * 128 + p
        k = np.arange(T)[None, :]
        n = (np.abs(q - k) <= 64).astype(np.float32) + ((q - k) % 4 == 0) + ((q - k) % 16 == 0)
        cnt.append(n)
        neg.append(np.where(n > 0, 0.0, NEG))
    out["cnt"] = np.concatenate(cnt, 1)
    out["neg"] = np.concatenate(neg, 1)
    inv = np.float32(500000.0) ** (-np.arange(0, 16, 2, dtype=np.float32) / np.float32(16))
    ang = np.concatenate([(th * 128 + p).astype(np.float32) * inv[None, :] for th in range(2)], 1)
    out["cos"] = np.cos(ang.astype(np.float32))
    out["sin"] = np.sin(ang.astype(np.float32))
    i = np.arange(4)[:, None]
    j = np.arange(4)[None, :]
    out["first"] = np.broadcast_to((j < i).astype(np.float32).reshape(1, 16), (128, 16))
    out["eps"] = np.full((128, 1), EPS)
    return {n: np.ascontiguousarray(a, dtype=np.float32) for n, a in out.items()}


def weight_plan():
    plan = []

    def by_cols(name, idx, rows, c0, n, split=True):
        kg = min(GRAN // n, rows // 128)
        for r in range(0, rows // 128, kg):
            plan.append(((name, idx, r * 128, c0), split, kg, n))

    def by_rows(name, idx, r0, k):
        kg = min(2, k)
        for r in range(0, k, kg):
            plan.append(((name, idx, r0 + r * 128, 0), True, kg, D))

    def mod(l, v):
        for half in range(2):
            by_cols("mod_w", (l,), D, v * D + half * 512, 512, False)

    def square(name, idx, c0=0, n=2):
        for half in range(n):
            by_cols(name, idx, D, c0 + half * 512, 512)

    def feed(groups):
        for i, g in enumerate(groups):
            (w1, w3, c0, n), _ = g
            by_cols(*w1, D, c0, n)
            by_cols(*w3, D, c0, n)
            if i:
                by_rows(*groups[i - 1][1])
        by_rows(*groups[-1][1])

    def moe(l):
        feed([((("ex_w1", (l, e)), ("ex_w3", (l, e)), 0, 512), ("ex_w2", (l, e), 0, 4)) for e in range(NE)])

    def ffn(l, pre):
        feed([(((pre + "_w_gate_2", (l,)), (pre + "_w_up_2", (l,)), g * 512, 512 if g < 5 else 256),
               (pre + "_w_down_2", (l,), g * 512, 4 if g < 5 else 2)) for g in range(6)])

    mod(0, 0)
    mod(0, 1)
    square("ev_in_w", (0,), 0, 5)
    mod(0, 2)
    mod(0, 3)
    mod(0, 4)
    for v in (0, 1, 3, 4):
        mod(1, v)
    square("ev_out_w", (0,))
    mod(0, 5)
    moe(0)
    mod(1, 2)
    mod(1, 5)
    square("od_in_w", (0,), D, 2)
    square("od_in_w", (0,), 0, 2)
    plan.append((("gates",), True, 16, 128))
    square("od_out_w", (0,))
    moe(1)
    for l in range(2):
        ffn(l, "ffn1")
        square("w_in_2", (l,), 0, 5)
        square("w_out_2", (l,))
        ffn(l, "ffn2")
    return plan


class Queue:

    def __init__(self, name, chained):
        self.name, self.chained = name, chained
        self.items, self.sem, self.n, self.last = [], None, 0, None

    def stage(self, sem):
        self.sem, self.n = sem, 0

    def add(self, fn, waits, signal=True, chain=None):
        waits = list(waits)
        if (self.chained if chain is None else chain) and self.last is not None:
            waits.append(self.last)
        tok = None
        if signal:
            self.n += 1
            tok = (self.sem, self.n)
            self.last = tok
        self.items.append((fn, waits, self.sem if signal else None, 1))
        return tok

    def add_dma(self, fn, waits, sem, value):
        self.items.append((fn, list(waits), sem, 16))
        return (sem, value)

    def emit(self, eng):
        seen = {}
        for fn, waits, sem, inc in self.items:
            for w in waits:
                if w is None:
                    continue
                s, v = w
                if seen.get(id(s), 0) < v:
                    eng.wait_ge(s, v)
                    seen[id(s)] = v
            if fn is None:
                continue
            ins = fn(eng)
            if sem is not None:
                ins.then_inc(sem, inc)


class Bank:

    def __init__(self, t):
        self.t, self.free = t, []


class Granule:

    def __init__(self):
        self.free = None


def program(nc, A, out, stop=None):
    ctx = ExitStack()
    with ctx:
        base = [(nc.sbuf_base + 63) // 64 * 64]

        def sb(name, *shape, dt=F32, at=None):
            where = base[0] if at is None else at
            t = nc.alloc_sbuf_tensor_at(name, [128, *shape], dt, offset=where)
            if at is None:
                base[0] += (4 * int(np.prod(shape)) + 63) // 64 * 64
            return t

        def sem(name):
            return ctx.enter_context(nc.semaphore(name))

        PE, AC, VE, PO, SP = Queue("pe", False), Queue("act", True), Queue("dve", True), Queue("pool", True), Queue("sp", False)

        def stage(name):
            for q in (PE, AC, VE, PO):
                q.stage(sem(f"s_{q.name}_{name}"))

        def pe(fn, *w, sig=False):
            return PE.add(fn, w, signal=sig)

        def ac(fn, *w):
            return AC.add(fn, w)

        def ve(fn, *w, chain=None):
            return VE.add(fn, w, chain=chain)

        def po(fn, *w):
            return PO.add(fn, w)

        def mm(o, lhsT, rhs, start, stop, *w, sig=False):
            return pe(lambda e: e.matmul(o, lhsT, rhs, start=start, stop=stop, skip_group_check=True), *w, sig=sig)

        def mm3(o, L, R, start, stop, *w, sig=False):
            mm(o, L[0], R[0], start, False, *w)
            mm(o, L[0], R[1], False, False)
            return mm(o, L[1], R[0], False, stop, sig=sig)

        def tr(o, i, *w, sig=False):
            return pe(lambda e: e.transpose(o, i, ident), *w, sig=sig)

        def act(o, i, func, *w, **kw):
            return ac(lambda e: e.activation(o, i, func, **kw), *w)

        def tt(o, a, b, op, *w, chain=None):
            return ve(lambda e: e.tensor_tensor(o, a, b, op), *w, chain=chain)

        def ts(o, a, s1, s2, op0, op1, *w, chain=None):
            if s2 is None:
                return ve(lambda e: e.tensor_scalar(o, a, s1, None, op0), *w, chain=chain)
            return ve(lambda e: e.tensor_scalar(o, a, s1, s2, op0, op1), *w, chain=chain)

        def stt(o, a, s, b, op0, op1, *w, chain=None):
            return ve(lambda e: e.scalar_tensor_tensor(out=o, in0=a, scalar=s, in1=b, op0=op0, op1=op1), *w, chain=chain)

        def red(o, i, op, *w):
            return ve(lambda e: e.tensor_reduce(o, i, X, op), *w)

        def recip(o, i, *w):
            return ve(lambda e: e.reciprocal(o, i), *w)

        def vcopy(o, i, *w):
            return ve(lambda e: e.tensor_copy(o, i), *w)

        def bc(ap, n, axis=1):
            a = ap.unsqueeze(axis)
            shape = list(a.shape)
            shape[axis] = n
            return a.to_broadcast(shape)

        consts = {n: a.shape[1] for n, a in constants().items()}
        cst = sb("cst", sum(consts.values()))
        C, at = {}, 0
        for n, w in consts.items():
            C[n] = cst[:, at:at + w]
            at += w
        ident, ones = C["ident"], C["ones"]
        eps = C["eps"]
        xres = sb("xres", 2, D)
        hT = [sb(f"hT{i}", KC, T, dt=F32R) for i in "hl"]
        at = base[0]
        catT = [sb(f"catT{i}", KC, T, dt=F32R) for i in "hl"]
        uT = [sb(f"uT{i}", 2, 4, T, dt=F32R, at=at + 8192 * n) for n, i in enumerate("hl")]
        acc = sb("acc", 2, D)
        gbc = sb("gbc", 2, D)
        cbc = sb("cbc", KC, 128)
        rows = sb("rows", 4, 128)
        cols = sb("cols", 4, 128)
        crow = sb("crow", 128)
        condT = sb("condT", KC)
        modc = sb("modc", 2, 4, KC)
        rw = sb("rw", KC, NE)
        rb = sb("rb", NE)
        qkg = sb("qkg", 2, 64)
        small = sb("small", 512)
        lnc = sb("lnc", 8 * 6)
        arena = sb("arena", 14336)
        raws = [(sb(f"raw{i}", GRAN), sem(f"s_raw{i}")) for i in range(NRAW)]
        pairs = [[sb(f"pair{i}{n}", GRAN, dt=F32R) for n in "hl"] for i in range(NPAIR)]
        assert base[0] <= nc.sbuf_usable_end, base[0]
        banks = [Bank(ctx.enter_context(nc.psum_tensor(f"bank{i}", [128, 512], F32))) for i in range(8)]

        def region(at, *shape):
            n = int(np.prod(shape))
            a = arena[:, at:at + n]
            if len(shape) == 1:
                return a
            names = "abcd"[:len(shape)]
            return a.rearrange(f"p ({' '.join(names)}) -> p {' '.join(names)}", **dict(zip(names, shape)))

        s_cst, s_x, s_rows, s_bc = sem("s_cst"), sem("s_x"), sem("s_rows"), sem("s_bc")
        s_g = [sem("s_g0"), sem("s_g1")]
        t_cst = AC.add_dma(lambda e: e.dma_start(cst[:, :], A["constants"]), [], s_cst, 16)

        def row_tile(k, parts):
            at = 0
            for src in parts:
                n = src.shape[0]
                AC.add_dma(lambda e, at=at, n=n, src=src: e.dma_start(rows[at:at + n, k, :], src), [], s_rows, 0)
                row_tile.n += 16
                at += n
            return at
        row_tile.n = 0

        def flat(name):
            a = A[name]
            k = len(a.shape)
            if k == 1:
                return a.rearrange("(k p) -> k p", p=128)
            if k == 2:
                return a.rearrange("a (k p) -> (a k) p", p=128)
            return a.rearrange("a b (k p) -> (a b k) p", p=128)

        crow8 = crow[0:8, :]
        AC.add_dma(lambda e: e.dma_start(crow8, flat("c")), [], s_rows, 0)
        row_tile.n += 16
        row_tile(0, [flat(n) for n in ("mix_norm_g", "ffn_norm_g", "mod_b")])
        row_tile(1, [flat(n) for n in ("ev_dw_w", "ev_dw_b")])
        row_tile(2, [flat(n) for n in ("ev_ln_g", "ev_ln_b", "od_conv_w", "od_conv_b", "od_rg_b", "od_ig_b", "od_lam",
                                       "norm_ffn1_2", "norm_mix_2", "sgu_b_2", "out_norm_attn_2")])
        n3 = row_tile(3, [flat(n) for n in ("out_norm_sgu_2", "norm_ffn2_2")])
        t_rows = (s_rows, row_tile.n)
        t_x = AC.add_dma(lambda e: e.dma_start(xres[:, :, :], A["x"].rearrange("a (t p) d -> p (a t) d", p=128)),
                         [], s_x, 16)
        nbc = 0
        for dst, src in ((qkg[:, 0, :], A["ev_q_g"][0, :]), (qkg[:, 1, :], A["ev_k_g"][0, :]),
                         (rb[:, :], A["router_b"])):
            AC.add_dma(lambda e, dst=dst, src=src: e.dma_start(dst, src.partition_broadcast(128)), [], s_bc, 0)
            nbc += 16
        AC.add_dma(lambda e: e.dma_start(rw[:, :, :], A["router_w"].rearrange("(k p) n -> p k n", p=128)),
                   [], s_bc, 0)
        t_bc = (s_bc, nbc + 16)

        plan = weight_plan()
        grans = [Granule() for _ in plan]
        at_raw, at_pair, at_take = [0], [0], [0]
        pair_of, raw_free = [], []

        def source(key):
            name, idx, r0, c0 = key
            w = A[name]
            for i in idx:
                w = w[i]
            return w[r0:, c0:]

        def shape_of(t, k, n):
            return t[:, 0:k * n].rearrange("p (k n) -> p k n", k=k)

        def issue():
            i = at_raw[0]
            if i == len(plan):
                return False
            w = []
            if i >= NRAW:
                w = raw_free[i - NRAW] if i - NRAW < len(raw_free) else None
                if w is None:
                    return False
            key, split, k, n = plan[i]
            t, s = raws[i % NRAW]
            if key[0] == "gates":
                parts = [(shape_of(t, 16, 128)[:, 8 * h:8 * h + 8, :], A[nm][0].rearrange("b k j -> k b j"))
                         for h, nm in enumerate(("od_rg_w", "od_ig_w"))]
            else:
                name, idx, r0, c0 = key
                a = A[name]
                for ix in idx:
                    a = a[ix]
                parts = [(shape_of(t, k, n), a[r0:r0 + 128 * k, c0:c0 + n].rearrange("(k p) n -> p k n", p=128))]
            for dst, src in parts:
                SP.add_dma(lambda e, dst=dst, src=src: e.dma_start(dst, src), w, s, 0)
                raw_n[i % NRAW] += 16
            grans[i].raw = (s, raw_n[i % NRAW])
            raw_free.append(None)
            at_raw[0] += 1
            return True

        raw_n = [0] * NRAW
        splits = [i for i, g in enumerate(plan) if g[1]]
        ordinal = {i: n for n, i in enumerate(splits)}

        def convert():
            m = at_pair[0]
            if m == len(splits) or splits[m] >= at_raw[0]:
                return False
            i = splits[m]
            w = []
            if m >= NPAIR:
                w = grans[splits[m - NPAIR]].free
                if w is None:
                    return False
            _, _, k, n = plan[i]
            t = raws[i % NRAW][0][:, 0:k * n]
            hi, lo = (p[:, 0:k * n] for p in pairs[m % NPAIR])
            a = ac(lambda e: e.activation(hi, t, ACT.Copy), grans[i].raw, *w)
            v = tt(lo, t, hi.bitcast(F32), ALU.subtract, a)
            grans[i].tok = v
            grans[i].views = [shape_of(p, k, n) for p in pairs[m % NPAIR]]
            raw_free[i] = [v]
            at_pair[0] += 1
            return True

        def advance():
            while issue() or convert():
                pass

        def take_weight(*key):
            advance()
            i = at_take[0]
            assert plan[i][0] == key, (plan[i][0], key)
            at_take[0] += 1
            g = grans[i]
            g.split, g.k, g.n = plan[i][1:]
            if not g.split:
                g.tok, g.views = g.raw, [shape_of(raws[i % NRAW][0], g.k, g.n)]

            def release(tok):
                g.free = [tok]
                if not g.split:
                    raw_free[i] = [tok]
            g.release = release
            return g

        def weight(name, idx, rows, c0, n):
            kg = min(GRAN // n, rows // 128)
            for r in range(0, rows // 128, kg):
                yield r, take_weight(name, idx, r * 128, c0)

        turns = {}

        def bank(*among):
            key = among
            i = turns.get(key, 0)
            turns[key] = i + 1
            return banks[among[i % len(among)]]

        def take(b):
            w, b.free = b.free, []
            return w

        def free(b, *toks):
            b.free = b.free + [t for t in toks if t is not None]

        def pair(t, *idx):
            return [x[idx] for x in t]

        def tok_major(src, name, idx, c0, bs, *waits, rows=D):
            ws = [take(b) for b in bs]
            K = rows // 128
            for r, g in weight(name, idx, rows, c0, 512):
                for th, b in enumerate(bs):
                    for c in range(g.k):
                        t = mm3(b.t[:, :], [x[:, r + c, th * 128:(th + 1) * 128] for x in src],
                                [x[:, c, :] for x in g.views], r + c == 0, r + c == K - 1,
                                g.tok, *waits, *ws[th], sig=c == g.k - 1)
                    bs[th].done = t
                g.release(t)
            return [b.done for b in bs]

        def chan_major(src, name, idx, c0, n, bs, *waits):
            ws = [take(b) for b in bs]
            for r, g in weight(name, idx, D, c0, n):
                for f in range(n // 128):
                    o = bs[f // 2].t[:, (f % 2) * T:(f % 2 + 1) * T]
                    for c in range(g.k):
                        t = mm3(o, [x[:, c, f * 128:(f + 1) * 128] for x in g.views], [x[:, r + c, :] for x in src],
                                r + c == 0 and f % 2 == 0, r + c == KC - 1,
                                g.tok, *waits, *ws[f // 2], sig=c == g.k - 1)
                    bs[f // 2].done = t
                g.release(t)
            return [b.done for b in bs]

        def split(dst, src, *w):
            a = act(dst[0], src, ACT.Copy, *w)
            return tt(dst[1], src, dst[0].bitcast(F32), ALU.subtract, a)

        state = {"x": [t_x, t_x], "hT": None, "cat": []}

        def rstd(at, n, of, *w):
            a = act(small[:, at:at + n], small[:, at:at + n], ACT.Sqrt, *w, scale=1.0 / of, bias=eps)
            return recip(small[:, at + n:at + 2 * n], small[:, at:at + n], a)

        def norm_T(scale, shift, *waits):
            xn = region(12288, 2, D)
            tl = []
            for th in range(2):
                tl.append(act(xn[:, th, :], xres[:, th, :], ACT.Square, *state["x"], state["arena"],
                              accum_out=small[:, th:th + 1]))
            r = rstd(0, 2, D, tl[-1])
            ts_ = [ts(xn[:, 0, :], xres[:, 0, :], small[:, 2:3], None, ALU.mult, None, r),
                   act(xn[:, 1, :], xres[:, 1, :], ACT.Copy, r, scale=small[:, 3:4])]
            hf = region(10240, KC, T)
            for c in range(KC):
                b = bank(0, 1, 2, 3)
                w = take(b)
                for th in range(2):
                    t = tr(b.t[:, th * 128:(th + 1) * 128], xn[:, th, c * 128:(c + 1) * 128], *w, ts_[th], sig=th == 1)
                o = hf[:, c, :]
                if shift is None:
                    hi, lo = pair(hT, slice(None), c)
                    a = act(hi, b.t[:, 0:T], ACT.Copy, t, *waits, *state.get("hT_free", []), scale=scale[:, c:c + 1])
                    e = stt(lo, b.t[:, 0:T], scale[:, c:c + 1], hi.bitcast(F32), ALU.mult, ALU.subtract, a)
                elif c % 2:
                    e = act(o, b.t[:, 0:T], ACT.Identity, t, *waits, scale=scale[:, c:c + 1], bias=shift[:, c:c + 1])
                else:
                    e = ts(o, b.t[:, 0:T], scale[:, c:c + 1], shift[:, c:c + 1], ALU.mult, ALU.add, t, *waits)
                    e0 = e
                free(b, e)
                if shift is not None and c % 4 == 3:
                    h4 = slice(c - 3, c + 1)
                    e = split(pair(hT, slice(None), h4), hf[:, h4, :], e, e0, *state.get("hT_free", []))
            state["arena"] = t
            state["hT"] = [e]
            return [e]

        stage("pre")
        state["arena"] = None
        t_cols = []
        for k in range(4):
            n = (128, 128, 120, n3)[k]
            b = bank(0, 1, 2, 3)
            t = pe(lambda e, b=b, k=k, n=n: e.transpose(b.t[:, 0:n], rows[0:n, k, :], ident[0:n, 0:n]),
                   t_rows, t_cst, *take(b), sig=True)
            t_cols = vcopy(cols[:, k, 0:n], b.t[:, 0:n], t)
            free(b, t_cols)
        c_mix = cols[:, 0, 0:16].rearrange("p (l k) -> p l k", l=2)
        c_ffn = cols[:, 0, 16:32].rearrange("p (l k) -> p l k", l=2)
        c_modb = cols[:, 0, 32:128].rearrange("p (l v k) -> p l v k", l=2, v=6)
        c_dw = cols[:, 1, 0:124].rearrange("p (t k) -> p t k", k=4)
        c_dwb = cols[:, 1, 124:128]
        c2, at2 = {}, 0
        for n, w in (("ln_g", 4), ("ln_b", 4), ("cw", 32), ("cb", 8), ("rgb", 8), ("igb", 8), ("lam", 8),
                     ("ffn1", 16), ("mix", 16), ("sgub", 8), ("attn", 8)):
            c2[n] = cols[:, 2, at2:at2 + w]
            at2 += w
        c2["sgu"], c2["ffn2"] = cols[:, 3, 0:8], cols[:, 3, 8:24]

        t = act(crow8, crow8, ACT.Silu, t_rows)
        b = bank(0, 1, 2, 3)
        t = pe(lambda e, b=b: e.transpose(b.t[:, 0:8], crow8, ident[0:8, 0:8]), t, *take(b), sig=True)
        t_cond = vcopy(condT[:, :], b.t[:, 0:8], t)
        free(b, t_cond)
        t_cbc = vcopy(cbc[:, :, :], bc(condT[:, :], 128, 2), t_cond)

        def mod_cols(l, vs, b):
            w = take(b)
            for v in vs:
                slot_of = {0: 0, 1: 1, 3: 2, 4: 3}[v]
                for half in range(2):
                    for r, g in weight("mod_w", (l,), D, v * D + half * 512, 512):
                        for f in range(4):
                            j = half * 4 + f
                            for c in range(g.k):
                                t = mm(b.t[:, j:j + 1], g.views[0][:, c, f * 128:(f + 1) * 128],
                                       condT[:, r + c:r + c + 1], j == 0 and r + c == 0, r + c == KC - 1,
                                       g.tok, t_cond, *w, sig=c == g.k - 1)
                        g.release(t)
                o = modc[:, l, slot_of, :]
                t = tt(o, b.t[:, 0:8], c_modb[:, l, v, :], ALU.add, t, t_cols)
                w = [t]
                if v in (1, 4):
                    g = (c_mix if v == 1 else c_ffn)[:, l, :]
                    t = stt(o, o, 1.0, g, ALU.add, ALU.mult)
            free(b, t)
            return t

        def mod_row(l, v, k, b0, b1):
            w = state.get(("gbc", k), [])
            gn[k] += 16
            td = AC.add_dma(lambda e: e.dma_start(gbc[:, k, :], A["mod_b"][l, v * D:(v + 1) * D].partition_broadcast(128)),
                            w, s_g[k], gn[k])
            for half, b in enumerate((b0, b1)):
                w = take(b)
                for r, g in weight("mod_w", (l,), D, v * D + half * 512, 512):
                    for c in range(g.k):
                        t = mm(b.t[:, :], cbc[:, r + c, :], g.views[0][:, c, :], r + c == 0, r + c == KC - 1,
                               g.tok, t_cbc, *w, sig=c == g.k - 1)
                    g.release(t)
                o = gbc[:, k, half * 512:(half + 1) * 512]
                t = tt(o, b.t[:, :], o, ALU.add, t, td)
                free(b, t)
            return t

        gn = [0, 0]

        def residual(name, idx, gate, *waits):
            done = []
            for nh in range(2):
                bs = [bank(4, 5, 6, 7) for _ in range(2)]
                tb = tok_major(catT, name, idx, nh * 512, bs, *waits)
                for th in range(2):
                    b, t = bs[th], tb[th]
                    o = xres[:, th, nh * 512:(nh + 1) * 512]
                    if gate is None:
                        t2 = tt(o, b.t[:, :], o, ALU.add, t)
                        free(b, t2)
                    else:
                        tmp = acc[:, th, nh * 512:(nh + 1) * 512]
                        t2 = tt(tmp, b.t[:, :], gate[:, nh * 512:(nh + 1) * 512], ALU.mult, t)
                        free(b, t2)
                        t2 = tt(o, o, tmp, ALU.add)
                    done.append(t2)
            state["x"] = [done[-1]]
            state["cat_free"] = [t]
            return done[-1]

        class Feed:
            def __init__(self):
                self.pending, self.n, self.last_u = None, 0, {}

            def down(self):
                w2, us, buf, nf, first, last, evac = self.pending
                self.pending = None
                name, idx, r0 = w2
                ws = [take(banks[4 + i]) if first else [] for i in range(4)]
                for r in range(0, nf, 2):
                    g = take_weight(name, idx, r0 + r * 128, 0)
                    for i in range(4):
                        th, nh = i // 2, i % 2
                        for f in range(r, r + 2):
                            t = mm3(banks[4 + i].t[:, :], [x[:, buf, f, th * 128:(th + 1) * 128] for x in uT],
                                    [x[:, f - r, nh * 512:(nh + 1) * 512] for x in g.views],
                                    first and f == 0, last and f == nf - 1, g.tok, us[r // 2], *ws[i], sig=f == r + 1)
                        banks[4 + i].done = t
                    g.release(t)
                if evac is not None:
                    for i in range(4):
                        free(banks[4 + i], evac(i // 2, i % 2, banks[4 + i], banks[4 + i].done))
                self.last_u[buf] = [t]

            def group(self, w1, w3, w2, c0, nf, first, last, evac):
                buf = self.n % 2
                self.n += 1
                b1, b3 = banks[0:2], banks[2:4]
                b1, b3 = b1[:nf // 2], b3[:nf // 2]
                t1 = chan_major(hT, *w1, c0, nf * 128, b1, *state["hT"])
                t3 = chan_major(hT, *w3, c0, nf * 128, b3)
                state["hT_free"] = [t3[-1]]
                us = []
                for i in range(nf // 2):
                    uf = region(7168 + 512 * i, 512)
                    a = act(uf, b1[i].t[:, :], ACT.Silu, t1[i], state["arena"])
                    free(b1[i], a)
                    v = tt(uf, uf, b3[i].t[:, :], ALU.mult, a, t3[i])
                    free(b3[i], v)
                    dst = [x[:, buf, 2 * i:2 * i + 2, :].rearrange("p f t -> p (f t)") for x in uT]
                    us.append(split(dst, uf, v, *self.last_u.get(buf, []), *state.get("cat_free", [])))
                if self.pending is not None:
                    self.down()
                self.pending = (w2, us, buf, nf, first, last, evac)

            def finish(self):
                self.down()

        feed = Feed()

        def moe(l, k):
            gate_row = gbc[:, k, :]
            b = bank(0, 1, 2, 3)
            w = take(b)
            for th in range(2):
                for c in range(KC):
                    t = mm(b.t[:, th * NE:(th + 1) * NE], region(10240, KC, T)[:, c, th * 128:(th + 1) * 128], rw[:, c, :],
                           c == 0, c == KC - 1, *w, *state["hT"], t_bc, sig=c == KC - 1)
            S = lambda at, n: small[:, 64 + at:64 + at + n]
            score, biased = S(0, 32), S(32, 32)
            t = act(score, b.t[:, 0:32], ACT.Sigmoid, t, state.get("gates"))
            free(b, t)
            v2 = lambda a, n: a.rearrange("p (t n) -> p t n", t=2)
            v8 = lambda a: a.rearrange("p (g n) -> p g n", g=8)
            t = tt(v2(biased, 16), v2(score, 16), bc(rb[:, :], 2), ALU.add, t, t_bc)
            b8 = v8(biased)
            ps = v8(S(64, 48))
            tt(ps[:, :, 0:3], b8[:, :, 0:3], b8[:, :, 1:4], ALU.add)
            tt(ps[:, :, 3:5], b8[:, :, 0:2], b8[:, :, 2:4], ALU.add)
            tt(ps[:, :, 5:6], b8[:, :, 0:1], b8[:, :, 3:4], ALU.add)
            gs = S(112, 8)
            red(gs, ps, ALU.max)

            def below(o, vals, g, limit):
                v = vals.rearrange("p (g n) -> p g n", g=g)
                vi, vj = bc(v, 4, 3), bc(v, 4, 2)
                gt = S(128, 16 * g)
                ge = S(256, 16 * g)
                g4 = lambda a: a.rearrange("p (g i j) -> p g i j", i=4, j=4)
                g16 = lambda a: a.rearrange("p (g i) -> p g i", i=16)
                tt(g4(gt), vj, vi, ALU.is_gt)
                tt(g4(ge), vj, vi, ALU.is_ge)
                tt(ge, ge, gt, ALU.subtract)
                tt(g16(ge), g16(ge), bc(C["first"], g), ALU.mult)
                tt(gt, ge, gt, ALU.add)
                red(o, gt.rearrange("p (gi j) -> p gi j", j=4), ALU.add)
                return ts(o, o, float(limit), None, ALU.is_lt, None)

            gm, em = S(120, 8), S(384, 32)
            below(gm, gs, 2, 1)
            below(em, biased, 8, 2)
            tt(v8(em), v8(em), bc(gm, 4, 2), ALU.mult)
            tt(em, em, score, ALU.mult)
            den = S(416, 2)
            red(den, v2(em, 16), ALU.add)
            recip(den, den)
            t_gate = tt(v2(em, 16), v2(em, 16), bc(den, 16, 2), ALU.mult)

            for e in range(NE):
                def evac(th, nh, b, t, e=e):
                    o = acc[:, th, nh * 512:(nh + 1) * 512]
                    g = em[:, th * NE + e:th * NE + e + 1]
                    if e == 0:
                        return ts(o, b.t[:, :], g, None, ALU.mult, None, t, t_gate)
                    return stt(o, b.t[:, :], g, o, ALU.mult, ALU.add, t)
                feed.group(("ex_w1", (l, e)), ("ex_w3", (l, e)), ("ex_w2", (l, e), 0), 0, 4, True, True, evac)
            feed.finish()
            for th in range(2):
                tt(acc[:, th, :], acc[:, th, :], gate_row, ALU.mult)
                t = tt(xres[:, th, :], xres[:, th, :], acc[:, th, :], ALU.add)
            state["x"] = [t]
            state["gates"] = t
            state[("gbc", k)] = [t]

        def ffn(l, pre):
            def evac(th, nh, b, t):
                o = xres[:, th, nh * 512:(nh + 1) * 512]
                t = stt(o, b.t[:, :], 0.5, o, ALU.mult, ALU.add, t)
                state["x"] = [t]
                return t
            for g in range(6):
                nf = 4 if g < 5 else 2
                feed.group((pre + "_w_gate_2", (l,)), (pre + "_w_up_2", (l,)), (pre + "_w_down_2", (l,), g * 512),
                           g * 512, nf, g == 0, g == 5, evac if g == 5 else None)
            feed.finish()

        t = mod_cols(0, (0, 1), banks[0])
        norm_T(modc[:, 0, 1, :], modc[:, 0, 0, :], t)

        stage("even")
        upad = region(0, 4, 286)
        u = region(1152, 4, T)
        qs = region(2176, 2, 512)
        ks = region(3200, 2, 512)
        vs = region(4224, 2, 512)
        qT = region(5248, 4, T)
        kT = region(6272, 4, T)
        L = region(7296, 6, 512)
        sq = region(10368, 1024)
        W = region(2176, 2, 512)

        t_pad = po(lambda e: e.memset(upad[:, :, 0:30], 0.0), state["arena"])
        ab = [banks[4], banks[5]]
        ta = chan_major(hT, "ev_in_w", (0,), 0, 512, ab, *state["hT"])
        gb = [banks[6], banks[7]]
        tg = chan_major(hT, "ev_in_w", (0,), 512, 512, gb)
        for i in range(2):
            a = act(u[:, 2 * i:2 * i + 2, :], gb[i].t[:, :].rearrange("p (a n) -> p a n", a=2), ACT.Sigmoid, tg[i],
                    state["arena"])
            free(gb[i], a)
            t_u = tt(upad[:, 2 * i:2 * i + 2, 30:286], u[:, 2 * i:2 * i + 2, :],
                     ab[i].t[:, :].rearrange("p (a n) -> p a n", a=2), ALU.mult, a, ta[i])
            free(ab[i], t_u)
        tq = {}
        for n, (name, dst) in enumerate((("q", qs), ("k", ks), ("v", vs))):
            bs = [bank(0, 1, 2, 3) for _ in range(2)]
            tb = tok_major(hT, "ev_in_w", (0,), 1024 + n * 512, bs)
            for th in range(2):
                tq[name, th] = act(dst[:, th, :], bs[th].t[:, :], ACT.Copy, tb[th])
                free(bs[th], tq[name, th])
        state["hT_free"] = [tb[1]]
        ts(qkg[:, 0, :], qkg[:, 0, :], 0.125, None, ALU.mult, None, t_bc)
        for name, dst, g in (("q", qs, 0), ("k", ks, 1)):
            hv = dst[:, :, :].rearrange("p t (h d) -> p (t h) d", d=64)
            sv = sq.rearrange("p (h d) -> p h d", d=64)
            tt(sv, hv, hv, ALU.mult, tq[name, 1])
            t = red(small[:, 32:48], sv, ALU.add)
            t = act(small[:, 32:48], small[:, 32:48], ACT.Sqrt, t, scale=1.0 / 64, bias=eps)
            recip(small[:, 48:64], small[:, 32:48], t)
            tt(hv, hv, bc(small[:, 48:64], 64, 2), ALU.mult)
            t = tt(hv, hv, bc(qkg[:, g, :], 16), ALU.mult)
            dT = (qT, kT)[g]
            for pr in range(2):
                b = banks[4 + 2 * g + pr]
                w = take(b)
                for a2 in range(2):
                    for th in range(2):
                        c = pr * 2 + a2
                        tp = tr(b.t[:, a2 * T + th * 128:a2 * T + (th + 1) * 128], dst[:, th, c * 128:(c + 1) * 128],
                                t, *w, sig=True)
                tp = act(dT[:, pr * 2:pr * 2 + 2, :], b.t[:, :].rearrange("p (a n) -> p a n", a=2), ACT.Copy, tp)
                free(b, tp)
        t_qk = tp
        tz = {}
        for par in range(2):
            r = slice(64 * par, 64 * par + 64)
            for j in range(2):
                b = banks[3 * par + j]
                w = take(b)
                for m in range(2):
                    tz[par, j] = mm(b.t[:, m * T:(m + 1) * T], kT[r, 2 * j + m, 0:128], qT[r, 2 * j + m, :],
                                    m == 0, m == 1, t_qk, *w, sig=m == 1)
            b = banks[3 * par + 2]
            w = take(b)
            for m in range(4):
                tz[par, 2] = mm(b.t[:, m * 128:(m + 1) * 128], kT[r, m, 128:256], qT[r, m, 128:256],
                                m == 0, m == 3, t_qk, *w, sig=m == 3)
        def diag(ap, j):
            if j == 2:
                return ap.rearrange("p (m q) -> p m q", q=128)
            return ap.rearrange("p (m n q) -> p m n q", m=2, q=128)[:, :, 0, :]
        def off(ap):
            return ap.rearrange("p (m n q) -> p m n q", m=2, q=128)[:, :, 1, :]
        tl = {}
        ta6 = {}
        for i in range(6):
            par, j = i // 3, i % 3
            t = act(L[:, i, :], banks[i].t[:, :], ACT.Abs, tz[par, j])
            t = act(L[:, i, :], L[:, i, :], ACT.Exp, scale=-1.0)
            ta6[i] = act(L[:, i, :], L[:, i, :], ACT.Ln, bias=1.0)
        for i in range(6):
            par, j = i // 3, i % 3
            t = stt(L[:, i, :], banks[i].t[:, :], 0.0, L[:, i, :], ALU.max, ALU.add, ta6[i])
            d = diag(L[:, i, :], j)
            tl[i] = tt(d, d, bc(C["below"], d.shape[1]), ALU.mult)
        tR = {}
        for par in range(2):
            for j in (2, 0, 1):
                i = 3 * par + j
                tR[i] = mm(banks[i].t[:, :], C["ntri"], L[:, i, :], False, True, tl[i], tl[3 * par + 2], sig=True)
                if j < 2:
                    tR[i] = mm(off(banks[i].t[:, :]), C["nones"],
                               L[:, 3 * par + 2, j * 256:(j + 1) * 256].rearrange("p (m q) -> p m q", q=128),
                               False, True, tl[3 * par + 2], sig=True)
        tw = {}
        t_tri = tR[4] if tR[4][1] > tR[5][1] else tR[5]
        for i in (2, 0, 1, 5, 3, 4):
            j = i % 3
            d = diag(L[:, i, :], j)
            t = tt(d, diag(banks[i].t[:, :], j), bc(C["negdiag"], d.shape[1]), ALU.add, t_tri)
            if j < 2:
                act(off(L[:, i, :]), off(banks[i].t[:, :]), ACT.Exp, t)
            tw[i] = act(d, d, ACT.Exp, t)
            free(banks[i], tw[i])
        for ch in range(4):
            if ch % 2 == 0:
                b = banks[6 + ch // 2]
                w = take(b)
            c0 = (ch % 2) * T
            for par in range(2):
                h = 2 * ch + par
                r = slice(64 * par, 64 * par + 64)
                i0, i2 = 3 * par + ch // 2, 3 * par + 2
                mm(b.t[r, c0:c0 + T], vs[:, 0, h * 64:(h + 1) * 64], L[:, i0, (ch % 2) * T:(ch % 2 + 1) * T],
                   ch % 2 == 0, False, tw[i0], tq["v", 1], *w)
                t = mm(b.t[r, c0 + 128:c0 + T], vs[:, 1, h * 64:(h + 1) * 64], L[:, i2, ch * 128:(ch + 1) * 128],
                       False, True, tw[i2], sig=par == 1)
            if ch % 2:
                bv = b.t[:, :].rearrange("p (a n) -> p a n", a=2)
                hi, lo = pair(catT, slice(None), slice(3 + ch, 5 + ch))
                a = act(hi, bv, ACT.Copy, t)
                t_o = tt(lo, bv, hi.bitcast(F32), ALU.subtract, a)
                free(b, t_o)

        cur = {}
        for k in range(31):
            for c in range(4):
                if k == 0:
                    cur[c] = ts(u[:, c, :], upad[:, c, 0:T], c_dw[:, 0, c:c + 1], c_dwb[:, c:c + 1], ALU.mult, ALU.add,
                                t_u, t_pad, t_cols, chain=False)
                else:
                    cur[c] = stt(u[:, c, :], upad[:, c, k:k + T], c_dw[:, k, c:c + 1], u[:, c, :], ALU.mult, ALU.add,
                                 cur[c], chain=False)
        t_g0 = mod_row(0, 2, 0, banks[0], banks[1])
        t_m0 = mod_cols(0, (3, 4), banks[2])
        t_m1 = mod_cols(1, (0, 1, 3, 4), banks[3])
        b = banks[4]
        w = take(b)
        for c in range(4):
            t = mm(b.t[:, 0:T], ones, u[:, c, :], c == 0, c == 3, cur[3], *w, sig=c == 3)
        t = stt(u, bc(b.t[:, 0:T], 4), -1.0 / 512, u, ALU.mult, ALU.add, t)
        free(b, t)
        t = act(region(2176, 4, T), u, ACT.Square, t)
        b = banks[5]
        w = take(b)
        for c in range(4):
            t = mm(b.t[:, 0:T], ones, region(2176, 4, T)[:, c, :], c == 0, c == 3, t, *w, sig=c == 3)
        t = act(sq[:, 0:T], b.t[:, 0:T], ACT.Sqrt, t, scale=1.0 / 512, bias=eps)
        free(b, t)
        recip(sq[:, 0:T], sq[:, 0:T], t)
        t = tt(u, u, bc(sq[:, 0:T], 4), ALU.mult)
        for c in range(4):
            t_c = act(u[:, c, :], u[:, c, :], ACT.Silu, t, scale=c2["ln_g"][:, c:c + 1], bias=c2["ln_b"][:, c:c + 1])
        t_c = split(pair(catT, slice(None), slice(0, 4)), u, t_c)
        state["arena"] = t_c
        t = residual("ev_out_w", (0,), gbc[:, 0, :], t_c, t_o, t_g0)
        state["gbc", 0] = [t]
        t_g1 = mod_row(0, 5, 1, banks[0], banks[1])
        norm_T(modc[:, 0, 3, :], modc[:, 0, 2, :], t_m0)
        stage("moe0")
        if stop != "even":
            moe(0, 1)

            t_g0 = mod_row(1, 2, 0, banks[0], banks[1])
            t_g1 = mod_row(1, 5, 1, banks[2], banks[3])
            norm_T(modc[:, 1, 1, :], modc[:, 1, 0, :], t_m1)
            stage("odd")
        if stop not in ("even", "moe0"):
            xb = region(0, 8, 259)
            xc = region(2080, 8, T)
            rr = region(4128, 8, T)
            ii = region(6176, 8, T)
            tn = region(8224, 8, T)
            gy = region(10272, 8, T)
            N8 = lambda i: lnc[:, 8 * i:8 * i + 8]
            lam = c2["lam"]
            t = act(N8(0), lam, ACT.Abs, t_cols)
            t = act(N8(0), N8(0), ACT.Exp, scale=-1.0)
            ts(N8(1), N8(0), 2.0, None, ALU.add, None, t)
            recip(N8(1), N8(1))
            tt(N8(1), N8(1), N8(0), ALU.mult)
            tt(N8(2), N8(1), N8(1), ALU.mult)
            ts(N8(3), N8(2), 1.0 / 19, None, ALU.mult, None)
            for k in range(17, 1, -2):
                stt(N8(3), N8(3), 1.0 / k, N8(2), ALU.add, ALU.mult)
            ts(N8(3), N8(3), 1.0, -16.0, ALU.add, ALU.mult)
            tt(N8(3), N8(3), N8(1), ALU.mult)
            ts(N8(4), lam, 0.0, 8.0, ALU.min, ALU.mult)
            t_c8 = tt(N8(3), N8(3), N8(4), ALU.add)
            c8 = N8(3)
            t_pad = po(lambda e: e.memset(xb[:, :, 0:3], 0.0), state["arena"])
            tx = []
            for half in range(2):
                bs = [bank(4, 5, 6, 7) for _ in range(2)]
                tb = chan_major(hT, "od_in_w", (0,), D + half * 512, 512, bs, *state["hT"])
                for i, b in enumerate(bs):
                    ch = half * 4 + 2 * i
                    a = act(xb[:, ch:ch + 2, 3:259], b.t[:, :].rearrange("p (a n) -> p a n", a=2), ACT.Copy, tb[i],
                            state["arena"])
                    free(b, a)
                    tx += [a, a]
            cur = {}
            for half in range(2):
                for k in range(4):
                    for ch in range(half * 4, half * 4 + 4):
                        sc = c2["cw"][:, k * 8 + ch:k * 8 + ch + 1]
                        if k == 0:
                            cur[ch] = ts(xc[:, ch, :], xb[:, ch, 0:T], sc, c2["cb"][:, ch:ch + 1], ALU.mult, ALU.add,
                                         tx[ch], t_pad, chain=False)
                        else:
                            cur[ch] = stt(xc[:, ch, :], xb[:, ch, k:k + T], sc, xc[:, ch, :], ALU.mult, ALU.add,
                                          cur[ch], chain=False)
            for half in range(2):
                bs = [bank(4, 5, 6, 7) for _ in range(2)]
                tb = chan_major(hT, "od_in_w", (0,), half * 512, 512, bs)
                for i, b in enumerate(bs):
                    ch = half * 4 + 2 * i
                    a = act(gy[:, ch:ch + 2, :], b.t[:, :].rearrange("p (a n) -> p a n", a=2), ACT.Gelu_apprx_tanh, tb[i])
                    free(b, a)
            state["hT_free"] = [tb[1]]
            txc = [split(pair(catT, slice(None), slice(4 * i, 4 * i + 4)), xc[:, 4 * i:4 * i + 4, :], cur[4 * i + 3],
                         *state["cat_free"]) for i in range(2)]
            g = take_weight("gates")
            for ch in range(8):
                for n, (dst, bias) in enumerate(((rr, "rgb"), (ii, "igb"))):
                    b = bank(0, 1, 2, 3)
                    t = mm3(b.t[:, 0:T], [x[:, 8 * n + ch, :] for x in g.views], [x[:, ch, :] for x in catT], True, True,
                            g.tok, txc[ch // 4], *take(b), sig=True)
                    a = act(dst[:, ch, :], b.t[:, 0:T], ACT.Sigmoid, t, bias=c2[bias][:, ch:ch + 1])
                    free(b, a)
            g.release(t)
            t_xc = t
            for half in range(2):
                h4 = slice(half * 4, half * 4 + 4)
                t = tt(rr[:, h4, :], rr[:, h4, :], bc(c8[:, h4], T, 2), ALU.mult, a, t_c8)
                act(tn[:, h4, :], rr[:, h4, :], ACT.Tanh, t, scale=-1.0)
                t_a = act(rr[:, h4, :], rr[:, h4, :], ACT.Exp)
                xb8 = xb[:, :, 0:T]
                ts(xb8[:, h4, :], tn[:, h4, :], 1.0, None, ALU.add, None, t_a)
                recip(xb8[:, h4, :], xb8[:, h4, :])
                t = tt(tn[:, h4, :], tn[:, h4, :], xb8[:, h4, :], ALU.mult)
                t_s = act(tn[:, h4, :], tn[:, h4, :], ACT.Sqrt, t, scale=2.0)
                tt(ii[:, h4, :], ii[:, h4, :], xc[:, h4, :], ALU.mult)
                tt(ii[:, h4, :], ii[:, h4, :], tn[:, h4, :], ALU.mult, t_s)
                for ch in range(half * 4, half * 4 + 4):
                    ve(lambda e, ch=ch: e.tensor_tensor_scan(tn[:, ch, :], rr[:, ch, :], ii[:, ch, :], 0.0, ALU.mult, ALU.add))
                t = tt(gy[:, h4, :], gy[:, h4, :], tn[:, h4, :], ALU.mult)
                t = split(pair(catT, slice(None), h4), gy[:, h4, :], t, t_xc)
            state["arena"] = t
            residual("od_out_w", (0,), gbc[:, 0, :], t, t_g0)
            norm_T(modc[:, 1, 3, :], modc[:, 1, 2, :])
            stage("moe1")
        if stop not in ("even", "moe0", "odd"):
            moe(1, 1)

        def mixer2(l):
            u_ = region(0, 2, 512)
            g_ = region(1024, 2, 512)
            q = region(2048, 2, 512)
            k = region(3072, 2, 512)
            v = region(4096, 2, 512)
            qT = region(5120, 4, T)
            kT = region(6144, 4, T)
            Px = region(7168, 4, 512)
            PT = region(9216, 4, 512)
            o_ = region(11264, 2, 512)
            lng, lnb = acc[:, 0, 0:512], acc[:, 0, 512:1024]
            wsT = acc[:, 1, 0:512].rearrange("p (g t) -> p g t", g=4)
            wsr = acc[:, 1, 512:1024].rearrange("p (g t) -> p g t", g=4)
            s_l = sem(f"s_sgu{l}")
            wx = [*state["x"], state["arena"]]
            AC.add_dma(lambda e: e.dma_start(lng, A["sgu_ln_g_2"][l, :].partition_broadcast(128)), wx, s_l, 0)
            AC.add_dma(lambda e: e.dma_start(lnb, A["sgu_ln_b_2"][l, :].partition_broadcast(128)), wx, s_l, 0)
            AC.add_dma(lambda e: e.dma_start(wsr, A["sgu_w_2"][l].rearrange("g t s -> t g s")), wx, s_l, 0)
            t_l = (s_l, 48)
            tq = {}
            small_at = 64

            def proj(n, dst, func):
                bs = [bank(4, 5, 6, 7) for _ in range(2)]
                tb = tok_major(hT, "w_in_2", (l,), n * 512, bs, *state["hT"])
                for th in range(2):
                    tq[n, th] = act(dst[:, th, :], bs[th].t[:, :], func, tb[th], state["arena"])
                    free(bs[th], tq[n, th])
                state["hT_free"] = [tb[1]]

            proj(0, q, ACT.Copy)
            proj(1, k, ACT.Copy)
            proj(2, v, ACT.Copy)
            b = bank(4, 5, 6, 7)
            w = take(b)
            for g in range(4):
                t = tr(b.t[:, g * 128:(g + 1) * 128], wsr[:, g, :], t_l, *w, sig=True)
            t_ws = act(wsT, b.t[:, :].rearrange("p (g t) -> p g t", g=4), ACT.Copy, t)
            free(b, t_ws)
            cs = [bc(C[n].rearrange("p (t f) -> p t f", t=2), 8, 2) for n in ("cos", "sin")]
            tT = {}
            for n, dst, dT in ((0, q, qT), (1, k, kT)):
                hv = dst.rearrange("p t (h d) -> p t h d", d=64)
                x1, x2 = hv[:, :, :, 0:8], hv[:, :, :, 8:16]
                R = [region(7168 + i * 128, 2, 8, 8) for i in range(4)]
                tt(R[0], x1, cs[0], ALU.mult, tq[n, 1])
                tt(R[1], x2, cs[1], ALU.mult)
                tt(R[2], x1, cs[1], ALU.mult)
                tt(R[3], x2, cs[0], ALU.mult)
                tt(x1, R[0], R[1], ALU.subtract)
                t = tt(x2, R[2], R[3], ALU.add)
                for pr in range(2):
                    b = bank(0, 1, 2, 3)
                    w = take(b)
                    for a2 in range(2):
                        for th in range(2):
                            c = pr * 2 + a2
                            tp = tr(b.t[:, a2 * T + th * 128:a2 * T + (th + 1) * 128],
                                    dst[:, th, c * 128:(c + 1) * 128], t, *w, sig=True)
                    tp = act(dT[:, pr * 2:pr * 2 + 2, :], b.t[:, :].rearrange("p (a n) -> p a n", a=2), ACT.Copy, tp)
                    free(b, tp)
            t_qk = tp
            nm, den = small[:, 64:80], small[:, 80:96]
            jobs = [(th, par, j) for th in range(2) for par in range(2) for j in range(2)]
            tz = {}

            def scores(n):
                th, par, j = jobs[n]
                r = slice(64 * par, 64 * par + 64)
                b = bank(0, 1, 2, 3)
                w = take(b)
                for m in range(2):
                    t = mm(b.t[:, m * T:(m + 1) * T], qT[r, 2 * j + m, th * 128:(th + 1) * 128], kT[r, 2 * j + m, :],
                           m == 0, m == 1, t_qk, *w, sig=m == 1)
                tz[n] = (b, t)

            tp_ = {}

            def soft(n):
                th, par, j = jobs[n]
                b, t = tz[n]
                P = Px[:, n % 4, :].rearrange("p (m k) -> p m k", m=2)
                neg = bc(C["neg"][:, th * T:(th + 1) * T], 2)
                cnt = bc(C["cnt"][:, th * T:(th + 1) * T], 2)
                t = stt(P, b.t[:, :].rearrange("p (m k) -> p m k", m=2), 0.125, neg, ALU.mult, ALU.add, t, tt4.get(n % 4))
                free(b, t)
                nn = nm[:, 2 * n:2 * n + 2]
                t = ve(lambda e: e.tensor_reduce(nn, P, X, ALU.max, negate=True))
                for m in range(2):
                    t = act(P[:, m, :], P[:, m, :], ACT.Exp, t, bias=nn[:, m:m + 1])
                tp_[n] = (t, P, cnt)

            def weigh(n):
                t, P, cnt = tp_[n]
                t = tt(P, P, cnt, ALU.mult, t)
                red(den[:, 2 * n:2 * n + 2], P, ALU.add)
                tp_[n] = t

            tt4 = {}
            tpt = {}
            ob = [banks[4], banks[5]]

            def turnP(n):
                b = bank(6, 7)
                w = take(b)
                P = Px[:, n % 4, :]
                for i in range(4):
                    t = tr(b.t[:, i * 128:(i + 1) * 128], P[:, i * 128:(i + 1) * 128], tp_[n], *w, sig=True)
                tt4[n % 4] = t
                t = act(PT[:, n % 4, :], b.t[:, :], ACT.Copy, t, tpv.get(n % 4))
                free(b, t)
                tpt[n] = t

            tpv = {}
            firsts = [True, True]

            def pv(n):
                th, par, j = jobs[n]
                b = ob[th]
                w = take(b) if firsts[th] else []
                for m in range(2):
                    h = 2 * (2 * j + m) + par
                    for kb in range(2):
                        i = m * 2 + kb
                        t = mm(b.t[:, h * 64:(h + 1) * 64], PT[:, n % 4, i * 128:(i + 1) * 128], v[:, kb, h * 64:(h + 1) * 64],
                               firsts[th], kb == 1, tpt[n], tq[2, 1], *w, sig=i == 3)
                        firsts[th] = False
                tpv[n % 4] = t
                tpv[th, "all"] = t

            for n in range(4):
                scores(n)
            for n in range(8):
                soft(n)
                if n >= 1:
                    weigh(n - 1)
                    turnP(n - 1)
                    if n - 1 + 4 < 8:
                        scores(n - 1 + 4)
                if n >= 2:
                    pv(n - 2)
            weigh(7)
            turnP(7)
            pv(6)
            pv(7)
            t_den = recip(den, den)
            for th in range(2):
                for par in range(2):
                    o4 = o_[:, th, :].rearrange("p (c two d) -> p c two d", two=2, d=64)[:, :, par, :]
                    b4 = ob[th].t[:, :].rearrange("p (c two d) -> p c two d", two=2, d=64)[:, :, par, :]
                    dd = den[:, 8 * th + 4 * par:8 * th + 4 * par + 4]
                    t = tt(o4, b4, bc(dd, 64, 2), ALU.mult, t_den, tpv[th, "all"])
                free(ob[th], t)
            t_o = t

            proj(3, u_, ACT.Gelu)
            proj(4, g_, ACT.Gelu)
            red(small[:, 96:98], g_, ALU.add, tq[4, 1])
            ts(small[:, 96:98], small[:, 96:98], -1.0 / 512, None, ALU.mult, None)
            for th in range(2):
                t = ts(g_[:, th, :], g_[:, th, :], small[:, 96 + th:97 + th], None, ALU.add, None)
            for th in range(2):
                t = act(Px[:, th, :], g_[:, th, :], ACT.Square, t, tt4[3], tt4[2], tt4[1], tt4[0],
                        accum_out=small[:, 100 + th:101 + th])
            t = rstd(100, 2, 512, t)
            for th in range(2):
                ts(g_[:, th, :], g_[:, th, :], small[:, 102 + th:103 + th], None, ALU.mult, None)
            tt(g_, g_, bc(lng, 2), ALU.mult, t_l)
            t_g = tt(g_, g_, bc(lnb, 2), ALU.add)
            for th in range(2):
                b = bank(4, 5, 6, 7)
                w = take(b)
                for g in range(4):
                    t = mm(b.t[:, g * 128:(g + 1) * 128], wsT[:, g, :], g_[:, th, g * 128:(g + 1) * 128], g == 0, g == 3,
                           t_g, t_ws, *w, sig=g == 3)
                for g in range(4):
                    s_ = slice(g * 128, (g + 1) * 128)
                    t2 = stt(u_[:, th, s_], b.t[:, s_], c2["sgub"][:, l * 4 + g:l * 4 + g + 1], u_[:, th, s_],
                             ALU.add, ALU.mult, t)
                free(b, t2)
            for th in range(2):
                act(Px[:, th, :], o_[:, th, :], ACT.Square, t_o, accum_out=small[:, 104 + th:105 + th])
                t = act(Px[:, 2 + th, :], u_[:, th, :], ACT.Square, t2, accum_out=small[:, 106 + th:107 + th])
            t = rstd(104, 4, 512, t)
            for th in range(2):
                ts(o_[:, th, :], o_[:, th, :], small[:, 108 + th:109 + th], None, ALU.mult, None)
                t = ts(u_[:, th, :], u_[:, th, :], small[:, 110 + th:111 + th], None, ALU.mult, None)
            for c in range(8):
                src, col = (o_, c2["attn"]) if c < 4 else (u_, c2["sgu"])
                b = bank(0, 1, 2, 3)
                w = take(b)
                cc = c % 4
                for th in range(2):
                    tp = tr(b.t[:, th * 128:(th + 1) * 128], src[:, th, cc * 128:(cc + 1) * 128], t, *w,
                            sig=th == 1)
                g = col[:, l * 4 + cc:l * 4 + cc + 1]
                hi, lo = pair(catT, slice(None), c)
                a = act(hi, b.t[:, 0:T], ACT.Copy, tp, *state["cat_free"], scale=g)
                e = stt(lo, b.t[:, 0:T], g, hi.bitcast(F32), ALU.mult, ALU.subtract, a)
                free(b, e)
            state["arena"] = tp
            residual("w_out_2", (l,), None, e)

        order = ["even", "moe0", "odd", "moe1"]
        if stop is None or stop not in order:
            c_f1 = c2["ffn1"].rearrange("p (l k) -> p l k", l=2)
            c_f2 = c2["ffn2"].rearrange("p (l k) -> p l k", l=2)
            c_mx = c2["mix"].rearrange("p (l k) -> p l k", l=2)
            for l in range(2):
                stage(f"ffa{l}")
                norm_T(c_f1[:, l, :], None)
                ffn(l, "ffn1")
                if stop == f"ffa{l}":
                    break
                stage(f"mix{l}")
                norm_T(c_mx[:, l, :], None)
                mixer2(l)
                if stop == f"mix{l}":
                    break
                stage(f"ffb{l}")
                norm_T(c_f2[:, l, :], None)
                ffn(l, "ffn2")
                if stop == f"ffb{l}":
                    break
        stage("end")
        s_out, s_fin = sem("s_out"), sem("s_fin")
        dst = out.rearrange("a (t p) d -> p (a t) d", p=128)
        if stop is not None:
            SP.add_dma(lambda e: e.dma_start(dst, xres[:, :, :]), state["x"], s_out, 16)
            SP.items.append((None, [(s_out, 16)], None, 0))
        else:
            fin = region(0, D)
            td = AC.add_dma(lambda e: e.dma_start(fin, A["final_norm_2"].partition_broadcast(128)),
                            [state["arena"]], s_fin, 16)
            xn = region(12288, 2, D)
            for th in range(2):
                t = act(xn[:, th, :], xres[:, th, :], ACT.Square, *state["x"], state["arena"],
                        accum_out=small[:, th:th + 1])
            t = rstd(0, 2, D, t)
            for th in range(2):
                t = stt(xn[:, th, :], xres[:, th, :], small[:, 2 + th:3 + th], fin, ALU.mult, ALU.mult, td)
                SP.add_dma(lambda e, th=th: e.dma_start(dst[:, th, :], xn[:, th, :]), [t], s_out, 16)
            SP.items.append((None, [(s_out, 32)], None, 0))

        block = ctx.enter_context(nc.Block())

        @block.sync
        def _(eng):
            SP.emit(eng)

        @block.gpsimd
        def _(eng):
            PO.emit(eng)

        @block.scalar
        def _(eng):
            AC.emit(eng)

        @block.vector
        def _(eng):
            VE.emit(eng)

        @block.tensor
        def _(eng):
            PE.emit(eng)


def build(nc, stop=None):
    A = {}
    for n, shape in SHAPES.items():
        A[n] = nc.dram_tensor(f"in_{n}", shape, F32, kind="ExternalInput").ap()
    k = constants()
    width = sum(a.shape[1] for a in k.values())
    A["constants"] = nc.dram_tensor("in_constants", (128, width), F32, kind="ExternalInput").ap()
    out = nc.dram_tensor("out_0", (1, T, D), F32, kind="ExternalOutput").ap()
    program(nc, A, out, stop)


def kernel(**inputs):
    import concourse.bacc as bacc
    from concourse.bass_utils import run_bass_kernel_spmd

    nc = bacc.Bacc("TRN2", target_bir_lowering=False, num_devices=1)
    build(nc)
    arrays = {f"in_{n}": np.ascontiguousarray(inputs[n]) for n in SHAPES}
    arrays["in_constants"] = np.concatenate(list(constants().values()), axis=1)
    r = run_bass_kernel_spmd(nc, [arrays], core_ids=[0])
    return r.results[0]["out_0"]
```

```python
from contextlib import ExitStack

import numpy as np

import concourse.bass as bass
from concourse import mybir

F32 = mybir.dt.float32
F32R = mybir.dt.float32r
ALU = mybir.AluOpType
ACT = mybir.ActivationFunctionType
X = mybir.AxisListType.X

T = 256
D = 1024
KC = D // 128
NE = 16
DFF = 2816
EPS = 1e-6
CAP = 128
GRAN = 2048
NRAW = 3
NPAIR = 3
SHARE = 0.25
SIDE = (1, 1, 0, 1, 1, 2, 1, 1)
NEG = -1e30

SHAPES = {
    "x": (1, T, D), "c": (1, D), "mod_w": (2, D, 6 * D), "mod_b": (2, 6 * D),
    "mix_norm_g": (2, D), "ffn_norm_g": (2, D), "ev_in_w": (1, D, 2560), "ev_dw_w": (1, 31, 512),
    "ev_dw_b": (1, 512), "ev_ln_g": (1, 512), "ev_ln_b": (1, 512), "ev_q_g": (1, 64), "ev_k_g": (1, 64),
    "ev_out_w": (1, D, D), "od_in_w": (1, D, 2 * D), "od_conv_w": (1, 4, D), "od_conv_b": (1, D),
    "od_rg_w": (1, 8, 128, 128), "od_rg_b": (1, D), "od_ig_w": (1, 8, 128, 128), "od_ig_b": (1, D),
    "od_lam": (1, D), "od_out_w": (1, D, D), "router_w": (D, NE), "router_b": (NE,),
    "ex_w1": (2, NE, D, 512), "ex_w3": (2, NE, D, 512), "ex_w2": (2, NE, 512, D),
    "norm_ffn1_2": (2, D), "ffn1_w_gate_2": (2, D, DFF), "ffn1_w_up_2": (2, D, DFF),
    "ffn1_w_down_2": (2, DFF, D), "norm_mix_2": (2, D), "w_in_2": (2, D, 2560),
    "sgu_ln_g_2": (2, 512), "sgu_ln_b_2": (2, 512), "sgu_w_2": (2, 4, 128, 128), "sgu_b_2": (2, 4, 128),
    "out_norm_attn_2": (2, 512), "out_norm_sgu_2": (2, 512), "w_out_2": (2, D, D),
    "norm_ffn2_2": (2, D), "ffn2_w_gate_2": (2, D, DFF), "ffn2_w_up_2": (2, D, DFF),
    "ffn2_w_down_2": (2, DFF, D), "final_norm_2": (D,),
}


def constants():
    p = np.arange(128)[:, None]
    f = np.arange(128)[None, :]
    out = {
        "ident": p == f,
        "ones": np.ones((128, 128)),
        "minushalf": np.full((128, 16), -0.5),
        "eps": np.full((128, 1), EPS),
        "ntri": -(p >= f).astype(np.float32),
        "nones": -np.ones((128, 128)),
        "below": p < f,
        "iota": np.broadcast_to(f, (128, 128)),
        "negdiag": np.where(p < f, 0.0, NEG),
    }
    cnt, neg = [], []
    for th in range(2):
        q = th * 128 + p
        k = np.arange(T)[None, :]
        n = (np.abs(q - k) <= 64).astype(np.float32) + ((q - k) % 4 == 0) + ((q - k) % 16 == 0)
        cnt.append(n)
        neg.append(np.where(n > 0, 0.0, NEG))
    out["cnt"] = np.concatenate(cnt, 1)
    out["neg"] = np.concatenate(neg, 1)
    inv = np.float32(500000.0) ** (-np.arange(0, 16, 2, dtype=np.float32) / np.float32(16))
    ang = np.concatenate([(th * 128 + p).astype(np.float32) * inv[None, :] for th in range(2)], 1)
    out["cos"] = np.cos(ang.astype(np.float32))
    out["sin"] = np.sin(ang.astype(np.float32))
    i = np.arange(4)[:, None]
    j = np.arange(4)[None, :]
    out["first"] = np.broadcast_to((j < i).astype(np.float32).reshape(1, 16), (128, 16))
    return {n: np.ascontiguousarray(a, dtype=np.float32) for n, a in out.items()}


EVEN_AT = ((5, 0), (4, 0), (0, 0), (6, 0), (0, 0), (0, 1), (0, 0), (0, 2), (1, 0),
           (7, 2), (4, 0), (0, 1), (1, 0), (2, 0), (0, 2), (31, 1), (0, 2))
EVEN_MODS = ((0, 2), (0, 3), (0, 4), (0, 5), (1, 0), (1, 1))
SUMMED = ((0, 0), (0, 1))
ODD_AT = (1, 1, 0, 1, 1)
ODD_MODS = ((1, 2), (1, 3), (1, 4), (1, 5))


def weight_plan():
    plan = []

    def by_cols(name, idx, rows, c0, n, split=True):
        kg = min(GRAN // n, rows // 128)
        for r in range(0, rows // 128, kg):
            plan.append(((name, idx, r * 128, c0), split, kg, n))

    def by_rows(name, idx, r0, k):
        kg = min(2, k)
        for r in range(0, k, kg):
            plan.append(((name, idx, r0 + r * 128, 0), True, kg, D))

    def mod(l, v):
        for half in range(2):
            by_cols("mod_w", (l,), D, v * D + half * 512, 512, False)

    def square(name, idx, c0=0, n=2):
        for half in range(n):
            by_cols(name, idx, D, c0 + half * 512, 512)

    def feed(groups):
        for i, g in enumerate(groups):
            (w1, w3, c0, n), _ = g
            by_cols(*w1, D, c0, n)
            by_cols(*w3, D, c0, n)
            if i:
                by_rows(*groups[i - 1][1])
        by_rows(*groups[-1][1])

    def moe(l):
        for e in range(NE):
            by_cols("ex_w1", (l, e), D, 0, 512)
            if 0 < e < NE - 1:
                by_rows("ex_w2", (l, e - 1), 0, 4)
            by_cols("ex_w3", (l, e), D, 0, 512)
        by_rows("ex_w2", (l, NE - 2), 0, 4)
        by_rows("ex_w2", (l, NE - 1), 0, 4)

    def ffn(l, pre):
        feed([(((pre + "_w_gate_2", (l,)), (pre + "_w_up_2", (l,)), g * 512, 512 if g < 5 else 256),
               (pre + "_w_down_2", (l,), g * 512, 4 if g < 5 else 2)) for g in range(6)])

    mod(0, 0)
    mod(0, 1)
    square("ev_in_w", (0,), 0, 5)
    for l, v in EVEN_MODS:
        mod(l, v)
    square("ev_out_w", (0,))
    moe(0)
    square("od_in_w", (0,), D, 2)
    square("od_in_w", (0,), 0, 2)
    plan.append((("gates",), True, 16, 128))
    for l, v in ODD_MODS:
        mod(l, v)
    square("od_out_w", (0,))
    moe(1)
    for l in range(2):
        ffn(l, "ffn1")
        for half in (0, 1, 4, 2, 3):
            by_cols("w_in_2", (l,), D, half * 512, 512)
        for r in (512, 0):
            for half in range(2):
                plan.append((("w_out_2", (l,), r, half * 512), True, 4, 512))
        ffn(l, "ffn2")
    return plan


class Queue:

    def __init__(self, name, chained):
        self.name, self.chained = name, chained
        self.items, self.sem, self.n, self.last = [], None, 0, None

    def stage(self, sem):
        self.sem, self.n = sem, 0

    def add(self, fn, waits, signal=True, chain=None):
        waits = list(waits)
        if (self.chained if chain is None else chain) and self.last is not None:
            waits.append(self.last)
        tok = None
        if signal:
            self.n += 1
            tok = (self.sem, self.n)
            self.last = tok
        self.items.append((fn, waits, self.sem if signal else None, 1))
        return tok

    def enter(self, flag, tok, sem):
        self.items.append(("if", flag, [tok, self.last], None))
        self.kept = (self.sem, self.n, self.last)
        self.sem, self.n, self.last = sem, 0, None

    def leave(self):
        self.items.append((None, [self.last], None, 0))
        self.items.append(("end", None, None, None))
        self.sem, self.n, self.last = self.kept

    def add_dma(self, fn, waits, sem, value):
        self.items.append((fn, list(waits), sem, 16))
        return (sem, value)

    def emit(self, eng):
        self.run(eng, iter(self.items), {})

    def run(self, eng, items, seen):
        def wait(waits):
            for w in waits:
                if w is None:
                    continue
                s, v = w
                if seen.get(id(s), 0) < v:
                    eng.wait_ge(s, v)
                    seen[id(s)] = v

        for item in items:
            if item[0] == "end":
                return
            if item[0] == "if":
                wait(item[2])
                flag = eng.value_load(item[1])
                with eng.If(flag):
                    self.run(eng, items, dict(seen))
                continue
            fn, waits, sem, inc = item
            wait(waits)
            if fn is None:
                continue
            ins = fn(eng)
            if sem is not None:
                ins.then_inc(sem, inc)


class Bank:

    def __init__(self, t):
        self.t, self.free = t, []


class Granule:

    def __init__(self):
        self.free = self.raw = self.tok = None


def program(nc, A, out, stop=None):
    ctx = ExitStack()
    with ctx:
        base = [(nc.sbuf_base + 63) // 64 * 64]

        def sb(name, *shape, dt=F32, at=None):
            where = base[0] if at is None else at
            t = nc.alloc_sbuf_tensor_at(name, [128, *shape], dt, offset=where)
            if at is None:
                base[0] += (4 * int(np.prod(shape)) + 63) // 64 * 64
            return t

        def sem(name):
            return ctx.enter_context(nc.semaphore(name))

        PE, AC, VE, PO, SP = Queue("pe", False), Queue("act", True), Queue("dve", True), Queue("pool", True), Queue("sp", False)

        def stage(name):
            for q in (PE, AC, VE, PO):
                q.stage(sem(f"s_{q.name}_{name}"))


        def pe(fn, *w, sig=False):
            return PE.add(fn, w, signal=sig)

        def ac(fn, *w, chain=None):
            return AC.add(fn, w, chain=chain)

        def ve(fn, *w, chain=None):
            return VE.add(fn, w, chain=chain)

        def po(fn, *w):
            return PO.add(fn, w)

        def mm(o, lhsT, rhs, start, stop, *w, sig=False):
            return pe(lambda e: e.matmul(o, lhsT, rhs, start=start, stop=stop, skip_group_check=True), *w, sig=sig)

        def mm3(o, L, R, start, stop, *w, sig=False):
            mm(o, L[0], R[0], start, False, *w)
            mm(o, L[0], R[1], False, False)
            return mm(o, L[1], R[0], False, stop, sig=sig)

        def tr(o, i, *w, sig=False):
            return pe(lambda e: e.transpose(o, i, ident), *w, sig=sig)

        def act(o, i, func, *w, chain=None, **kw):
            return ac(lambda e: e.activation(o, i, func, **kw), *w, chain=chain)

        def tt(o, a, b, op, *w, chain=None):
            return ve(lambda e: e.tensor_tensor(o, a, b, op), *w, chain=chain)

        def ts(o, a, s1, s2, op0, op1, *w, chain=None):
            if s2 is None:
                return ve(lambda e: e.tensor_scalar(o, a, s1, None, op0), *w, chain=chain)
            return ve(lambda e: e.tensor_scalar(o, a, s1, s2, op0, op1), *w, chain=chain)

        def stt(o, a, s, b, op0, op1, *w, chain=None):
            return ve(lambda e: e.scalar_tensor_tensor(out=o, in0=a, scalar=s, in1=b, op0=op0, op1=op1), *w, chain=chain)

        def red(o, i, op, *w):
            return ve(lambda e: e.tensor_reduce(o, i, X, op), *w)

        def recip(o, i, *w):
            return ve(lambda e: e.reciprocal(o, i), *w)

        def vcopy(o, i, *w):
            return ve(lambda e: e.tensor_copy(o, i), *w)

        def bc(ap, n, axis=1):
            a = ap.unsqueeze(axis)
            shape = list(a.shape)
            shape[axis] = n
            return a.to_broadcast(shape)

        consts = {n: a.shape[1] for n, a in constants().items()}
        cst = sb("cst", sum(consts.values()))
        C, at = {}, 0
        for n, w in consts.items():
            C[n] = cst[:, at:at + w]
            at += w
        ident, ones = C["ident"], C["ones"]
        eps = C["eps"]
        xres = sb("xres", 2, D)
        hT = [sb(f"hT{i}", KC, T, dt=F32R) for i in "hl"]
        at = base[0]
        catT = [sb(f"catT{i}", KC, T, dt=F32R) for i in "hl"]
        uT = [sb(f"uT{i}", 2, 4, T, dt=F32R, at=at + 8192 * n) for n, i in enumerate("hl")]
        acc = sb("acc", 2, D)
        gbc = sb("gbc", 2, D)
        cbc = sb("cbc", KC, 128)
        rows = sb("rows", 4, 128)
        cols = sb("cols", 4, 128)
        crow = sb("crow", 128)
        identr = sb("identr", 128, dt=F32R)
        condT = sb("condT", KC)
        modc = sb("modc", 2, 4, KC)
        rw = sb("rw", KC, NE)
        rb = sb("rb", NE)
        qkg = sb("qkg", 2, 64)
        small = sb("small", 512)
        lnc = sb("lnc", 8 * 6)
        arena_at = base[0]
        arena = sb("arena", 14336)

        def over(name, where, *shape):
            return sb(name, *shape, dt=F32R, at=arena_at + 4 * where)

        htok = [over(f"htok{i}", 2048 * n, 2, D) for n, i in enumerate("hl")]
        xg = [[x[:, :, 0:2 * CAP] for x in hT], [over(f"xg{i}", 4096 + 2048 * n, KC, 2 * CAP) for n, i in enumerate("hl")]]
        ug = [x[:, 0:2, :].rearrange("p a b -> p (a b)")[:, 0:4 * CAP].rearrange("p (f c) -> p f c", f=4) for x in catT]
        yg = [x[:, 4:8, :].rearrange("p a b -> p (a b)") for x in catT]
        G = [over(f"G{i}", 8192 + 4 * CAP * i, 2, 2 * CAP) for i in range(2)]
        GT = [over(f"GT{i}", 12288 + 256 * i, 2, 128) for i in range(3)]
        gr = over("gr", 13568, 2, NE, 2)
        ms = sb("ms", 160)
        flag = sb("flag", 8, dt=mybir.dt.int32)
        raws = [(sb(f"raw{i}", GRAN), sem(f"s_raw{i}")) for i in range(NRAW)]
        pairs = [[sb(f"pair{i}{n}", GRAN, dt=F32R) for n in "hl"] for i in range(NPAIR)]
        assert base[0] <= nc.sbuf_usable_end, base[0]
        banks = [Bank(ctx.enter_context(nc.psum_tensor(f"bank{i}", [128, 512], F32))) for i in range(8)]

        def region(at, *shape):
            n = int(np.prod(shape))
            a = arena[:, at:at + n]
            if len(shape) == 1:
                return a
            names = "abcd"[:len(shape)]
            return a.rearrange(f"p ({' '.join(names)}) -> p {' '.join(names)}", **dict(zip(names, shape)))

        stage("pre")
        s_cst, s_x, s_rows, s_bc = sem("s_cst"), sem("s_x"), sem("s_rows"), sem("s_bc")
        s_g = [sem("s_g0"), sem("s_g1")]
        crow8 = crow[0:8, :]
        s_c = sem("s_c")
        t_c0 = SP.add_dma(lambda e: e.dma_start(crow8, A["c"].rearrange("a (k p) -> (a k) p", p=128)), [], s_c, 16)
        t_id = SP.add_dma(lambda e: e.dma_start(cst[:, 0:128], A["constants"][:, 0:128]), [], s_c, 32)
        t_silu = act(crow8, crow8, ACT.Silu, t_id)
        t_cst = AC.add_dma(lambda e: e.dma_start(cst[:, 128:273], A["constants"][:, 128:273]), [], s_cst, 16)

        def row_tile(k, parts):
            at = 0
            for src in parts:
                n = src.shape[0]
                AC.add_dma(lambda e, at=at, n=n, src=src: e.dma_start(rows[at:at + n, k, :], src), [], s_rows, 0)
                row_tile.n += 16
                at += n
            return at
        row_tile.n = 0

        def flat(name):
            a = A[name]
            k = len(a.shape)
            if k == 1:
                return a.rearrange("(k p) -> k p", p=128)
            if k == 2:
                return a.rearrange("a (k p) -> (a k) p", p=128)
            return a.rearrange("a b (k p) -> (a b k) p", p=128)

        row_tile(0, [flat(n) for n in ("mix_norm_g", "ffn_norm_g", "mod_b")])
        row_tile(1, [flat(n) for n in ("ev_dw_w", "ev_dw_b")])
        row_tile(2, [flat(n) for n in ("ev_ln_g", "ev_ln_b", "od_conv_w", "od_conv_b", "od_rg_b", "od_ig_b", "od_lam",
                                       "norm_ffn1_2", "norm_mix_2", "sgu_b_2", "out_norm_attn_2")])
        n3 = row_tile(3, [flat(n) for n in ("out_norm_sgu_2", "norm_ffn2_2")])
        t_rows = (s_rows, row_tile.n)
        t_x, t_bc = (s_x, 16), (s_bc, 80)

        plan = weight_plan()
        grans = [Granule() for _ in plan]
        at_raw, at_work, at_pair, at_take = [0], [0], [0], [0]
        pair_of, raw_free = [], []

        def source(key):
            name, idx, r0, c0 = key
            w = A[name]
            for i in idx:
                w = w[i]
            return w[r0:, c0:]

        def shape_of(t, k, n):
            return t[:, 0:k * n].rearrange("p (k n) -> p k n", k=k)

        def issue():
            i = at_raw[0]
            if i == len(plan):
                return False
            w = []
            if i >= NRAW:
                w = raw_free[i - NRAW] if i - NRAW < len(raw_free) else None
                if w is None:
                    return False
            key, split, k, n = plan[i]
            t, s = raws[i % NRAW]
            if key[0] == "gates":
                parts = [(shape_of(t, 16, 128)[:, 8 * h:8 * h + 8, :], A[nm][0].rearrange("b k j -> k b j"))
                         for h, nm in enumerate(("od_rg_w", "od_ig_w"))]
            else:
                name, idx, r0, c0 = key
                a = A[name]
                for ix in idx:
                    a = a[ix]
                parts = [(shape_of(t, k, n), a[r0:r0 + 128 * k, c0:c0 + n].rearrange("(k p) n -> p k n", p=128))]
            for dst, src in parts:
                SP.add_dma(lambda e, dst=dst, src=src: e.dma_start(dst, src), w, s, 0)
                raw_n[i % NRAW] += 16
            grans[i].raw = (s, raw_n[i % NRAW])
            raw_free.append(None)
            at_raw[0] += 1
            return True

        raw_n = [0] * NRAW
        splits = [i for i, g in enumerate(plan) if g[1]]

        def summed(key):
            return key[0] == "mod_w" and key[2] > 0 and (key[1][0], key[3] // D) in SUMMED

        share = [SHARE]

        def convert():
            i = at_work[0]
            while i < len(plan) and not plan[i][1] and not summed(plan[i][0]):
                i += 1
            if i >= at_raw[0]:
                return False
            key, is_split, k, n = plan[i]
            t = raws[i % NRAW][0][:, 0:k * n]
            if not is_split:
                wv, c0 = shape_of(t, k, n), key[2] // 128
                v = ts(wv[:, 0, :], wv[:, 0, :], condT[:, c0:c0 + 1], None, ALU.mult, None, grans[i].raw, state["cond"])
                for c in range(1, k):
                    v = stt(wv[:, 0, :], wv[:, c, :], condT[:, c0 + c:c0 + c + 1], wv[:, 0, :], ALU.mult, ALU.add)
                grans[i].tok = [v]
                at_work[0] = i + 1
                return True
            m = at_pair[0]
            w = []
            if m >= NPAIR:
                w = grans[splits[m - NPAIR]].free
                if w is None:
                    return False
            hi, lo = (p[:, 0:k * n] for p in pairs[m % NPAIR])
            a = ac(lambda e: e.activation(hi, t, ACT.Copy), grans[i].raw, *w)
            cut = int(k * n * share[0]) // 128 * 128
            v = [tt(lo[:, cut:], t[:, cut:], hi[:, cut:].bitcast(F32), ALU.subtract, a)]
            if cut:
                v.append(po(lambda e: e.tensor_tensor(lo[:, 0:cut], t[:, 0:cut], hi[:, 0:cut].bitcast(F32), ALU.subtract), a))
            grans[i].tok = v
            grans[i].views = [shape_of(p, k, n) for p in pairs[m % NPAIR]]
            raw_free[i] = v
            at_pair[0] += 1
            at_work[0] = i + 1
            return True

        def advance():
            while issue() or convert():
                pass

        def take_weight(*key):
            advance()
            i = at_take[0]
            assert plan[i][0] == key, (plan[i][0], key)
            at_take[0] += 1
            g = grans[i]
            g.split, g.k, g.n = plan[i][1:]
            if not g.split:
                g.tok, g.views = g.tok or [g.raw], [shape_of(raws[i % NRAW][0], g.k, g.n)]

            def release(tok):
                g.free = [tok]
                if not g.split:
                    raw_free[i] = [tok]
            g.release = release
            return g

        def weight(name, idx, rows, c0, n):
            kg = min(GRAN // n, rows // 128)
            for r in range(0, rows // 128, kg):
                yield r, take_weight(name, idx, r * 128, c0)

        turns = {}

        def bank(*among):
            key = among
            i = turns.get(key, 0)
            turns[key] = i + 1
            return banks[among[i % len(among)]]

        def take(b):
            w, b.free = b.free, []
            return w

        def free(b, *toks):
            b.free = b.free + [t for t in toks if t is not None]

        def pair(t, *idx):
            return [x[idx] for x in t]

        def tok_major(src, name, idx, c0, bs, *waits, rows=D):
            ws = [take(b) for b in bs]
            K = rows // 128
            for r, g in weight(name, idx, rows, c0, 512):
                for th, b in enumerate(bs):
                    for c in range(g.k):
                        t = mm3(b.t[:, :], [x[:, r + c, th * 128:(th + 1) * 128] for x in src],
                                [x[:, c, :] for x in g.views], r + c == 0, r + c == K - 1,
                                *g.tok, *waits, *ws[th], sig=c == g.k - 1)
                    bs[th].done = t
                g.release(t)
            return [b.done for b in bs]

        def chan_major(src, name, idx, c0, n, bs, *waits):
            ws = [take(b) for b in bs]
            for r, g in weight(name, idx, D, c0, n):
                for f in range(n // 128):
                    o = bs[f // 2].t[:, (f % 2) * T:(f % 2 + 1) * T]
                    for c in range(g.k):
                        t = mm3(o, [x[:, c, f * 128:(f + 1) * 128] for x in g.views], [x[:, r + c, :] for x in src],
                                r + c == 0 and f % 2 == 0, r + c == KC - 1,
                                *g.tok, state["hTc"].get(r + c), *waits, *ws[f // 2], sig=c == g.k - 1)
                    bs[f // 2].done = t
                g.release(t)
            return [b.done for b in bs]

        def split(dst, src, *w):
            a = act(dst[0], src, ACT.Copy, *w)
            return tt(dst[1], src, dst[0].bitcast(F32), ALU.subtract, a)

        state = {"x": [t_x, t_x], "xq": {(th, nh): t_x for th in range(2) for nh in range(2)}, "hT": None, "hTc": {}, "cat": []}

        def rstd(at, n, of, *w):
            t = ts(small[:, at:at + n], small[:, at:at + n], 1.0 / of, EPS, ALU.mult, ALU.add, *w)
            return po(lambda e: e.tensor_tensor(small[:, at + n:at + 2 * n], small[:, at:at + n], C["minushalf"][:, 0:n],
                                                ALU.pow), t, t_cst)

        def x_rms(sq):
            for nh in range(2):
                for th in range(2):
                    h5 = slice(nh * 512, nh * 512 + 512)
                    a = act(sq[:, th, h5], xres[:, th, h5], ACT.Square, state["xq"][th, nh], state["arena"],
                            accum_out=small[:, 2 * th + nh:2 * th + nh + 1])
            t = red(small[:, 4:6], small[:, 0:4].rearrange("p (t n) -> p t n", t=2), ALU.add, a)
            return rstd(4, 2, D, t), a

        def turn_x(scale):
            for c in range(KC):
                b = bank(0, 1, 2, 3)
                w = take(b)
                for th in range(2):
                    t = tr(b.t[:, th * 128:(th + 1) * 128], xres[:, th, c * 128:(c + 1) * 128], *w,
                           state["xq"][th, c // 4], sig=th == 1)
                hi, lo = pair(hT, slice(None), c)
                a = act(hi, b.t[:, 0:T], ACT.Copy, t, *state.get("hT_free", []), scale=scale[:, c:c + 1], chain=False)
                e = stt(lo, b.t[:, 0:T], scale[:, c:c + 1], hi.bitcast(F32), ALU.mult, ALU.subtract, a, chain=False)
                free(b, e)
                state["hTc"][c] = e
            state["hT"] = []
            r, state["arena"] = x_rms(region(12288, 2, D))
            return r

        def norm_T(scale, shift, *waits, pairs=True):
            xn = region(12288, 2, D)
            r, _ = x_rms(xn)
            ts_ = {}
            for half in range(2):
                h5 = slice(512 * half, 512 * half + 512)
                ts_[0, half] = ts(xn[:, 0, h5], xres[:, 0, h5], small[:, 6:7], None, ALU.mult, None, r)
                ts_[1, half] = act(xn[:, 1, h5], xres[:, 1, h5], ACT.Copy, r, scale=small[:, 7:8])
            hf = region(10240, KC, T)
            state["hTc"] = {}
            for c in range(KC):
                b = bank(0, 1, 2, 3)
                w = take(b)
                for th in range(2):
                    t = tr(b.t[:, th * 128:(th + 1) * 128], xn[:, th, c * 128:(c + 1) * 128], *w, ts_[th, c // 4], sig=th == 1)
                o = hf[:, c, :]
                if shift is None:
                    hi, lo = pair(hT, slice(None), c)
                    a = act(hi, b.t[:, 0:T], ACT.Copy, t, *waits, *state.get("hT_free", []), scale=scale[:, c:c + 1])
                    e = stt(lo, b.t[:, 0:T], scale[:, c:c + 1], hi.bitcast(F32), ALU.mult, ALU.subtract, a)
                elif c % 2:
                    e = act(o, b.t[:, 0:T], ACT.Identity, t, *waits, scale=scale[:, c:c + 1], bias=shift[:, c:c + 1],
                            chain=False)
                else:
                    e = ts(o, b.t[:, 0:T], scale[:, c:c + 1], shift[:, c:c + 1], ALU.mult, ALU.add, t, *waits, chain=False)
                    e0 = e
                free(b, e)
                if pairs and shift is not None and c % 4 == 3:
                    h4 = slice(c - 3, c + 1)
                    e = split(pair(hT, slice(None), h4), hf[:, h4, :], e, e0, *state.get("hT_free", []))
                    for i in range(c - 3, c + 1):
                        state["hTc"][i] = e
            state["arena"] = t
            state["hT"] = [] if pairs else [e, e0]
            return [e]

        state["arena"] = None
        c_mix = cols[:, 0, 0:16].rearrange("p (l k) -> p l k", l=2)
        c_ffn = cols[:, 0, 16:32].rearrange("p (l k) -> p l k", l=2)
        c_modb = cols[:, 0, 32:128].rearrange("p (l v k) -> p l v k", l=2, v=6)
        c_dw = cols[:, 1, 0:124].rearrange("p (t k) -> p t k", k=4)
        c_dwb = cols[:, 1, 124:128]
        c2, at2 = {}, 0
        for n, w in (("ln_g", 4), ("ln_b", 4), ("cw", 32), ("cb", 8), ("rgb", 8), ("igb", 8), ("lam", 8),
                     ("ffn1", 16), ("mix", 16), ("sgub", 8), ("attn", 8)):
            c2[n] = cols[:, 2, at2:at2 + w]
            at2 += w
        c2["sgu"], c2["ffn2"] = cols[:, 3, 0:8], cols[:, 3, 8:24]

        t_idr = vcopy(identr[:, :], ident, t_id)
        b = bank(0, 1, 2, 3)
        t = pe(lambda e, b=b: e.transpose(b.t[:, 0:8], crow8, ident[0:8, 0:8]), t_silu, t_id, *take(b), sig=True)
        t_cond = vcopy(condT[:, :], b.t[:, 0:8], t)
        free(b, t_cond)
        t_cbc = vcopy(cbc[:, :, :], bc(condT[:, :], 128, 2), t_cond)
        state["cond"] = t_cbc

        mrow = acc[:, 0, :].rearrange("p (a n) -> p a n", a=2)

        class Mods:

            def __init__(self, vectors, bs):
                self.todo = [(l, v, half) for l, v in vectors for half in range(2)]
                self.bs, self.n, self.turns, self.tok = bs, 0, None, {}

            def turn(self):
                if self.turns is None:
                    return
                l, v, half, b, a, row, slot = self.turns
                self.turns = None
                for f in range(4):
                    t = pe(lambda e, f=f: e.transpose(b.t[:, f:f + 1], row[0:1, f * 128:(f + 1) * 128], ident[0:1, 0:1]),
                           a, sig=True)
                self.row_free[slot] = t
                k = {0: 0, 1: 1, 3: 2, 4: 3}[v]
                o = modc[:, l, k, 4 * half:4 * half + 4]
                t = tt(o, b.t[:, 0:4], c_modb[:, l, v, 4 * half:4 * half + 4], ALU.add, t, t_cols)
                free(b, t)
                if v in (1, 4):
                    g = (c_mix if v == 1 else c_ffn)[:, l, 4 * half:4 * half + 4]
                    t = stt(o, o, 1.0, g, ALU.add, ALU.mult)
                self.tok[l, v] = t

            row_free = {}

            def half(self):
                l, v, half = self.todo.pop(0)
                b = self.bs[self.n % 2]
                w = take(b)
                gate = v in (2, 5)
                m = 128 if gate else 1
                k = v // 5
                if gate and half == 0:
                    gn[k] += 16
                    self.td = AC.add_dma(lambda e: e.dma_start(
                        gbc[:, k, :], A["mod_b"][l, v * D:(v + 1) * D].partition_broadcast(128)),
                        state.get(("gbc", k), []), s_g[k], gn[k])
                for r, g in weight("mod_w", (l,), D, v * D + half * 512, 512):
                    wv = g.views[0]
                    if r == 0 or (l, v) not in SUMMED:
                        for c in range(g.k):
                            lhs = cbc[:, r + c, :] if gate else condT[:, r + c:r + c + 1]
                            t = mm(b.t[0:m, :], lhs, wv[:, c, :], r + c == 0, r + c == KC - 1, *g.tok, t_cbc, *w,
                                   sig=c == g.k - 1)
                    else:
                        t = mm(b.t[0:m, :], ones[:, 0:m], wv[:, 0, :], False, True, *g.tok, t_cst, sig=True)
                    g.release(t)
                    if r == 0:
                        self.turn()
                if gate:
                    o = gbc[:, k, half * 512:(half + 1) * 512]
                    t = tt(o, b.t[:, :], o, ALU.add, t, self.td)
                    free(b, t)
                    self.tok[l, v] = t
                    self.n += 1
                    return
                row = mrow[0:1, self.n % 2, :]
                a = act(row, b.t[0:1, :], ACT.Copy, t, self.row_free.get(self.n % 2))
                self.turns = (l, v, half, b, a, row, self.n % 2)
                self.n += 1

            def fill(self, n):
                for _ in range(min(n, len(self.todo))):
                    self.half()

            def finish(self):
                self.fill(99)
                self.turn()

        gn = [0, 0]

        def residual(name, idx, gate, *waits):
            done = []
            for nh in range(2):
                bs = [bank(4, 5, 6, 7) for _ in range(2)]
                tb = tok_major(catT, name, idx, nh * 512, bs, *waits)
                for th in range(2):
                    b, t = bs[th], tb[th]
                    o = xres[:, th, nh * 512:(nh + 1) * 512]
                    if gate is None:
                        t2 = tt(o, b.t[:, :], o, ALU.add, t)
                        free(b, t2)
                    else:
                        tmp = acc[:, th, nh * 512:(nh + 1) * 512]
                        t2 = tt(tmp, b.t[:, :], gate[:, nh * 512:(nh + 1) * 512], ALU.mult, t)
                        free(b, t2)
                        t2 = tt(o, o, tmp, ALU.add)
                    state["xq"][th, nh] = t2
                    done.append(t2)
            state["x"] = [done[-1]]
            state["cat_free"] = [t]
            return done[-1]

        rms_row = region(9216, 2, T).rearrange("p a t -> p (a t)")

        def spread_rms(t):
            dg = region(9728, 2, 128)
            b = banks[4]
            w = take(b)
            for th in range(2):
                v = ts(dg[:, th, :], ident, small[:, 6 + th:7 + th], None, ALU.mult, None, t, state["arena"])
            for half in range(2):
                for th in range(2):
                    t = mm(b.t[:, half * T + th * 128:half * T + (th + 1) * 128], ones, dg[:, th, :], half + th == 0, True,
                           v, *w, sig=True)
            v = act(rms_row, b.t[:, :], ACT.Copy, t)
            free(b, v)
            state["rms_row"] = v

        class Feed:
            def __init__(self):
                self.pending, self.n, self.last_u = None, 0, {}

            def down(self):
                w2, us, buf, nf, first, last, evac = self.pending
                self.pending = None
                name, idx, r0 = w2
                ws = [take(banks[4 + i]) if first else [] for i in range(4)]
                for r in range(0, nf, 2):
                    g = take_weight(name, idx, r0 + r * 128, 0)
                    for i in range(4):
                        th, nh = i // 2, i % 2
                        for f in range(r, r + 2):
                            t = mm3(banks[4 + i].t[:, :], [x[:, buf, f, th * 128:(th + 1) * 128] for x in uT],
                                    [x[:, f - r, nh * 512:(nh + 1) * 512] for x in g.views],
                                    first and f == 0, last and f == nf - 1, *g.tok, us[r // 2], *ws[i], sig=f == r + 1)
                        banks[4 + i].done = t
                    g.release(t)
                if evac is not None:
                    for i in range(4):
                        free(banks[4 + i], evac(i // 2, i % 2, banks[4 + i], banks[4 + i].done))
                self.last_u[buf] = [t]

            def group(self, w1, w3, w2, c0, nf, first, last, evac):
                buf = self.n % 2
                self.n += 1
                b1, b3 = banks[0:2], banks[2:4]
                b1, b3 = b1[:nf // 2], b3[:nf // 2]
                t1 = chan_major(hT, *w1, c0, nf * 128, b1, *state["hT"])
                if first:
                    spread_rms(state["rms"])
                t3 = chan_major(hT, *w3, c0, nf * 128, b3)
                state["hT_free"] = [t3[-1]]
                us = []
                for i in range(nf // 2):
                    uf = region(7168 + 512 * i, 512)
                    v = tt(uf, b1[i].t[:, :], rms_row, ALU.mult, t1[i], state["rms_row"], state["arena"])
                    free(b1[i], v)
                    a = act(uf, uf, ACT.Silu, v)
                    v = tt(uf, uf, b3[i].t[:, :], ALU.mult, a, t3[i])
                    free(b3[i], v)
                    v = tt(uf, uf, rms_row, ALU.mult)
                    dst = [x[:, buf, 2 * i:2 * i + 2, :].rearrange("p f t -> p (f t)") for x in uT]
                    us.append(split(dst, uf, v, *self.last_u.get(buf, []), *state.get("cat_free", [])))
                if self.pending is not None:
                    self.down()
                self.pending = (w2, us, buf, nf, first, last, evac)

            def finish(self):
                self.down()

        feed = Feed()

        def moe(l, k):
            gate_row = gbc[:, k, :]
            b = bank(0, 1, 2, 3)
            w = take(b)
            for th in range(2):
                for c in range(KC):
                    t = mm(b.t[:, th * NE:(th + 1) * NE], region(10240, KC, T)[:, c, th * 128:(th + 1) * 128], rw[:, c, :],
                           c == 0, c == KC - 1, *w, *state["hT"], t_bc, sig=c == KC - 1)
            t_score = t
            hf = region(10240, KC, T)
            by_token = []
            for i, bt in enumerate(banks[4:8]):
                wt = take(bt)
                th, cs = i // 2, slice(512 * (i % 2), 512 * (i % 2) + 512)
                for c in range(4):
                    t = tr(bt.t[:, c * 128:(c + 1) * 128], hf[:, 4 * (i % 2) + c, th * 128:(th + 1) * 128], *wt,
                           *state["hT"], sig=c == 3)
                by_token.append((bt, [x[:, th, cs] for x in htok]))
                bt.done = t
            S = lambda at, n: small[:, 64 + at:64 + at + n]
            score, biased = S(0, 32), S(32, 32)
            t = act(score, b.t[:, 0:32], ACT.Sigmoid, t_score, state.get("gates"))
            free(b, t)
            for bt, (hi, _) in by_token:
                got_hi = act(hi, bt.t[:, :], ACT.Copy, bt.done)
            v2 = lambda a, n: a.rearrange("p (t n) -> p t n", t=2)
            v8 = lambda a: a.rearrange("p (g n) -> p g n", g=8)
            t = tt(v2(biased, 16), v2(score, 16), bc(rb[:, :], 2), ALU.add, t, t_bc)
            b8 = v8(biased)
            ps = v8(S(64, 48))
            tt(ps[:, :, 0:3], b8[:, :, 0:3], b8[:, :, 1:4], ALU.add)
            tt(ps[:, :, 3:5], b8[:, :, 0:2], b8[:, :, 2:4], ALU.add)
            tt(ps[:, :, 5:6], b8[:, :, 0:1], b8[:, :, 3:4], ALU.add)
            gs = S(112, 8)
            red(gs, ps, ALU.max)

            def below(o, vals, g, limit):
                v = vals.rearrange("p (g n) -> p g n", g=g)
                vi, vj = bc(v, 4, 3), bc(v, 4, 2)
                gt = S(128, 16 * g)
                ge = S(256, 16 * g)
                g4 = lambda a: a.rearrange("p (g i j) -> p g i j", i=4, j=4)
                g16 = lambda a: a.rearrange("p (g i) -> p g i", i=16)
                tt(g4(gt), vj, vi, ALU.is_gt)
                tt(g4(ge), vj, vi, ALU.is_ge)
                tt(ge, ge, gt, ALU.subtract)
                tt(g16(ge), g16(ge), bc(C["first"], g), ALU.mult)
                tt(gt, ge, gt, ALU.add)
                red(o, gt.rearrange("p (gi j) -> p gi j", j=4), ALU.add)
                return ts(o, o, float(limit), None, ALU.is_lt, None)

            gm, em = S(120, 8), S(384, 32)
            below(gm, gs, 2, 1)
            below(em, biased, 8, 2)
            tt(v8(em), v8(em), bc(gm, 4, 2), ALU.mult)
            t_sel = vcopy(ms[:, 0:32], em)
            tt(em, em, score, ALU.mult)
            den = S(416, 2)
            red(den, v2(em, 16), ALU.add)
            recip(den, den)
            t_gate = tt(v2(em, 16), v2(em, 16), bc(den, 16, 2), ALU.mult)

            mask, place, late, gg = (ms[:, 32 * i:32 * i + 32] for i in range(4))
            t_mask = t_sel
            b = bank(0, 1, 2, 3)
            w = take(b)
            mm(b.t[:, 0:16], C["below"], mask[:, 0:16], True, True, t_mask, *w)
            mm(b.t[:, 16:32], ones, mask[:, 0:16], False, False)
            mm(b.t[:, 16:32], C["below"], mask[:, 16:32], False, True)
            mm(b.t[:, 32:48], ones, mask[:, 0:16], False, False)
            t = mm(b.t[:, 32:48], ones, mask[:, 16:32], False, True, sig=True)
            stt(place, b.t[:, 0:32], 1.0, mask, ALU.add, ALU.mult, t)
            t_place = ts(place, place, -1.0, None, ALU.add, None)
            iota = C["iota"]
            got = {}

            def one_hot(p):
                g = G[p % 2]
                w = [t_place, got.get(("turned", 2 * p - 3)), state["arena"]]
                for th in range(2):
                    for m in range(2):
                        at_ = place[:, th * NE + 2 * p + m:th * NE + 2 * p + m + 1]
                        o = g[:, th, m * CAP:(m + 1) * CAP]
                        if p == 0 and th == 1:
                            t2 = ts(o, iota[:, 0:CAP], at_, None, ALU.is_equal, None, *w)
                        else:
                            t = t2 = po(lambda q, o=o, at_=at_: q.tensor_scalar(o, iota[:, 0:CAP], at_, None, ALU.is_equal), *w)
                        if th == 0:
                            t0 = t
                got["G", p] = [t0, t2]

            one_hot(0)
            b_place = b
            for b, (hi, lo) in by_token:
                t_htok = tt(lo, b.t[:, :], hi.bitcast(F32), ALU.subtract, got_hi)
                free(b, t_htok)
            t = red(ms[:, 128:129], b_place.t[:, 32:48], ALU.max)
            free(b_place, t)
            t_flag = ts(flag[:, 0:1], ms[:, 128:129], float(CAP), None, ALU.is_gt, None)
            ts(late, place, float(CAP), None, ALU.is_ge, None)
            tt(late, late, em, ALU.mult)
            a = act(gr[:, :, :, 0], v2(em, 16), ACT.Copy, t_gate, state["arena"])
            t_gr = tt(gr[:, :, :, 1], v2(em, 16), gr[:, :, :, 0].bitcast(F32), ALU.subtract, a)

            bA, bB, bC, bD = banks[0:4]

            def gather(p, half, bs):
                g = G[p % 2]
                for i, b in enumerate(bs):
                    w = take(b)
                    for c in range(2):
                        ch = 4 * half + 2 * i + c
                        for n in range(2):
                            for th in range(2):
                                t = mm(b.t[:, c * 2 * CAP:(c + 1) * 2 * CAP], htok[n][:, th, ch * 128:(ch + 1) * 128],
                                       g[:, th, :], c == 0 and n == 0 and th == 0, n == 1 and th == 1,
                                       *got["G", p], t_htok, *w, sig=c == 1 and n == 1 and th == 1)
                    ch = 4 * half + 2 * i
                    hi, lo = (x[:, ch:ch + 2, :] for x in xg[p % 2])
                    bv = b.t[:, 0:4 * CAP].rearrange("p (k c) -> p k c", k=2)
                    a = act(hi, bv, ACT.Copy, t, *(state.get("hT_free", []) if p == 0 else []))
                    v = tt(lo, bv, hi.bitcast(F32), ALU.subtract, a)
                    free(b, v)
                got["x", p] = v

            def turn_hot(e):
                b = bB
                w = take(b)
                g, gt = G[e // 2 % 2][:, :, e % 2 * CAP:(e % 2 + 1) * CAP], GT[e % 3]
                for th in range(2):
                    mm(b.t[0:CAP, 256:258], g[:, th, :], gr[:, th, e, :], th == 0, th == 1, t_gr, *got["G", e // 2], *w)
                for th in range(2):
                    t = pe(lambda q, th=th: q.transpose(b.t[0:CAP, th * 128:(th + 1) * 128].bitcast(F32R), g[:, th, :],
                                                        identr[:, :]), *w, t_idr, sig=True)
                got["turned", e] = t
                a = act(gt[0:CAP, :, :].rearrange("p a b -> p (a b)"), b.t[0:CAP, 0:256], ACT.Copy, t,
                        got.get(("scattered", e - 3)))
                v = red(gg[0:CAP, e:e + 1], b.t[0:CAP, 256:258], ALU.add, a)
                free(b, v)
                got["GT", e], got["gg", e] = a, v

            def rows_times(name, e, b, between, *waits):
                w = take(b)
                for r, g in weight(name, (l, e), D, 0, 512):
                    for c in range(g.k):
                        t = mm3(b.t[0:CAP, :], [x[:, r + c, e % 2 * CAP:(e % 2 + 1) * CAP] for x in xg[e // 2 % 2]], [x[:, c, :] for x in g.views],
                                r + c == 0, r + c == KC - 1, *g.tok, *waits, *w, sig=c == g.k - 1)
                    g.release(t)
                    if r == 0:
                        between()
                return t

            def turn_hidden(e, bC=bC):
                w = take(bC)
                uf = got["uf", e][0]
                for f in range(4):
                    t = pe(lambda q, f=f: q.transpose(bC.t[:, f * CAP:(f + 1) * CAP], uf[0:CAP, f * 128:(f + 1) * 128],
                                                      ident[0:CAP, 0:CAP]), *w, got["uf", e][1], sig=f == 3)
                hi, lo = (x[:, :, :].rearrange("p f c -> p (f c)") for x in ug)
                a = act(hi, bC.t[:, 0:4 * CAP], ACT.Copy, t, *(state["cat_free"] if e == 0 else []))
                v = tt(lo, bC.t[:, 0:4 * CAP], hi.bitcast(F32), ALU.subtract, a)
                free(bC, v)
                got["u", e] = v

            def down(e):
                ws = [take(bC), take(bD)]
                for r in (0, 2):
                    g = take_weight("ex_w2", (l, e), r * 128, 0)
                    for nh, b in enumerate((bC, bD)):
                        for f in (r, r + 1):
                            t = mm3(b.t[0:CAP, :], [x[:, f, :] for x in ug],
                                    [x[:, f - r, nh * 512:(nh + 1) * 512] for x in g.views],
                                    f == 0, f == 3, *g.tok, got["u", e], *ws[nh], sig=f == r + 1)
                        b.done = t
                    g.release(t)
                for nh, b in enumerate((bC, bD)):
                    hi, lo = (x[0:CAP, nh * 512:(nh + 1) * 512] for x in yg)
                    gate = gg[0:CAP, e:e + 1]
                    a = act(hi, b.t[0:CAP, :], ACT.Copy, b.done, got["gg", e], scale=gate)
                    v = stt(lo, b.t[0:CAP, :], gate, hi.bitcast(F32), ALU.mult, ALU.subtract, a)
                    free(b, v)
                got["y", e] = v

            def scatter(e):
                for i in range(4):
                    th, nh = i % 2, i // 2
                    b = banks[4 + i]
                    w = take(b) if e == 0 else []
                    gt = GT[e % 3][0:CAP, th, :]
                    for n in range(2):
                        t = mm(b.t[:, :], gt, yg[n][0:CAP, nh * 512:(nh + 1) * 512], e == 0 and n == 0, e == NE - 1 and n == 1,
                               got["y", e], got["GT", e], *w, sig=n == 1)
                    b.done = t
                got["scattered", e] = t

            gather(0, 0, (bC, bD))
            gather(0, 1, (bA, bB))
            for e in range(NE):
                if e % 2 == 0 and e + 2 < NE:
                    one_hot(e // 2 + 1)
                t1 = rows_times("ex_w1", e, bA, lambda: e and turn_hidden(e - 1), got["x", e // 2])
                uf = region(13056, 512)
                a = act(uf[0:CAP, :], bA.t[0:CAP, :], ACT.Silu, t1)
                free(bA, a)
                turn_hot(e)
                if 0 < e < NE - 1:
                    down(e - 1)

                def between():
                    if e // 2 + 1 < NE // 2:
                        gather(e // 2 + 1, e % 2, (bC, bD))
                t3 = rows_times("ex_w3", e, bB, between)
                v = tt(uf[0:CAP, :], uf[0:CAP, :], bB.t[0:CAP, :], ALU.mult, a, t3)
                free(bB, v)
                got["uf", e] = (uf, v)
                if 0 < e < NE - 1:
                    scatter(e - 1)
            down(NE - 2)
            turn_hidden(NE - 1, bA)
            scatter(NE - 2)
            down(NE - 1)
            scatter(NE - 1)
            state["hT_free"] = [t3]
            state["cat_free"] = [got["scattered", NE - 1]]
            for i in range(4):
                th, nh = i % 2, i // 2
                b = banks[4 + i]
                o, x = acc[:, th, nh * 512:(nh + 1) * 512], xres[:, th, nh * 512:(nh + 1) * 512]
                t = tt(o, b.t[:, :], gate_row[:, nh * 512:(nh + 1) * 512], ALU.mult, b.done)
                free(b, t)
                if i % 2:
                    t = tt(x, x, o, ALU.add)
                else:
                    t_x = po(lambda q, o=o, x=x: q.tensor_tensor(x, x, o, ALU.add), t)
                state["xq"][th, nh] = t if i % 2 else t_x
            overflow(l, gate_row, late, t_flag, t_x)
            state["x"] = [t, t_x]
            state["gates"] = t
            state["arena"] = got["scattered", NE - 1]
            state[("gbc", k)] = [t]

        def overflow(l, gate_row, late, t_flag, t_x):
            f1 = flag[0:1, 0:1]
            s_w = [sem(f"s_over_w{l}{i}") for i in range(4)]
            for q in (PE, AC, VE):
                q.enter(f1, t_flag, sem(f"s_over_{q.name}{l}"))
            VE.items.append((None, [t_x], None, 0))
            start = [b.done for b in banks[4:8]] + [VE.kept[2]]
            buf = [region(2048 * i, GRAN) for i in range(4)]
            u = region(8192, 4, T)
            hf = region(10240, KC, T)
            used = [0] * 4
            buf_free = [start] * 4
            v = u_free = None
            y_free = [None] * 4

            def fetch(i, name, e, r, k, n):
                used[i] += 16
                src = A[name][l, e, r:r + 128 * k, :].rearrange("(k p) n -> p k n", p=128)
                dst = shape_of(buf[i], k, n)
                return dst, AC.add_dma(lambda q: q.dma_start(dst, src), buf_free[i], s_w[i], used[i])

            for e in range(NE):
                ws = [fetch(i, "ex_w1" if i < 2 else "ex_w3", e, 512 * (i % 2), 4, 512) for i in range(4)]
                for i in range(4):
                    for f in range(4):
                        o = banks[2 * (i // 2) + f // 2].t[:, (f % 2) * T:(f % 2 + 1) * T]
                        for c in range(4):
                            t = mm(o, ws[i][0][:, c, f * 128:(f + 1) * 128], hf[:, 4 * (i % 2) + c, :],
                                   i % 2 == 0 and c == 0 and f % 2 == 0, i % 2 == 1 and c == 3, ws[i][1], v, *start,
                                   sig=c == 3)
                    buf_free[i] = [t]
                w2 = [fetch(i, "ex_w2", e, 256 * i, 2, D) for i in range(2)]
                for i in range(2):
                    dst = u[:, 2 * i:2 * i + 2, :].rearrange("p f t -> p (f t)")
                    a = act(dst, banks[i].t[:, :], ACT.Silu, t, u_free)
                    v = tt(dst, dst, banks[2 + i].t[:, :], ALU.mult, a)
                for j in range(4):
                    th, nh = j // 2, j % 2
                    for f in range(4):
                        ty = mm(banks[4 + j].t[:, :], u[:, f, th * 128:(th + 1) * 128],
                                w2[f // 2][0][:, f % 2, nh * 512:(nh + 1) * 512], f == 0, f == 3, w2[f // 2][1], v,
                                y_free[j], sig=f == 3)
                    o, x = acc[:, th, nh * 512:(nh + 1) * 512], xres[:, th, nh * 512:(nh + 1) * 512]
                    y_free[j] = stt(o, banks[4 + j].t[:, :], late[:, th * NE + e:th * NE + e + 1],
                                    gate_row[:, nh * 512:(nh + 1) * 512], ALU.mult, ALU.mult, ty)
                    tt(x, x, o, ALU.add)
                buf_free[0] = buf_free[1] = [ty]
                u_free = ty
            for q in (PE, AC):
                q.items.append((None, [VE.last], None, 0))
            for q in (PE, AC, VE):
                q.leave()

        def ffn(l, pre):
            def evac(th, nh, b, t):
                o = xres[:, th, nh * 512:(nh + 1) * 512]
                t = stt(o, b.t[:, :], 0.5, o, ALU.mult, ALU.add, t)
                state["xq"][th, nh] = t
                state["x"] = [t]
                return t
            for g in range(6):
                nf = 4 if g < 5 else 2
                feed.group((pre + "_w_gate_2", (l,)), (pre + "_w_up_2", (l,)), (pre + "_w_down_2", (l,), g * 512),
                           g * 512, nf, g == 0, g == 5, evac if g == 5 else None)
            feed.finish()

        mods = Mods(((0, 0), (0, 1)), (banks[0], banks[1]))
        mods.fill(1)
        t_cols = []
        for k in range(4):
            n = (128, 128, 120, n3)[k]
            b = bank(4, 5, 6, 7)
            t = pe(lambda e, b=b, k=k, n=n: e.transpose(b.t[:, 0:n], rows[0:n, k, :], ident[0:n, 0:n]),
                   t_rows, t_cst, *take(b), sig=True)
            t_cols = vcopy(cols[:, k, 0:n], b.t[:, 0:n], t)
            free(b, t_cols)
        AC.add_dma(lambda e: e.dma_start(xres[:, :, :], A["x"].rearrange("a (t p) d -> p (a t) d", p=128)),
                         [], s_x, 16)
        mods.finish()
        norm_T(modc[:, 0, 1, :], modc[:, 0, 0, :], mods.tok[0, 1], mods.tok[0, 0])
        for dst, src in ((qkg[:, 0, :], A["ev_q_g"][0, :]), (qkg[:, 1, :], A["ev_k_g"][0, :]),
                         (rb[:, :], A["router_b"])):
            AC.add_dma(lambda e, dst=dst, src=src: e.dma_start(dst, src.partition_broadcast(128)), [], s_bc, 0)
        AC.add_dma(lambda e: e.dma_start(rw[:, :, :], A["router_w"].rearrange("(k p) n -> p k n", p=128)),
                   [], s_bc, 0)
        AC.add_dma(lambda e: e.dma_start(cst[:, 273:], A["constants"][:, 273:]), [], s_bc, 0)

        stage("even")
        upad = region(0, 4, 286)
        u = region(1152, 4, T)
        qs = region(2176, 2, 512)
        ks = region(3200, 2, 512)
        vs = region(4224, 2, 512)
        qT = region(5248, 4, T)
        kT = region(6272, 4, T)
        L = region(7296, 6, 512)
        sq = region(10368, 1024)
        W = region(2176, 2, 512)

        t_pad = po(lambda e: e.memset(upad[:, :, 0:30], 0.0), state["arena"])
        ab = [banks[4], banks[5]]
        ta = chan_major(hT, "ev_in_w", (0,), 0, 512, ab, *state["hT"])
        gb = [banks[6], banks[7]]
        tg = chan_major(hT, "ev_in_w", (0,), 512, 512, gb)
        for i in range(2):
            a = act(u[:, 2 * i:2 * i + 2, :], gb[i].t[:, :].rearrange("p (a n) -> p a n", a=2), ACT.Sigmoid, tg[i],
                    state["arena"])
            free(gb[i], a)
            t_u = tt(upad[:, 2 * i:2 * i + 2, 30:286], u[:, 2 * i:2 * i + 2, :],
                     ab[i].t[:, :].rearrange("p (a n) -> p a n", a=2), ALU.mult, a, ta[i])
            free(ab[i], t_u)
        def taps():
            for k in range(31):
                for c in range(4):
                    if k == 0:
                        cur[c] = ts(u[:, c, :], upad[:, c, 0:T], c_dw[:, 0, c:c + 1], c_dwb[:, c:c + 1], ALU.mult, ALU.add,
                                    t_u, t_pad, t_cols, chain=False)
                    else:
                        cur[c] = stt(u[:, c, :], upad[:, c, k:k + T], c_dw[:, k, c:c + 1], u[:, c, :], ALU.mult, ALU.add,
                                     cur[c], chain=False)
                yield

        cur, tap = {}, taps()

        def conv(n):
            for _ in range(n):
                next(tap, None)

        mods = Mods(EVEN_MODS, (banks[6], banks[7]))
        todo = iter(EVEN_AT)

        def between():
            taps_, halves = next(todo)
            mods.fill(halves)
            conv(taps_)

        between()
        tq = {}
        for n, (name, dst) in enumerate((("q", qs), ("k", ks), ("v", vs))):
            bs = [bank(0, 1, 2, 3) for _ in range(2)]
            tb = tok_major(hT, "ev_in_w", (0,), 1024 + n * 512, bs)
            for th in range(2):
                tq[name, th] = act(dst[:, th, :], bs[th].t[:, :], ACT.Copy, tb[th])
                free(bs[th], tq[name, th])
            between()
        state["hT_free"] = [tb[1]]
        between()
        ts(qkg[:, 0, :], qkg[:, 0, :], 0.125, None, ALU.mult, None, t_bc)
        for name, dst, g in (("q", qs, 0), ("k", ks, 1)):
            hv = dst[:, :, :].rearrange("p t (h d) -> p (t h) d", d=64)
            sv = sq.rearrange("p (h d) -> p h d", d=64)
            tt(sv, hv, hv, ALU.mult, tq[name, 1])
            t = red(small[:, 32:48], sv, ALU.add)
            t = act(small[:, 32:48], small[:, 32:48], ACT.Sqrt, t, scale=1.0 / 64, bias=eps)
            between()
            recip(small[:, 48:64], small[:, 32:48], t)
            tt(hv, hv, bc(small[:, 48:64], 64, 2), ALU.mult)
            t = tt(hv, hv, bc(qkg[:, g, :], 16), ALU.mult)
            dT = (qT, kT)[g]
            for pr in range(2):
                b = banks[2 * g + pr]
                w = take(b)
                for a2 in range(2):
                    for th in range(2):
                        c = pr * 2 + a2
                        tp = tr(b.t[:, a2 * T + th * 128:a2 * T + (th + 1) * 128], dst[:, th, c * 128:(c + 1) * 128],
                                t, *w, sig=True)
                tp = act(dT[:, pr * 2:pr * 2 + 2, :], b.t[:, :].rearrange("p (a n) -> p a n", a=2), ACT.Copy, tp)
                free(b, tp)
            between()
        t_qk = tp
        tz = {}
        for par in range(2):
            r = slice(64 * par, 64 * par + 64)
            for j in range(2):
                b = banks[3 * par + j]
                w = take(b)
                for m in range(2):
                    tz[par, j] = mm(b.t[:, m * T:(m + 1) * T], kT[r, 2 * j + m, 0:128], qT[r, 2 * j + m, :],
                                    m == 0, m == 1, t_qk, *w, sig=m == 1)
            b = banks[3 * par + 2]
            w = take(b)
            for m in range(4):
                tz[par, 2] = mm(b.t[:, m * 128:(m + 1) * 128], kT[r, m, 128:256], qT[r, m, 128:256],
                                m == 0, m == 3, t_qk, *w, sig=m == 3)
        def diag(ap, j):
            if j == 2:
                return ap.rearrange("p (m q) -> p m q", q=128)
            return ap.rearrange("p (m n q) -> p m n q", m=2, q=128)[:, :, 0, :]
        def off(ap):
            return ap.rearrange("p (m n q) -> p m n q", m=2, q=128)[:, :, 1, :]
        between()
        tl = {}
        ta6 = {}
        for i in range(6):
            par, j = i // 3, i % 3
            t = act(L[:, i, :], banks[i].t[:, :], ACT.Abs, tz[par, j])
            t = act(L[:, i, :], L[:, i, :], ACT.Exp, scale=-1.0)
            ta6[i] = act(L[:, i, :], L[:, i, :], ACT.Ln, bias=1.0)
        for i in range(6):
            if i % 2:
                between()
            par, j = i // 3, i % 3
            t = stt(L[:, i, :], banks[i].t[:, :], 0.0, L[:, i, :], ALU.max, ALU.add, ta6[i])
            d = diag(L[:, i, :], j)
            tl[i] = tt(d, d, bc(C["below"], d.shape[1]), ALU.mult)
        tR = {}
        for par in range(2):
            for j in (2, 0, 1):
                i = 3 * par + j
                tR[i] = mm(banks[i].t[:, :], C["ntri"], L[:, i, :], False, True, tl[i], tl[3 * par + 2], sig=True)
                if j < 2:
                    tR[i] = mm(off(banks[i].t[:, :]), C["nones"],
                               L[:, 3 * par + 2, j * 256:(j + 1) * 256].rearrange("p (m q) -> p m q", q=128),
                               False, True, tl[3 * par + 2], sig=True)
        between()
        tw = {}
        t_tri = tR[4] if tR[4][1] > tR[5][1] else tR[5]
        for i in (2, 0, 1, 5, 3, 4):
            j = i % 3
            d = diag(L[:, i, :], j)
            t = tt(d, diag(banks[i].t[:, :], j), bc(C["negdiag"], d.shape[1]), ALU.add, t_tri)
            if j < 2:
                act(off(L[:, i, :]), off(banks[i].t[:, :]), ACT.Exp, t)
            tw[i] = act(d, d, ACT.Exp, t)
            free(banks[i], tw[i])
        between()
        for ch in range(4):
            if ch % 2 == 0:
                b = banks[6 + ch // 2]
                w = take(b)
            c0 = (ch % 2) * T
            for par in range(2):
                h = 2 * ch + par
                r = slice(64 * par, 64 * par + 64)
                i0, i2 = 3 * par + ch // 2, 3 * par + 2
                mm(b.t[r, c0:c0 + T], vs[:, 0, h * 64:(h + 1) * 64], L[:, i0, (ch % 2) * T:(ch % 2 + 1) * T],
                   ch % 2 == 0, False, tw[i0], tq["v", 1], *w)
                t = mm(b.t[r, c0 + 128:c0 + T], vs[:, 1, h * 64:(h + 1) * 64], L[:, i2, ch * 128:(ch + 1) * 128],
                       False, True, tw[i2], sig=par == 1)
            if ch % 2:
                bv = b.t[:, :].rearrange("p (a n) -> p a n", a=2)
                hi, lo = pair(catT, slice(None), slice(3 + ch, 5 + ch))
                a = act(hi, bv, ACT.Copy, t)
                t_o = tt(lo, bv, hi.bitcast(F32), ALU.subtract, a)
                free(b, t_o)

        between()
        b = banks[4]
        w = take(b)
        conv_done = list(cur.values())
        for c in range(4):
            t = mm(b.t[:, 0:T], ones, u[:, c, :], c == 0, c == 3, cur[3], *w, sig=c == 3)
        t = stt(u, bc(b.t[:, 0:T], 4), -1.0 / 512, u, ALU.mult, ALU.add, t)
        free(b, t)
        t = act(region(2176, 4, T), u, ACT.Square, t)
        between()
        b = banks[5]
        w = take(b)
        for c in range(4):
            t = mm(b.t[:, 0:T], ones, region(2176, 4, T)[:, c, :], c == 0, c == 3, t, *w, sig=c == 3)
        t = act(sq[:, 0:T], b.t[:, 0:T], ACT.Sqrt, t, scale=1.0 / 512, bias=eps)
        free(b, t)
        recip(sq[:, 0:T], sq[:, 0:T], t)
        t = tt(u, u, bc(sq[:, 0:T], 4), ALU.mult)
        for c in range(4):
            t_c = act(u[:, c, :], u[:, c, :], ACT.Silu, t, scale=c2["ln_g"][:, c:c + 1], bias=c2["ln_b"][:, c:c + 1])
        t_c = split(pair(catT, slice(None), slice(0, 4)), u, t_c)
        state["arena"] = t_c
        mods.finish()
        t = residual("ev_out_w", (0,), gbc[:, 0, :], t_c, t_o, mods.tok[0, 2])
        state["gbc", 0] = [t]
        norm_T(modc[:, 0, 3, :], modc[:, 0, 2, :], mods.tok[0, 3], mods.tok[0, 4], pairs=False)
        stage("moe0")
        if stop != "even":
            moe(0, 1)

            norm_T(modc[:, 1, 1, :], modc[:, 1, 0, :])
            stage("odd")
        if stop not in ("even", "moe0"):
            xb = region(0, 8, 259)
            xc = region(2080, 8, T)
            rr = region(4128, 8, T)
            ii = region(6176, 8, T)
            tn = region(8224, 8, T)
            gy = region(10272, 8, T)
            N8 = lambda i: lnc[:, 8 * i:8 * i + 8]
            lam = c2["lam"]
            t = act(N8(0), lam, ACT.Abs, t_cols)
            t = act(N8(0), N8(0), ACT.Exp, scale=-1.0)
            ts(N8(1), N8(0), 2.0, None, ALU.add, None, t)
            recip(N8(1), N8(1))
            tt(N8(1), N8(1), N8(0), ALU.mult)
            tt(N8(2), N8(1), N8(1), ALU.mult)
            ts(N8(3), N8(2), 1.0 / 19, None, ALU.mult, None)
            for k in range(17, 1, -2):
                stt(N8(3), N8(3), 1.0 / k, N8(2), ALU.add, ALU.mult)
            ts(N8(3), N8(3), 1.0, -16.0, ALU.add, ALU.mult)
            tt(N8(3), N8(3), N8(1), ALU.mult)
            ts(N8(4), lam, 0.0, 8.0, ALU.min, ALU.mult)
            t_c8 = tt(N8(3), N8(3), N8(4), ALU.add)
            c8 = N8(3)
            t_pad = po(lambda e: e.memset(xb[:, :, 0:3], 0.0), state["arena"])
            tx = []
            for half in range(2):
                bs = [bank(4, 5, 6, 7) for _ in range(2)]
                tb = chan_major(hT, "od_in_w", (0,), D + half * 512, 512, bs, *state["hT"])
                for i, b in enumerate(bs):
                    ch = half * 4 + 2 * i
                    a = act(xb[:, ch:ch + 2, 3:259], b.t[:, :].rearrange("p (a n) -> p a n", a=2), ACT.Copy, tb[i],
                            state["arena"])
                    free(b, a)
                    tx += [a, a]
            cur = {}
            for half in range(2):
                for k in range(4):
                    for ch in range(half * 4, half * 4 + 4):
                        sc = c2["cw"][:, k * 8 + ch:k * 8 + ch + 1]
                        if k == 0:
                            cur[ch] = ts(xc[:, ch, :], xb[:, ch, 0:T], sc, c2["cb"][:, ch:ch + 1], ALU.mult, ALU.add,
                                         tx[ch], t_pad, chain=False)
                        else:
                            cur[ch] = stt(xc[:, ch, :], xb[:, ch, k:k + T], sc, xc[:, ch, :], ALU.mult, ALU.add,
                                          cur[ch], chain=False)
            for half in range(2):
                bs = [bank(4, 5, 6, 7) for _ in range(2)]
                tb = chan_major(hT, "od_in_w", (0,), half * 512, 512, bs)
                for i, b in enumerate(bs):
                    ch = half * 4 + 2 * i
                    a = act(gy[:, ch:ch + 2, :], b.t[:, :].rearrange("p (a n) -> p a n", a=2), ACT.Gelu_apprx_tanh, tb[i])
                    free(b, a)
            state["hT_free"] = [tb[1]]
            mods = Mods(ODD_MODS, (banks[6], banks[7]))
            txc = [split(pair(catT, slice(None), slice(4 * i, 4 * i + 4)), xc[:, 4 * i:4 * i + 4, :], cur[4 * i + 3],
                         *state["cat_free"]) for i in range(2)]
            g = take_weight("gates")
            for ch in range(8):
                for n, (dst, bias) in enumerate(((rr, "rgb"), (ii, "igb"))):
                    b = bank(0, 1, 2, 3)
                    t = mm3(b.t[:, 0:T], [x[:, 8 * n + ch, :] for x in g.views], [x[:, ch, :] for x in catT], True, True,
                            *g.tok, txc[ch // 4], *take(b), sig=True)
                    a = act(dst[:, ch, :], b.t[:, 0:T], ACT.Sigmoid, t, bias=c2[bias][:, ch:ch + 1])
                    free(b, a)
            g.release(t)
            t_xc = t
            xb8 = xb[:, :, 0:T]
            halves = [slice(0, 4), slice(4, 8)]
            mods.fill(ODD_AT[0])
            t = [tt(rr[:, h4, :], rr[:, h4, :], bc(c8[:, h4], T, 2), ALU.mult, a, t_c8) for h4 in halves]
            t_th = [act(tn[:, h4, :], rr[:, h4, :], ACT.Tanh, t[i], scale=-1.0) for i, h4 in enumerate(halves)]
            for i, h4 in enumerate(halves):
                t_a = act(rr[:, h4, :], rr[:, h4, :], ACT.Exp)
            for h4 in halves:
                tt(ii[:, h4, :], ii[:, h4, :], xc[:, h4, :], ALU.mult)
            t = []
            for i, h4 in enumerate(halves):
                for q in (slice(4 * i, 4 * i + 2), slice(4 * i + 2, 4 * i + 4)):
                    ts(xb8[:, q, :], tn[:, q, :], 1.0, None, ALU.add, None, t_th[i], cur[4 * i + 3])
                    recip(xb8[:, q, :], xb8[:, q, :])
                    mods.fill(ODD_AT[1])
                t.append(tt(tn[:, h4, :], tn[:, h4, :], xb8[:, h4, :], ALU.mult))
            mods.fill(ODD_AT[2])
            t_s = [act(tn[:, h4, :], tn[:, h4, :], ACT.Sqrt, t[i], scale=2.0) for i, h4 in enumerate(halves)]
            for i, h4 in enumerate(halves):
                tt(ii[:, h4, :], ii[:, h4, :], tn[:, h4, :], ALU.mult, t_s[i])
                for ch in range(4 * i, 4 * i + 4):
                    ve(lambda e, ch=ch: e.tensor_tensor_scan(tn[:, ch, :], rr[:, ch, :], ii[:, ch, :], 0.0, ALU.mult, ALU.add),
                       t_a)
                t = tt(gy[:, h4, :], gy[:, h4, :], tn[:, h4, :], ALU.mult)
                t = split(pair(catT, slice(None), h4), gy[:, h4, :], t, t_xc)
                mods.fill(ODD_AT[3 + i])
            state["arena"] = t
            mods.finish()
            residual("od_out_w", (0,), gbc[:, 0, :], t, mods.tok[1, 2])
            norm_T(modc[:, 1, 3, :], modc[:, 1, 2, :], pairs=False)
            stage("moe1")
        if stop not in ("even", "moe0", "odd"):
            moe(1, 1)

        def mixer2(l, t_rms):
            u_ = region(0, 2, 512)
            g_ = region(1024, 2, 512)
            q = region(2048, 2, 512)
            k = region(3072, 2, 512)
            v = region(4096, 2, 512)
            qT = region(5120, 4, T)
            kT = region(6144, 4, T)
            Px = region(7168, 4, 512)
            PT = region(9216, 4, 512)
            o_ = region(11264, 2, 512)
            lng, lnb = acc[:, 0, 0:512], acc[:, 0, 512:1024]
            wsT = acc[:, 1, 0:512].rearrange("p (g t) -> p g t", g=4)
            wsr = acc[:, 1, 512:1024].rearrange("p (g t) -> p g t", g=4)
            s_l = sem(f"s_sgu{l}")
            wx = [*state["x"], state["arena"]]
            AC.add_dma(lambda e: e.dma_start(lng, A["sgu_ln_g_2"][l, :].partition_broadcast(128)), wx, s_l, 0)
            AC.add_dma(lambda e: e.dma_start(lnb, A["sgu_ln_b_2"][l, :].partition_broadcast(128)), wx, s_l, 0)
            AC.add_dma(lambda e: e.dma_start(wsr, A["sgu_w_2"][l].rearrange("g t s -> t g s")), wx, s_l, 0)
            t_l = (s_l, 48)
            tq = {}
            small_at = 64

            def proj(n, dst, func, *among):
                bs = [banks[i] for i in among]
                ws = [take(b) for b in bs]
                for r, g in weight("w_in_2", (l,), D, n * 512, 512):
                    for th, b in enumerate(bs):
                        for c in range(g.k):
                            t = mm3(b.t[:, :], [x[:, r + c, th * 128:(th + 1) * 128] for x in hT],
                                    [x[:, c, :] for x in g.views], r + c == 0, r + c == KC - 1,
                                    *g.tok, state["hTc"].get(r + c), *ws[th], sig=c == g.k - 1)
                        b.done = t
                    g.release(t)
                    if r:
                        for th, b in enumerate(bs):
                            tq[n, th] = act(dst[:, th, :], b.t[:, :], func, b.done, t_rms, state["arena"],
                                            scale=small[:, 6 + th:7 + th])
                            free(b, tq[n, th])
                        state["hT_free"] = [t]
                    yield

            for _ in proj(0, q, ACT.Copy, 4, 5):
                pass
            for _ in proj(1, k, ACT.Copy, 6, 7):
                pass
            b = banks[4]
            w = take(b)
            for g in range(4):
                t = tr(b.t[:, g * 128:(g + 1) * 128], wsr[:, g, :], t_l, *w, sig=True)
            t_ws = act(wsT, b.t[:, :].rearrange("p (g t) -> p g t", g=4), ACT.Copy, t)
            free(b, t_ws)
            cs = [bc(C[n].rearrange("p (t f) -> p t f", t=2), 8, 2) for n in ("cos", "sin")]
            pg = proj(4, g_, ACT.Gelu, 2, 3)
            for n, dst, dT in ((0, q, qT), (1, k, kT)):
                hv = dst.rearrange("p t (h d) -> p t h d", d=64)
                x1, x2 = hv[:, :, :, 0:8], hv[:, :, :, 8:16]
                R = [region(7168 + i * 128, 2, 8, 8) for i in range(4)]
                tt(R[0], x1, cs[0], ALU.mult, tq[n, 1])
                tt(R[1], x2, cs[1], ALU.mult)
                tt(R[2], x1, cs[1], ALU.mult)
                tt(R[3], x2, cs[0], ALU.mult)
                tt(x1, R[0], R[1], ALU.subtract)
                t = tt(x2, R[2], R[3], ALU.add)
                next(pg)
                for pr in range(2):
                    b = bank(0, 1)
                    w = take(b)
                    for a2 in range(2):
                        for th in range(2):
                            c = pr * 2 + a2
                            tp = tr(b.t[:, a2 * T + th * 128:a2 * T + (th + 1) * 128],
                                    dst[:, th, c * 128:(c + 1) * 128], t, *w, sig=True)
                    tp = act(dT[:, pr * 2:pr * 2 + 2, :], b.t[:, :].rearrange("p (a n) -> p a n", a=2), ACT.Copy, tp)
                    free(b, tp)
            t_qk = tp
            nm, den = small[:, 64:80], small[:, 80:96]
            jobs = [(th, par, j) for th in range(2) for par in range(2) for j in range(2)]
            tz = {}

            def scores(n):
                th, par, j = jobs[n]
                r = slice(64 * par, 64 * par + 64)
                b = bank(0, 1)
                w = take(b)
                for m in range(2):
                    t = mm(b.t[:, m * T:(m + 1) * T], qT[r, 2 * j + m, th * 128:(th + 1) * 128], kT[r, 2 * j + m, :],
                           m == 0, m == 1, t_qk, *w, sig=m == 1)
                tz[n] = (b, t)

            tp_ = {}

            def soft(n):
                th, par, j = jobs[n]
                b, t = tz[n]
                P = Px[:, n % 4, :].rearrange("p (m k) -> p m k", m=2)
                neg = bc(C["neg"][:, th * T:(th + 1) * T], 2)
                cnt = bc(C["cnt"][:, th * T:(th + 1) * T], 2)
                t = stt(P, b.t[:, :].rearrange("p (m k) -> p m k", m=2), 0.125, neg, ALU.mult, ALU.add, t, tt4.get(n % 4))
                free(b, t)
                nn = nm[:, 2 * n:2 * n + 2]
                t = ve(lambda e: e.tensor_reduce(nn, P, X, ALU.max, negate=True))
                for m in range(2):
                    t = act(P[:, m, :], P[:, m, :], ACT.Exp, t, bias=nn[:, m:m + 1])
                tp_[n] = (t, P, cnt)

            def weigh(n):
                t, P, cnt = tp_[n]
                t = tt(P, P, cnt, ALU.mult, t)
                red(den[:, 2 * n:2 * n + 2], P, ALU.add)
                tp_[n] = t

            tt4 = {}
            tpt = {}
            sq2 = region(11264, 2, 512)

            def side():
                pv_ = proj(2, v, ACT.Copy, 2, 3)
                pu_ = proj(3, u_, ACT.Gelu, 2, 3)
                red(small[:, 96:98], g_, ALU.add, tq[4, 1])
                ts(small[:, 96:98], small[:, 96:98], -1.0 / 512, None, ALU.mult, None)
                for th in range(2):
                    t = ts(g_[:, th, :], g_[:, th, :], small[:, 96 + th:97 + th], None, ALU.add, None)
                yield next(pv_)
                for th in range(2):
                    t = act(sq2[:, th, :], g_[:, th, :], ACT.Square, t, accum_out=small[:, 100 + th:101 + th])
                r = rstd(100, 2, 512, t)
                yield next(pv_)
                for th in range(2):
                    ts(g_[:, th, :], g_[:, th, :], small[:, 102 + th:103 + th], None, ALU.mult, None, r)
                tt(g_, g_, bc(lng, 2), ALU.mult, t_l)
                t_g = tt(g_, g_, bc(lnb, 2), ALU.add)
                yield next(pu_)
                yield next(pu_)
                for th in range(2):
                    b = bank(2, 3)
                    w = take(b)
                    for g in range(4):
                        t = mm(b.t[:, g * 128:(g + 1) * 128], wsT[:, g, :], g_[:, th, g * 128:(g + 1) * 128], g == 0, g == 3,
                               t_g, t_ws, *w, sig=g == 3)
                    for g in range(4):
                        s_ = slice(g * 128, (g + 1) * 128)
                        t2 = stt(u_[:, th, s_], b.t[:, s_], c2["sgub"][:, l * 4 + g:l * 4 + g + 1], u_[:, th, s_],
                                 ALU.add, ALU.mult, t, tq[3, th])
                    free(b, t2)
                    yield
                t_rm[1] = rms_half(u_, 104, sq2, t2)
                yield
                t_cat[1] = turn_half(u_, 1, t2, (2, 3))[1]
                yield
                out_half(1, 0)
                yield
                out_half(1, 1)
                yield

            ob = [banks[4], banks[5]]

            def turnP(n):
                b = bank(6, 7)
                w = take(b)
                P = Px[:, n % 4, :]
                for i in range(4):
                    t = tr(b.t[:, i * 128:(i + 1) * 128], P[:, i * 128:(i + 1) * 128], tp_[n], *w, sig=True)
                tt4[n % 4] = t
                t = act(PT[:, n % 4, :], b.t[:, :], ACT.Copy, t, tpv.get(n % 4))
                free(b, t)
                tpt[n] = t

            tpv = {}
            firsts = [True, True]

            def pv(n):
                th, par, j = jobs[n]
                b = ob[th]
                w = take(b) if firsts[th] else []
                for m in range(2):
                    h = 2 * (2 * j + m) + par
                    for kb in range(2):
                        i = m * 2 + kb
                        t = mm(b.t[:, h * 64:(h + 1) * 64], PT[:, n % 4, i * 128:(i + 1) * 128], v[:, kb, h * 64:(h + 1) * 64],
                               firsts[th], kb == 1, tpt[n], tq[2, 1], *w, sig=i == 3)
                        firsts[th] = False
                tpv[n % 4] = t
                tpv[th, "all"] = t

            def rms_half(src, at, sq, t):
                for th in range(2):
                    t = act(sq[:, th, :], src[:, th, :], ACT.Square, t, accum_out=small[:, at + th:at + th + 1])
                return rstd(at, 2, 512, t)

            def turn_half(src, part, t_n, among):
                col = c2[("attn", "sgu")[part]]
                for cc in range(4):
                    b = bank(*among)
                    w = take(b)
                    for th in range(2):
                        tp = tr(b.t[:, th * 128:(th + 1) * 128], src[:, th, cc * 128:(cc + 1) * 128], t_n, *w,
                                sig=th == 1)
                    g = col[:, l * 4 + cc:l * 4 + cc + 1]
                    hi, lo = pair(catT, slice(None), 4 * part + cc)
                    a = act(hi, b.t[:, 0:T], ACT.Copy, tp, *state["cat_free"], scale=g)
                    e = stt(lo, b.t[:, 0:T], g, hi.bitcast(F32), ALU.mult, ALU.subtract, a)
                    free(b, e)
                return tp, e

            def out_half(part, nh):
                g = take_weight("w_out_2", (l,), part * 512, nh * 512)
                for th in range(2):
                    b = banks[2 * nh + th]
                    w = take(b)
                    for c in range(4):
                        t = mm3(b.t[:, :], [x[:, 4 * part + c, th * 128:(th + 1) * 128] for x in catT],
                                [x[:, c, :] for x in g.views], c == 0, c == 3, *g.tok, t_cat[part], *w, sig=c == 3)
                    b.done = t
                    o = xres[:, th, nh * 512:(nh + 1) * 512]
                    at = (110, 106)[part] + th
                    t_r = stt(o, b.t[:, :], small[:, at:at + 1], o, ALU.mult, ALU.add, t, t_rm[part])
                    free(b, t_r)
                    state["xq"][th, nh] = t_r
                g.release(t)
                return t_r

            t_cat, t_rm = {}, {}
            for n in range(2):
                scores(n)
            rest = side()
            for n in range(8):
                soft(n)
                for _ in range(SIDE[n]):
                    next(rest)
                if n >= 1:
                    weigh(n - 1)
                    turnP(n - 1)
                if n + 2 < 8:
                    scores(n + 2)
                if n >= 2:
                    pv(n - 2)
            weigh(7)
            pv(6)
            next(rest)
            turnP(7)
            next(rest)
            pv(7)
            t_den = recip(den, den)
            for th in range(2):
                for par in range(2):
                    o4 = o_[:, th, :].rearrange("p (c two d) -> p c two d", two=2, d=64)[:, :, par, :]
                    b4 = ob[th].t[:, :].rearrange("p (c two d) -> p c two d", two=2, d=64)[:, :, par, :]
                    dd = den[:, 8 * th + 4 * par:8 * th + 4 * par + 4]
                    t = tt(o4, b4, bc(dd, 64, 2), ALU.mult, t_den, tpv[th, "all"])
                free(ob[th], t)
            state["arena"], t_cat[0] = turn_half(o_, 0, t, (6, 7))
            t_rm[0] = rms_half(o_, 108, Px[:, 0:2, :], t)
            for nh in range(2):
                t = out_half(0, nh)
            state["x"] = [t]
            state["cat_free"] = [banks[3].done]

        order = ["even", "moe0", "odd", "moe1"]
        if stop is None or stop not in order:
            c_f1 = c2["ffn1"].rearrange("p (l k) -> p l k", l=2)
            c_f2 = c2["ffn2"].rearrange("p (l k) -> p l k", l=2)
            c_mx = c2["mix"].rearrange("p (l k) -> p l k", l=2)
            for l in range(2):
                stage(f"ffa{l}")
                state["rms"] = turn_x(c_f1[:, l, :])
                ffn(l, "ffn1")
                if stop == f"ffa{l}":
                    break
                stage(f"mix{l}")
                mixer2(l, turn_x(c_mx[:, l, :]))
                if stop == f"mix{l}":
                    break
                stage(f"ffb{l}")
                state["rms"] = turn_x(c_f2[:, l, :])
                ffn(l, "ffn2")
                if stop == f"ffb{l}":
                    break
        stage("end")
        s_out, s_fin = sem("s_out"), sem("s_fin")
        dst = out.rearrange("a (t p) d -> p (a t) d", p=128)
        if stop is not None:
            SP.add_dma(lambda e: e.dma_start(dst, xres[:, :, :]), state["x"], s_out, 16)
            SP.items.append((None, [(s_out, 16)], None, 0))
        else:
            fin = region(0, D)
            td = AC.add_dma(lambda e: e.dma_start(fin, A["final_norm_2"].partition_broadcast(128)),
                            [state["arena"]], s_fin, 16)
            xn = region(12288, 2, D)
            r, _ = x_rms(xn)
            for th in range(2):
                t = stt(xn[:, th, :], xres[:, th, :], small[:, 6 + th:7 + th], fin, ALU.mult, ALU.mult, r, td)
                SP.add_dma(lambda e, th=th: e.dma_start(dst[:, th, :], xn[:, th, :]), [t], s_out, 16)
            SP.items.append((None, [(s_out, 32)], None, 0))

        block = ctx.enter_context(nc.Block())

        @block.sync
        def _(eng):
            SP.emit(eng)

        @block.gpsimd
        def _(eng):
            PO.emit(eng)

        @block.scalar
        def _(eng):
            AC.emit(eng)

        @block.vector
        def _(eng):
            VE.emit(eng)

        @block.tensor
        def _(eng):
            PE.emit(eng)


def build(nc, stop=None):
    A = {}
    for n, shape in SHAPES.items():
        A[n] = nc.dram_tensor(f"in_{n}", shape, F32, kind="ExternalInput").ap()
    k = constants()
    width = sum(a.shape[1] for a in k.values())
    A["constants"] = nc.dram_tensor("in_constants", (128, width), F32, kind="ExternalInput").ap()
    out = nc.dram_tensor("out_0", (1, T, D), F32, kind="ExternalOutput").ap()
    program(nc, A, out, stop)


def kernel(**inputs):
    import concourse.bacc as bacc
    from concourse.bass_utils import run_bass_kernel_spmd

    nc = bacc.Bacc("TRN2", target_bir_lowering=False, num_devices=1)
    build(nc)
    arrays = {f"in_{n}": np.ascontiguousarray(inputs[n]) for n in SHAPES}
    arrays["in_constants"] = np.concatenate(list(constants().values()), axis=1)
    r = run_bass_kernel_spmd(nc, [arrays], core_ids=[0])
    return r.results[0]["out_0"]
```
